# Optimizing a Trainium2 kernel written in Bass

```python
import math
import jax
import jax.numpy as jnp
from jax import lax
import numpy as np

D_MODEL = 1024
BATCH = 1
SEQ = 256
DEPTH = 2

GRID_W = 64
CTX_LEN = 256
MIX_WIDTH = D_MODEL
N_BRANCH = 3
EPS = 1e-6
ROPE_THETA = 10000.0

SSD_HEAD_DIM = 64
SSD_HEADS = MIX_WIDTH // SSD_HEAD_DIM
SSD_GROUPS = 4
SSD_HPG = SSD_HEADS // SSD_GROUPS
SSD_STATE = 128
SSD_CONV = 5
SSD_CHUNK = 128
SSD_CONV_DIM = MIX_WIDTH + 2 * SSD_GROUPS * SSD_STATE
SSD_PROJ = MIX_WIDTH + SSD_CONV_DIM + 2 * SSD_HEADS

RWKV_HEAD_DIM = 64
RWKV_HEADS = MIX_WIDTH // RWKV_HEAD_DIM
RWKV_DECAY_LORA = 64
RWKV_AAA_LORA = 64
RWKV_GATE_LORA = 128
RWKV_GN_EPS = 64e-5
RWKV_PROJ = 3 * MIX_WIDTH + RWKV_DECAY_LORA + RWKV_AAA_LORA + RWKV_GATE_LORA
RWKV_SPLITS = [MIX_WIDTH, 2 * MIX_WIDTH, 3 * MIX_WIDTH, 3 * MIX_WIDTH + RWKV_DECAY_LORA, 3 * MIX_WIDTH + RWKV_DECAY_LORA + RWKV_AAA_LORA]

NA_HEAD_DIM = 64
NA_HEADS = MIX_WIDTH // NA_HEAD_DIM
NA_ROWS = 8
NA_COLS = 16
NA_QBLK = 16
NA_PROJ = 3 * MIX_WIDTH

GATE_PROJ = N_BRANCH * D_MODEL
IN_PROJ = SSD_PROJ + RWKV_PROJ + NA_PROJ + GATE_PROJ

MOE_GROUPS = 4
MOE_EXPERTS_PER_GROUP = 4
MOE_EXPERTS = MOE_GROUPS * MOE_EXPERTS_PER_GROUP
MOE_TOP_K = 2
MOE_HIDDEN = 768
MOE_BLOCK = 128

kernel_name = 'hybrid_ssd_rwkv7_natten_hmoe_dit'

def rmsnorm(x, w):
    xf = x.astype(jnp.float32)
    y = xf * lax.rsqrt(jnp.mean(xf * xf, axis=-1, keepdims=True) + EPS)
    return (y * w.astype(jnp.float32)).astype(x.dtype)

def dwconv_centred(u, w, bias):
    k = w.shape[0]
    y = lax.conv_general_dilated(u, w[:, None, :].astype(u.dtype), window_strides=(1,),
                                 padding=[(k // 2, k // 2)],
                                 dimension_numbers=('NWC', 'WIO', 'NWC'),
                                 feature_group_count=u.shape[-1])
    return y + bias

def rope_2d(u, rows, cols):
    n = u.shape[-1]
    half, quarter = n // 2, n // 4
    inv = ROPE_THETA ** (-jnp.arange(quarter, dtype=jnp.float32) / quarter)

    def rot(v, pos):
        ang = pos.astype(jnp.float32)[:, None] * inv
        cos = jnp.cos(ang)[:, None, :].astype(v.dtype)
        sin = jnp.sin(ang)[:, None, :].astype(v.dtype)
        v1, v2 = v[..., :quarter], v[..., quarter:]
        return jnp.concatenate([v1 * cos - v2 * sin, v1 * sin + v2 * cos], axis=-1)

    return jnp.concatenate([rot(u[..., :half], rows), rot(u[..., half:], cols)], axis=-1)

def ssd_chunked(X, dA, Bm, Cm, h0):
    b, t, g, j, p = X.shape
    n = Bm.shape[-1]
    nc, q = t // SSD_CHUNK, SSD_CHUNK
    X = X.astype(jnp.float32).reshape(b, nc, q, g, j, p)
    dA = dA.astype(jnp.float32).reshape(b, nc, q, g, j)
    Bm = Bm.astype(jnp.float32).reshape(b, nc, q, g, n)
    Cm = Cm.astype(jnp.float32).reshape(b, nc, q, g, n)
    acs = jnp.cumsum(dA, axis=2)
    lower = jnp.tril(jnp.ones((q, q), bool))
    seg = acs[:, :, :, None] - acs[:, :, None, :]
    L = jnp.exp(jnp.where(lower[None, None, :, :, None, None], seg, -jnp.inf))
    cb = jnp.einsum('bclgn,bcsgn->bclsg', Cm, Bm)
    y_diag = jnp.einsum('bclsg,bclsgj,bcsgjp->bclgjp', cb, L, X)
    decay_end = jnp.exp(acs[:, :, -1:] - acs)
    chunk_states = jnp.einsum('bcsgn,bcsgj,bcsgjp->bcgjpn', Bm, decay_end, X)
    chunk_decay = jnp.exp(acs[:, :, -1])

    def step(h, inp):
        st, dec = inp
        return h * dec[..., None, None] + st, h

    h_fin, h_in = lax.scan(step, h0, (jnp.moveaxis(chunk_states, 1, 0), jnp.moveaxis(chunk_decay, 1, 0)))
    y_off = jnp.einsum('bclgn,cbgjpn,bclgj->bclgjp', Cm, h_in, jnp.exp(acs))
    return (y_diag + y_off).reshape(b, t, g, j, p), h_fin

def _ssd_prep(p, conv_w, conv_b, dt_bias, pos):
    b, t, _ = p.shape
    z, xbc, dt_raw = jnp.split(p, [MIX_WIDTH, MIX_WIDTH + SSD_CONV_DIM], axis=-1)
    xbc = jax.nn.silu(dwconv_centred(xbc, conv_w, conv_b))
    xs, bm, cm = jnp.split(xbc, [MIX_WIDTH, MIX_WIDTH + SSD_GROUPS * SSD_STATE], axis=-1)
    bm = bm.reshape(b, t, SSD_GROUPS, SSD_STATE)
    cm = cm.reshape(b, t, SSD_GROUPS, SSD_STATE)
    if pos is not None:
        bm = rope_2d(bm, pos[0], pos[1])
        cm = rope_2d(cm, pos[0], pos[1])
    xs = xs.reshape(b, t, SSD_GROUPS, SSD_HPG, SSD_HEAD_DIM)
    dt = jax.nn.softplus(dt_raw.astype(jnp.float32).reshape(b, t, 2, SSD_GROUPS, SSD_HPG)
                         + dt_bias.astype(jnp.float32).reshape(2, SSD_GROUPS, SSD_HPG))
    return z, xs, bm, cm, dt

def _ssd_direction(xs, dt, a_d, bm, cm, h0, reverse):
    f = (lambda u: jnp.flip(u, axis=1)) if reverse else (lambda u: u)
    y, h = ssd_chunked(f(xs * dt[..., None]), f(dt * a_d), f(bm), f(cm), h0)
    return f(y), h

def _ssd_out(y, xs, z, d_skip, norm_w):
    b, t = z.shape[:2]
    y = y + d_skip.astype(jnp.float32).reshape(SSD_GROUPS, SSD_HPG, 1) * xs
    y = y.reshape(b, t, MIX_WIDTH) * jax.nn.silu(z.astype(jnp.float32))
    return rmsnorm(y, norm_w).astype(z.dtype)

def ssd_mixer(pc, pl, pos, conv_w, conv_b, dt_bias, a_log, d_skip, norm_w, ctx_out):
    zc, xc, bc, cc, dtc = _ssd_prep(pc, conv_w, conv_b, dt_bias, None)
    zl, xl, bl, cl, dtl = _ssd_prep(pl, conv_w, conv_b, dt_bias, pos)
    a = -jnp.exp(a_log.astype(jnp.float32)).reshape(2, SSD_GROUPS, SSD_HPG)
    h0 = jnp.zeros((pc.shape[0], SSD_GROUPS, SSD_HPG, SSD_HEAD_DIM, SSD_STATE), jnp.float32)
    yc_dirs, yl_dirs = [], []
    for d in range(2):
        yc_d, h_ctx = _ssd_direction(xc, dtc[:, :, d], a[d], bc, cc, h0, d == 1)
        yl_d, _ = _ssd_direction(xl, dtl[:, :, d], a[d], bl, cl, h_ctx, d == 1)
        yc_dirs.append(yc_d)
        yl_dirs.append(yl_d)
    y_lat = _ssd_out(yl_dirs[0] + yl_dirs[1], xl, zl, d_skip, norm_w)
    y_ctx = _ssd_out(yc_dirs[0] + yc_dirs[1], xc, zc, d_skip, norm_w) if ctx_out else None
    return y_ctx, y_lat

def bi_shift(p):
    pp = jnp.pad(p, ((0, 0), (1, 1), (0, 0)))
    return 0.5 * (pp[:, :-2] + pp[:, 2:]) - p

def _rwkv_prep(p, mu, w0, w2, a0, a2, g2, k_k, k_a):
    b, t, _ = p.shape
    p = p + mu * bi_shift(p)
    r, k, v, wl, al, gl = jnp.split(p, RWKV_SPLITS, axis=-1)
    w = -jax.nn.softplus(-(w0[:, None, None, :] + jnp.einsum('btr,zrc->zbtc', jnp.tanh(wl), w2))) - 0.5
    decay = jnp.exp(-jnp.exp(w.astype(jnp.float32)))
    a = jax.nn.sigmoid((a0[:, None, None, :] + jnp.einsum('btr,zrc->zbtc', al, a2)).astype(jnp.float32))
    g = jax.nn.sigmoid(gl) @ g2
    kf = k.astype(jnp.float32)
    heads = lambda u: u.reshape(u.shape[:-1] + (RWKV_HEADS, RWKV_HEAD_DIM))
    kk = heads(kf * k_k)
    kk = kk / jnp.maximum(jnp.sqrt(jnp.sum(kk * kk, axis=-1, keepdims=True)), 1e-12)
    k_dir = kf[None] * (1 + (a - 1) * k_a)
    return heads(r.astype(jnp.float32)), heads(decay), heads(k_dir), heads(v.astype(jnp.float32)), kk, heads(a), g

def _wkv_bidir(r, w, k, v, kk, a, s0):
    fwd_bwd = lambda u: jnp.stack([u, jnp.flip(u, axis=1)])
    per_dir = lambda u: jnp.stack([u[0], jnp.flip(u[1], axis=1)])
    seqs = (fwd_bwd(r), per_dir(w), per_dir(k), fwd_bwd(v), fwd_bwd(kk), per_dir(a))

    def step(S, inp):
        r_t, w_t, k_t, v_t, kk_t, a_t = inp
        s_kk = jnp.einsum('...vk,...k->...v', S, kk_t)
        S = (S * w_t[..., None, :] - s_kk[..., :, None] * (kk_t * a_t)[..., None, :]
             + v_t[..., :, None] * k_t[..., None, :])
        return S, jnp.einsum('...vk,...k->...v', S, r_t)

    s_fin, y = lax.scan(step, s0, tuple(jnp.moveaxis(u, 2, 0) for u in seqs))
    y = jnp.moveaxis(y, 0, 2)
    return y[0] + jnp.flip(y[1], axis=1), s_fin

def _rwkv_out(y, r, k_dir, v, g, ln_w, ln_b, r_k):
    b, t = g.shape[:2]
    mean = jnp.mean(y, axis=-1, keepdims=True)
    var = jnp.mean(jnp.square(y - mean), axis=-1, keepdims=True)
    yn = ((y - mean) * lax.rsqrt(var + RWKV_GN_EPS)).reshape(b, t, MIX_WIDTH) * ln_w + ln_b
    k_b = 0.5 * (k_dir[0] + k_dir[1])
    bonus = (jnp.sum(r * k_b * r_k, axis=-1, keepdims=True) * v).reshape(b, t, MIX_WIDTH)
    return ((yn + bonus) * g).astype(g.dtype)

def rwkv_mixer(pc, pl, mu, w0, w2, a0, a2, g2, k_k, k_a, r_k, ln_w, ln_b, ctx_out):
    rc, wc, kdc, vc, kkc, ac, gc = _rwkv_prep(pc, mu, w0, w2, a0, a2, g2, k_k, k_a)
    rl, wl, kdl, vl, kkl, al, gl = _rwkv_prep(pl, mu, w0, w2, a0, a2, g2, k_k, k_a)
    s0 = jnp.zeros((2, pc.shape[0], RWKV_HEADS, RWKV_HEAD_DIM, RWKV_HEAD_DIM), jnp.float32)
    yc, s_ctx = _wkv_bidir(rc, wc, kdc, vc, kkc, ac, s0)
    yl, _ = _wkv_bidir(rl, wl, kdl, vl, kkl, al, s_ctx)
    y_lat = _rwkv_out(yl, rl, kdl, vl, gl, ln_w, ln_b, r_k)
    y_ctx = _rwkv_out(yc, rc, kdc, vc, gc, ln_w, ln_b, r_k) if ctx_out else None
    return y_ctx, y_lat

def _na_latent(q, k, v, kc, vc, rpb):
    b, t, h, dh = q.shape
    rows = t // GRID_W
    kr = min(NA_ROWS, rows)
    n_cb = GRID_W // NA_QBLK
    band = 2 * NA_COLS
    qcol = np.arange(GRID_W).reshape(n_cb, NA_QBLK)
    cb = np.clip(np.arange(n_cb) * NA_QBLK - NA_COLS // 2, 0, GRID_W - band)
    kcol = cb[:, None] + np.arange(band)
    cs = np.clip(qcol - NA_COLS // 2, 0, GRID_W - NA_COLS)
    valid = (kcol[:, None, :] >= cs[:, :, None]) & (kcol[:, None, :] < cs[:, :, None] + NA_COLS)
    dc = np.clip(kcol[:, None, :] - qcol[:, :, None], 1 - NA_COLS, NA_COLS - 1) + NA_COLS - 1
    bias_c = rpb[:, :, dc]
    scale = dh ** -0.5
    qg, kg, vg = (u.reshape(b, rows, GRID_W, h, dh) for u in (q, k, v))
    n_loc = kr * band

    def row_block(r):
        rs = jnp.clip(r - kr // 2, 0, rows - kr)
        kb = lax.dynamic_slice_in_dim(kg, rs, kr, axis=1)[:, :, kcol]
        vb = lax.dynamic_slice_in_dim(vg, rs, kr, axis=1)[:, :, kcol]
        qr = lax.dynamic_index_in_dim(qg, r, axis=1, keepdims=False).reshape(b, n_cb, NA_QBLK, h, dh)
        bias = jnp.take(bias_c, rs + jnp.arange(kr) - r + NA_ROWS - 1, axis=1).transpose(0, 2, 3, 1, 4)
        s_loc = jnp.einsum('bjqhd,bijkhd->bhjqik', qr, kb).astype(jnp.float32) * scale + bias
        s_loc = jnp.where(valid[:, :, None, :], s_loc, -jnp.inf).reshape(b, h, n_cb, NA_QBLK, n_loc)
        s_ctx = jnp.einsum('bjqhd,bkhd->bhjqk', qr, kc).astype(jnp.float32) * scale
        prob = jax.nn.softmax(jnp.concatenate([s_loc, s_ctx], axis=-1), axis=-1).astype(v.dtype)
        p_loc = prob[..., :n_loc].reshape(b, h, n_cb, NA_QBLK, kr, band)
        o = (jnp.einsum('bhjqik,bijkhd->bjqhd', p_loc, vb)
             + jnp.einsum('bhjqk,bkhd->bjqhd', prob[..., n_loc:], vc))
        return o.reshape(b, GRID_W, h, dh)

    out = lax.map(row_block, jnp.arange(rows))
    return out.transpose(1, 0, 2, 3, 4).reshape(b, t, h * dh)

def na_mixer(pc, pl, rpb, ctx_out):
    heads = lambda u: u.reshape(u.shape[0], u.shape[1], NA_HEADS, NA_HEAD_DIM)
    qc, kc, vc = (heads(u) for u in jnp.split(pc, 3, axis=-1))
    ql, kl, vl = (heads(u) for u in jnp.split(pl, 3, axis=-1))
    y_lat = _na_latent(ql, kl, vl, kc, vc, rpb)
    y_ctx = None
    if ctx_out:
        s = jnp.einsum('bqhd,bkhd->bhqk', qc, kc).astype(jnp.float32) * NA_HEAD_DIM ** -0.5
        y_ctx = jnp.einsum('bhqk,bkhd->bqhd', jax.nn.softmax(s, axis=-1).astype(vc.dtype), vc)
        y_ctx = y_ctx.reshape(pc.shape[0], pc.shape[1], MIX_WIDTH)
    return y_ctx, y_lat

def merge_branches(ys, gate_logits, w_branch, w_out):
    b, t, _ = gate_logits.shape
    gates = jax.nn.sigmoid(gate_logits.reshape(b, t, N_BRANCH, D_MODEL))
    proj = jnp.einsum('btiw,iwd->btid', jnp.stack(ys, axis=2), w_branch)
    return jnp.sum(gates * proj, axis=2) @ w_out

def route_hierarchical(toks, w_group, b_group, w_expert, b_expert):
    tf = toks.astype(jnp.float32)
    n = tf.shape[0]
    p_group = jax.nn.softmax(tf @ w_group.astype(jnp.float32) + b_group.astype(jnp.float32), axis=-1)
    p_top, g_sel = lax.top_k(p_group, 1)
    logit_e = (tf @ w_expert.astype(jnp.float32) + b_expert.astype(jnp.float32)).reshape(n, MOE_GROUPS, MOE_EXPERTS_PER_GROUP)
    logit_e = logit_e[jnp.arange(n), g_sel[:, 0]]
    p_e, e_loc = lax.top_k(jax.nn.softmax(logit_e, axis=-1), MOE_TOP_K)
    weights = p_top * p_e / jnp.sum(p_e, axis=-1, keepdims=True)
    return g_sel * MOE_EXPERTS_PER_GROUP + e_loc, weights

def moe_ffn(toks, e_idx, e_w, w_gate, w_up, w_down):
    n, d = toks.shape
    a_len = n * MOE_TOP_K
    flat_e = e_idx.reshape(-1)
    order = jnp.argsort(flat_e)
    se = flat_e[order]
    stok = jnp.repeat(jnp.arange(n), MOE_TOP_K)[order]
    sw = e_w.reshape(-1)[order]
    counts = jnp.bincount(flat_e, length=MOE_EXPERTS)
    seg_start = jnp.cumsum(counts) - counts
    padded = (counts + MOE_BLOCK - 1) // MOE_BLOCK * MOE_BLOCK
    pad_end = jnp.cumsum(padded)
    pad_start = pad_end - padded
    slot = jnp.arange(a_len) - seg_start[se] + pad_start[se]
    n_blocks = -(-a_len // MOE_BLOCK) + MOE_EXPERTS
    slot_tok = jnp.full((n_blocks * MOE_BLOCK,), n, jnp.int32).at[slot].set(stok)
    block_e = jnp.minimum(jnp.searchsorted(pad_end, jnp.arange(n_blocks) * MOE_BLOCK, side='right'), MOE_EXPERTS - 1)
    t_pad = jnp.concatenate([toks, jnp.zeros((1, d), toks.dtype)], axis=0)

    def expert_block(args):
        tok, e = args
        xb = t_pad[tok]
        hdn = jax.nn.silu(xb @ w_gate[e]) * (xb @ w_up[e])
        return hdn @ w_down[e]

    yb = lax.map(expert_block, (slot_tok.reshape(n_blocks, MOE_BLOCK), block_e)).reshape(-1, d)
    return jnp.zeros_like(toks).at[stok].add(yb[slot] * sw[:, None].astype(toks.dtype))

def setup_inputs(seed: int = 0) -> dict:
    keys = iter(jax.random.split(jax.random.key(seed), 64))

    def nrm(shape, scale=1.0):
        return scale * jax.random.normal(next(keys), shape, jnp.float32)

    def unif(shape, lo, hi):
        return jax.random.uniform(next(keys), shape, jnp.float32, lo, hi)

    L, D = DEPTH, D_MODEL
    dt0 = jnp.exp(unif((L, 2, SSD_HEADS), math.log(1e-3), math.log(1e-1)))
    return {
        'x': nrm((BATCH, SEQ, D)),
        'c': nrm((BATCH, D)),
        'ctx': nrm((BATCH, CTX_LEN, D)),
        'c_ctx': nrm((D,)),
        'w_mod': nrm((L, D, 6 * D), 0.5 * D ** -0.5),
        'b_mod': nrm((L, 6 * D), 0.02),
        'norm1_w': 1.0 + nrm((L, D), 0.02),
        'norm2_w': 1.0 + nrm((L, D), 0.02),
        'w_in': nrm((L, D, IN_PROJ), D ** -0.5),
        'ssd_conv_w': nrm((L, SSD_CONV, SSD_CONV_DIM), SSD_CONV ** -0.5),
        'ssd_conv_b': nrm((L, SSD_CONV_DIM), 0.02),
        'ssd_dt_bias': dt0 + jnp.log(-jnp.expm1(-dt0)),
        'ssd_a_log': jnp.log(unif((L, 2, SSD_HEADS), 1.0, 16.0)),
        'ssd_d': 1.0 + nrm((L, SSD_HEADS), 0.1),
        'ssd_norm_w': 1.0 + nrm((L, MIX_WIDTH), 0.02),
        'rwkv_mu': unif((L, RWKV_PROJ), 0.0, 1.0),
        'rwkv_w0': unif((L, 2, MIX_WIDTH), -6.0, -1.0),
        'rwkv_w2': nrm((L, 2, RWKV_DECAY_LORA, MIX_WIDTH), 0.1 * RWKV_DECAY_LORA ** -0.5),
        'rwkv_a0': nrm((L, 2, MIX_WIDTH), 0.1),
        'rwkv_a2': nrm((L, 2, RWKV_AAA_LORA, MIX_WIDTH), RWKV_AAA_LORA ** -0.5),
        'rwkv_g2': nrm((L, RWKV_GATE_LORA, MIX_WIDTH), RWKV_GATE_LORA ** -0.5),
        'rwkv_k_k': 0.85 + nrm((L, MIX_WIDTH), 0.02),
        'rwkv_k_a': 1.0 + nrm((L, MIX_WIDTH), 0.02),
        'rwkv_r_k': nrm((L, RWKV_HEADS, RWKV_HEAD_DIM), 0.1),
        'rwkv_ln_w': 1.0 + nrm((L, MIX_WIDTH), 0.02),
        'rwkv_ln_b': nrm((L, MIX_WIDTH), 0.02),
        'na_rpb': nrm((L, NA_HEADS, 2 * NA_ROWS - 1, 2 * NA_COLS - 1), 0.1),
        'w_branch': nrm((L, N_BRANCH, MIX_WIDTH, D), MIX_WIDTH ** -0.5),
        'w_out': nrm((L, D, D), D ** -0.5),
        'moe_w_group': nrm((L, D, MOE_GROUPS), D ** -0.5),
        'moe_b_group': nrm((L, MOE_GROUPS), 0.01),
        'moe_w_expert': nrm((L, D, MOE_EXPERTS), D ** -0.5),
        'moe_b_expert': nrm((L, MOE_EXPERTS), 0.01),
        'moe_w_gate': nrm((L, MOE_EXPERTS, D, MOE_HIDDEN), D ** -0.5),
        'moe_w_up': nrm((L, MOE_EXPERTS, D, MOE_HIDDEN), D ** -0.5),
        'moe_w_down': nrm((L, MOE_EXPERTS, MOE_HIDDEN, D), MOE_HIDDEN ** -0.5),
        'final_norm_w': 1.0 + nrm((D,), 0.02),
    }

def reference(x, c, ctx, c_ctx, w_mod, b_mod, norm1_w, norm2_w, w_in,
              ssd_conv_w, ssd_conv_b, ssd_dt_bias, ssd_a_log, ssd_d, ssd_norm_w,
              rwkv_mu, rwkv_w0, rwkv_w2, rwkv_a0, rwkv_a2, rwkv_g2, rwkv_k_k, rwkv_k_a,
              rwkv_r_k, rwkv_ln_w, rwkv_ln_b, na_rpb, w_branch, w_out,
              moe_w_group, moe_b_group, moe_w_expert, moe_b_expert,
              moe_w_gate, moe_w_up, moe_w_down, final_norm_w):
    b, t, d = x.shape
    tok = jnp.arange(t)
    pos = (tok // GRID_W, tok % GRID_W)
    split_at = [SSD_PROJ, SSD_PROJ + RWKV_PROJ, SSD_PROJ + RWKV_PROJ + NA_PROJ]
    n_lat = b * t
    for l in range(DEPTH):
        last = l == DEPTH - 1
        mod_l = jax.nn.silu(c) @ w_mod[l] + b_mod[l]
        mod_c = jax.nn.silu(c_ctx) @ w_mod[l] + b_mod[l]
        sh1, sc1, g1, sh2, sc2, g2 = jnp.split(mod_l[:, None, :], 6, axis=-1)
        csh1, csc1, cg1, csh2, csc2, cg2 = jnp.split(mod_c, 6, axis=-1)
        hl = rmsnorm(x, norm1_w[l]) * (1 + sc1) + sh1
        hc = rmsnorm(ctx, norm1_w[l]) * (1 + csc1) + csh1
        pl_ssd, pl_rwkv, pl_na, pl_gate = jnp.split(hl @ w_in[l], split_at, axis=-1)
        pc_ssd, pc_rwkv, pc_na, pc_gate = jnp.split(hc @ w_in[l], split_at, axis=-1)
        ya_c, ya_l = ssd_mixer(pc_ssd, pl_ssd, pos, ssd_conv_w[l], ssd_conv_b[l], ssd_dt_bias[l],
                               ssd_a_log[l], ssd_d[l], ssd_norm_w[l], not last)
        yb_c, yb_l = rwkv_mixer(pc_rwkv, pl_rwkv, rwkv_mu[l], rwkv_w0[l], rwkv_w2[l], rwkv_a0[l],
                                rwkv_a2[l], rwkv_g2[l], rwkv_k_k[l], rwkv_k_a[l], rwkv_r_k[l],
                                rwkv_ln_w[l], rwkv_ln_b[l], not last)
        yc_c, yc_l = na_mixer(pc_na, pl_na, na_rpb[l], not last)
        x = x + g1 * merge_branches((ya_l, yb_l, yc_l), pl_gate, w_branch[l], w_out[l])
        toks = (rmsnorm(x, norm2_w[l]) * (1 + sc2) + sh2).reshape(n_lat, d)
        if not last:
            ctx = ctx + cg1 * merge_branches((ya_c, yb_c, yc_c), pc_gate, w_branch[l], w_out[l])
            h2c = rmsnorm(ctx, norm2_w[l]) * (1 + csc2) + csh2
            toks = jnp.concatenate([toks, h2c.reshape(-1, d)], axis=0)
        e_idx, e_w = route_hierarchical(toks, moe_w_group[l], moe_b_group[l], moe_w_expert[l], moe_b_expert[l])
        ffn = moe_ffn(toks, e_idx, e_w, moe_w_gate[l], moe_w_up[l], moe_w_down[l])
        x = x + g2 * ffn[:n_lat].reshape(b, t, d)
        if not last:
            ctx = ctx + cg2 * ffn[n_lat:].reshape(ctx.shape)
    return rmsnorm(x, final_norm_w)


_drawn_inputs = setup_inputs


def setup_inputs(seed=0):
    import zlib

    import numpy as np

    out = dict(_drawn_inputs(seed))
    spreads = {}
    factors = {'norm1_w': 3.586,
     'norm2_w': 4.577,
     'ssd_conv_b': 7.033,
     'ssd_d': 3.687,
     'ssd_norm_w': 8.0,
     'rwkv_w2': 8.0,
     'rwkv_a0': 5.922,
     'rwkv_k_k': 6.839,
     'rwkv_k_a': 6.982,
     'rwkv_ln_w': 8.0,
     'rwkv_ln_b': 8.0,
     'na_rpb': 8.0,
     'moe_b_group': 7.994,
     'moe_b_expert': 6.541}
    for name, (base, spread) in spreads.items():
        noise = np.random.default_rng([zlib.crc32(name.encode()), seed]).standard_normal(out[name].shape)
        drawn = base * np.exp(spread * noise) if base else spread * noise
        out[name] = jnp.asarray(drawn.astype(out[name].dtype))
    for name, factor in factors.items():
        out[name] = (out[name] * factor).astype(out[name].dtype)
    return out
```

```python
from collections import namedtuple
from contextlib import ExitStack, contextmanager

import numpy as np

import concourse.bass as bass
from concourse import mybir

F32 = mybir.dt.float32
ALU = mybir.AluOpType
ACT = mybir.ActivationFunctionType
AX = mybir.AxisListType

P = 128
D = 1024
KT = D // P
LC = 256
TT = 512
NT = TT // P
DEPTH = 2
EPS = 1e-6
GN_EPS = 64e-5
HEADS = 16
GROUPS = 4
EXPERTS = 16
HID = 768
HT = HID // P
C_Z, C_XBC, C_DT, C_R, C_WA, C_G, C_Q, C_V, C_GATE = 0, 1024, 3072, 3104, 6176, 6304, 6432, 8480, 9504
ORDER = ((0, 1, 2, 3), (1, 0, 3, 2))
DECAY_SCALE = float(np.exp(-0.5))
NEG = -1e30

CONSTS = {}


def _layout(parts):
    at = 0
    for name, n in parts:
        CONSTS[name] = (at, n)
        at += n
    return at


N_CONST = _layout([("ident", P), ("ones", P), ("headones", P), ("rope_perm", P), ("cos", 256),
                   ("sin", 256), ("gmask", 2 * 512), ("amask", 2 * P), ("bd16", P), ("off32", P),
                   ("off64", P), ("off128", P), ("ssdmask", 2 * P), ("namask", 256), ("pref", 4)])

COLS = {}


def _columns():
    at = 0
    for name, n in [("norm1", 8), ("norm2", 8), ("b_mod", 48), ("conv_b", 16), ("conv_w", 80),
                    ("ssd_d", 8), ("ssd_norm", 8), ("mu_wa", 1), ("mu_g", 1)]:
        COLS[name] = (at, n)
        at += n
    return at


N_COL = _columns()
N_RCOL = 12
MU, W0, A0, KK, KA, RK, LNW, LNB = 0, 3, 5, 7, 8, 9, 10, 11


def constants():
    c = np.zeros((P, N_CONST), np.float32)

    def put(name, a):
        at, n = CONSTS[name]
        c[:, at:at + n] = a.reshape(P, n)

    i = np.arange(P)
    put("ident", np.eye(P))
    put("ones", np.ones((P, P)))
    put("headones", (i[:, None] // 64 == i[None] // 64).astype(np.float32))
    perm = np.zeros((P, P))
    for m in range(P):
        if (m // 32) % 2 == 0:
            perm[m + 32, m] = -1.0
        else:
            perm[m - 32, m] = 1.0
    put("rope_perm", perm)
    inv = (10000.0 ** (-np.arange(32, dtype=np.float32) / np.float32(32))).astype(np.float32)
    tok = np.arange(256)
    pos = np.stack([tok // 64, tok % 64]).astype(np.float32)
    ang = (pos[(i // 64)] * inv[i % 32][:, None]).astype(np.float32)
    put("cos", np.cos(ang))
    put("sin", np.sin(ang))
    up = (i[:, None] < i[None]).astype(np.float32)
    eye = np.eye(P, dtype=np.float32)
    put("gmask", np.stack([np.concatenate([s, s + eye, s, s + eye], 1) for s in (up, up.T)], 1))
    put("amask", np.stack([up.T, up], 1))
    bd = {n: (i[:, None] // n == i[None] // n).astype(np.float32) for n in (16, 32, 64, 128)}
    put("bd16", bd[16])
    put("off32", bd[32] - bd[16])
    put("off64", bd[64] - bd[32])
    put("off128", bd[128] - bd[64])
    put("ssdmask", np.stack([np.where(s + eye > 0, 0.0, NEG) for s in (up, up.T)], 1))
    col = np.arange(64)
    first = np.clip(col - 8, 0, 48)
    ok = (col[None] >= first[:, None]) & (col[None] < first[:, None] + 16)
    put("namask", np.tile(np.where(ok, 0.0, NEG), (2, 4)))
    put("pref", np.tile(np.arange(4, 0, -1, dtype=np.float32), (P, 1)))
    return c


class Steps:

    def __init__(self, eng, sem, turn=0, per=0, before=0):
        self.eng, self.sem, self.base, self.per, self.n = eng, sem, turn * per if per else 0, per, before
        self.before = before

    def put(self, ins):
        ins.then_inc(self.sem, 1)
        self.n += 1

    def settle(self):
        self.eng.wait_ge(self.sem, self.base + self.n)

    def do(self, ins):
        self.put(ins)
        self.settle()

    def end(self):
        assert self.n - self.before == self.per, f"a turn takes {self.n - self.before} steps, not {self.per}"


_phase = [0]


@contextmanager
def phase(nc, names):
    _phase[0] += 1
    with ExitStack() as st:
        sems = namedtuple("Semaphores", names)(*(st.enter_context(nc.semaphore(f"{n}_{_phase[0]}")) for n in names.split()))
        yield sems
        for s in sems:
            nc.sync.sem_clear(s)
        nc.all_engine_barrier()


def const(k, name):
    at, n = CONSTS[name]
    return k.const[:, at:at + n]


def col(k, name, j=0, n=1):
    at, _ = COLS[name]
    return k.cols[:, k.layer, at + j:at + j + n]


def three(ap, a):
    return ap.rearrange("p (a b) -> p a b", a=a)



STREAM = "loaded0 loaded1 slab_free0 slab_free1 tile_done bank_free"


def load_slabs(sp, s, ring, w, col0, turns):
    wv = w.rearrange("(kt p) c -> p kt c", p=P)
    loaded, free = (s.loaded0, s.loaded1), (s.slab_free0, s.slab_free1)
    with sp.Fori(0, turns) as it:
        for h in range(2):
            sp.wait_ge(free[h], it + 1)
            sp.dma_start(ring[:, h], wv[:, :, bass.ds(it * 1024 + (col0 + 512 * h), 512)]).then_inc(loaded[h], 16)


def multiply_slabs(pe, nc, s, ring, rhs, banks, turns, out=None):
    loaded, free = (s.loaded0, s.loaded1), (s.slab_free0, s.slab_free1)
    pe.sem_inc(s.slab_free0, 1)
    pe.sem_inc(s.slab_free1, 1)
    with pe.Fori(0, turns) as it:
        for h in range(2):
            pe.wait_ge(loaded[h], it * 16 + 16)
            for j in range(4):
                pe.wait_ge(s.bank_free, it * 8 + (4 * h + j + 1))
                dst = out(it, 4 * h + j) if out else banks[(4 * h + j) % len(banks)]
                for kt in range(KT):
                    mm = nc.tensor.matmul(dst, ring[:, h, kt, P * j:P * j + P], rhs[:, kt],
                                          start=kt == 0, stop=kt == KT - 1)
                mm.then_inc(s.tile_done, 1)
            pe.wait_ge(s.tile_done, it * 8 + (4 * h + 4))
            pe.sem_inc(free[h], 1)



def modulation(k):
    nc, l = k.nc, k.layer
    with ExitStack() as st:
        s = st.enter_context(phase(nc, STREAM + " silu_c vec"))
        sc = st.enter_context(nc.sbuf_tensor(f"silu_c{l}", [P, KT, 2], F32))
        block = st.enter_context(nc.Block())
        pm = three(k.bank[0][:, 0:96], 48)

        @block.sync
        def _(sp):
            load_slabs(sp, s, k.ring, k.d.w_mod[l], 0, 6)

        @block.scalar
        def _(act):
            nc.scalar.activation(sc[:], k.cvec[:], ACT.Silu).then_inc(s.silu_c, 1)

        @block.tensor
        def _(pe):
            pe.wait_ge(s.silu_c, 1)
            pe.sem_inc(s.bank_free, 48)
            multiply_slabs(pe, nc, s, k.ring, sc, [], 6, out=lambda it, j: pm[:, bass.ds(it * 8 + j, 1), :])

        @block.vector
        def _(v):
            do = Steps(v, s.vec)
            v.wait_ge(s.tile_done, 48)
            b = col(k, "b_mod", 0, 48)
            for c in range(2):
                do.do(nc.vector.tensor_tensor(k.mod[:, :, c], pm[:, :, c], b, ALU.add))
            for n, (name, at) in enumerate((("norm1", 8), ("norm2", 32))):
                for c in range(2):
                    do.do(nc.vector.scalar_tensor_tensor(k.nscale[:, n, :, c], k.mod[:, at:at + 8, c], 1.0,
                                                         col(k, name, 0, 8), ALU.add, ALU.mult))



def norm(k, src, dst, t0, mode):
    nc, l = k.nc, k.layer
    n = TT - t0
    with ExitStack() as st:
        s = st.enter_context(phase(nc, "square square_used sum root inv scaled moved"))
        sq = st.enter_context(nc.sbuf_tensor(f"sq{_phase[0]}", [P, 2, TT], F32))
        ms = st.enter_context(nc.sbuf_tensor(f"ms{_phase[0]}", [P, TT], F32))
        rinv = st.enter_context(nc.sbuf_tensor(f"rinv{_phase[0]}", [P, TT], F32))
        xr = st.enter_context(nc.sbuf_tensor(f"xr{_phase[0]}", [P, 2, TT], F32))
        block = st.enter_context(nc.Block())

        @block.scalar
        def _(act):
            for m in range(KT):
                if m >= 2:
                    act.wait_ge(s.square_used, m - 1)
                nc.scalar.activation(sq[:, m % 2, t0:], src[:, m, t0:], ACT.Square).then_inc(s.square, 1)
            act.wait_ge(s.root, 1)
            nc.scalar.activation(ms[:, t0:], ms[:, t0:], ACT.Sqrt).then_inc(s.root, 1)
            if mode == "cols":
                return
            shift = 0 if mode == 0 else 24
            for m in range(KT):
                act.wait_ge(s.scaled, m + 1)
                for c in range(t0 // LC, 2):
                    nc.scalar.activation(dst[:, m, LC * c:LC * c + LC], xr[:, m % 2, LC * c:LC * c + LC], ACT.Identity,
                                         bias=k.mod[:, shift + m, c:c + 1],
                                         scale=k.nscale[:, mode, m, c:c + 1]).then_inc(s.moved, 1)

        @block.tensor
        def _(pe):
            for m in range(KT):
                pe.wait_ge(s.square, m + 1)
                nc.tensor.matmul(k.bank[0][:, 0:n], const(k, "ones"), sq[:, m % 2, t0:],
                                 start=m == 0, stop=m == KT - 1).then_inc(s.square_used, 1)

        @block.vector
        def _(v):
            v.wait_ge(s.square_used, KT)
            nc.vector.tensor_scalar(ms[:, t0:], k.bank[0][:, 0:n], 1.0 / D, EPS, ALU.mult, ALU.add).then_inc(s.root, 1)
            v.wait_ge(s.root, 2)
            nc.vector.reciprocal(rinv[:, t0:], ms[:, t0:]).then_inc(s.inv, 1)
            v.wait_ge(s.inv, 1)
            each = 2 - t0 // LC
            for m in range(KT):
                if mode == "cols":
                    nc.vector.scalar_tensor_tensor(dst[:, m, t0:], src[:, m, t0:], k.normcol(m), rinv[:, t0:],
                                                   ALU.mult, ALU.mult).then_inc(s.scaled, 1)
                    continue
                if m >= 2:
                    v.wait_ge(s.moved, each * (m - 1))
                nc.vector.tensor_tensor(xr[:, m % 2, t0:], src[:, m, t0:], rinv[:, t0:], ALU.mult).then_inc(s.scaled, 1)



def project(k, w, col0, tiles, dst, t0=0):
    nc = k.nc
    with ExitStack() as st:
        s = st.enter_context(phase(nc, STREAM))
        block = st.enter_context(nc.Block())
        banks = [b[:, t0:] for b in k.bank[0:4]]
        turns = tiles // 8

        @block.sync
        def _(sp):
            load_slabs(sp, s, k.ring, w, col0, turns)

        @block.tensor
        def _(pe):
            multiply_slabs(pe, nc, s, k.ring, k.h[:, :, t0:], banks, turns)

        @block.scalar
        def _(act):
            act.sem_inc(s.bank_free, 4)
            with act.Fori(0, turns) as it:
                for j in range(8):
                    act.wait_ge(s.tile_done, it * 8 + (j + 1))
                    nc.scalar.activation(dst[:, bass.ds(it * 8 + j, 1), t0:], three(banks[j % 4], 1), ACT.Copy)\
                        .then_inc(s.bank_free, 1)


def merge(k, b, src, t0):
    nc, l = k.nc, k.layer
    wg = k.d.w_in[l].rearrange("(kt p) c -> p kt c", p=P)
    wb = k.d.w_branch[l, b].rearrange("(kt p) c -> p kt c", p=P)
    with ExitStack() as st:
        s = st.enter_context(phase(nc, "loaded0 loaded1 slab_free gate_done proj_done gate_free sig_done added"))
        sg = st.enter_context(nc.sbuf_tensor(f"sg{l}{b}", [P, 2, TT], F32))
        block = st.enter_context(nc.Block())
        n = TT - t0
        turns = KT // 4
        ring = k.ring[:].rearrange("p h kt c -> p h (kt c)")

        def slab(h):
            return ring[:, h].rearrange("p (w kt c) -> p w kt c", w=2, kt=KT)

        @block.sync
        def _(sp):
            with sp.Fori(0, turns) as it:
                for h in range(2):
                    sp.wait_ge(s.slab_free, it * 2 + (h + 1))
                    loaded = (s.loaded0, s.loaded1)[h]
                    sp.dma_start(slab(h)[:, 0], wg[:, :, bass.ds(it * 512 + (C_GATE + D * b + 256 * h), 256)]).then_inc(loaded, 16)
                    sp.dma_start(slab(h)[:, 1], wb[:, :, bass.ds(it * 512 + 256 * h, 256)]).then_inc(loaded, 16)

        @block.tensor
        def _(pe):
            pe.sem_inc(s.slab_free, 2)
            with pe.Fori(0, turns) as it:
                for h in range(2):
                    pe.wait_ge((s.loaded0, s.loaded1)[h], it * 32 + 32)
                    for j in range(2):
                        t = 2 * h + j
                        pe.wait_ge(s.gate_free, it * 4 + (t + 1))
                        for kt in range(KT):
                            mm = nc.tensor.matmul(k.bank[t % 2][:, 0:n], slab(h)[:, 0, kt, P * j:P * j + P], k.h[:, kt, t0:],
                                                  start=kt == 0, stop=kt == KT - 1)
                        mm.then_inc(s.gate_done, 1)
                        for kt in range(KT):
                            mm = nc.tensor.matmul(k.bank[2 + t % 2][:, 0:n], slab(h)[:, 1, kt, P * j:P * j + P], src[:, kt, t0:],
                                                  start=kt == 0, stop=kt == KT - 1)
                        mm.then_inc(s.proj_done, 1)
                    pe.wait_ge(s.proj_done, it * 4 + (2 * h + 2))
                    pe.sem_inc(s.slab_free, 1)

        @block.scalar
        def _(act):
            act.sem_inc(s.gate_free, 2)
            with act.Fori(0, turns) as it:
                for t in range(4):
                    act.wait_ge(s.gate_done, it * 4 + (t + 1))
                    act.wait_ge(s.gate_free, it * 4 + (t + 1))
                    nc.scalar.activation(sg[:, t % 2, t0:], k.bank[t % 2][:, 0:n], ACT.Sigmoid).then_inc(s.sig_done, 1)

        @block.vector
        def _(v):
            with v.Fori(0, turns) as it:
                for t in range(4):
                    v.wait_ge(s.sig_done, it * 4 + (t + 1))
                    v.wait_ge(s.proj_done, it * 4 + (t + 1))
                    dst = k.acc[:, bass.ds(it * 4 + t, 1), t0:]
                    a, pj = three(sg[:, t % 2, t0:], 1), three(k.bank[2 + t % 2][:, 0:n], 1)
                    if b == 0:
                        nc.vector.tensor_tensor(dst, a, pj, ALU.mult).then_inc(s.gate_free, 1)
                    else:
                        nc.vector.tensor_tensor(a, a, pj, ALU.mult).then_inc(s.added, 1)
                        v.wait_ge(s.added, it * 4 + (t + 1))
                        nc.vector.tensor_tensor(dst, dst, a, ALU.add).then_inc(s.gate_free, 1)


def residual_out(k, t0):
    nc, l = k.nc, k.layer
    with ExitStack() as st:
        s = st.enter_context(phase(nc, STREAM))
        block = st.enter_context(nc.Block())
        banks = [b[:, t0:] for b in k.bank[0:4]]

        @block.sync
        def _(sp):
            load_slabs(sp, s, k.ring, k.d.w_out[l], 0, 1)

        @block.tensor
        def _(pe):
            multiply_slabs(pe, nc, s, k.ring, k.acc[:, :, t0:], banks, 1)

        @block.vector
        def _(v):
            add_gated(nc, v, s, k, banks, 16, t0)


def add_gated(nc, v, s, k, banks, at, t0):
    v.sem_inc(s.bank_free, 4)
    for m in range(KT):
        v.wait_ge(s.tile_done, m + 1)
        for c in range(t0 // LC, 2):
            ins = nc.vector.scalar_tensor_tensor(k.x[:, m, LC * c:LC * c + LC], banks[m % 4][:, LC * c - t0:LC * c - t0 + LC],
                                                 k.mod[:, at + m, c:c + 1], k.x[:, m, LC * c:LC * c + LC], ALU.mult, ALU.add)
        ins.then_inc(s.bank_free, 1)



def conv_project(k, xbc):
    nc, l = k.nc, k.layer
    with ExitStack() as st:
        s = st.enter_context(phase(nc, STREAM + " padded taps conv_done taps_free"))
        raw = st.enter_context(nc.sbuf_tensor(f"raw{l}", [P, 2, 2, LC + 4], F32))
        cv = st.enter_context(nc.sbuf_tensor(f"conv{l}", [P, 2, 2, LC], F32))
        block = st.enter_context(nc.Block())
        banks = k.bank[0:4]

        @block.sync
        def _(sp):
            load_slabs(sp, s, k.ring, k.d.w_in[l], C_XBC, 2)

        @block.tensor
        def _(pe):
            multiply_slabs(pe, nc, s, k.ring, k.h, banks, 2)

        def finish(act, it, j):
            act.wait_ge(s.conv_done, it * 8 + (j + 1))
            nc.scalar.activation(xbc[:, bass.ds(it * 8 + j, 1), :], cv[:, j % 2].rearrange("p a b -> p (a b)").rearrange("p (o c) -> p o c", o=1),
                                 ACT.Silu).then_inc(s.taps_free, 1)

        @block.scalar
        def _(act):
            act.sem_inc(s.bank_free, 4)
            act.wait_ge(s.taps, 1)
            with act.Fori(0, 2) as it:
                for j in range(8):
                    act.wait_ge(s.tile_done, it * 8 + (j + 1))
                    act.wait_ge(s.taps_free, it * 8 + (j + 1))
                    nc.scalar.activation(raw[:, j % 2, :, 2:2 + LC], three(banks[j % 4][:], 2), ACT.Copy).then_inc(s.padded, 1)
                    act.wait_ge(s.padded, it * 8 + (j + 1))
                    act.sem_inc(s.bank_free, 1)
                    if j >= 1:
                        finish(act, it, j - 1)
                finish(act, it, 7)

        @block.vector
        def _(v):
            v.sem_inc(s.taps_free, 2)
            do = Steps(v, s.taps)
            do.do(nc.vector.memset(raw[:], 0.0))
            with v.Fori(0, 2) as it:
                do = Steps(v, s.taps, it, 40, 1)
                for j in range(8):
                    v.wait_ge(s.padded, it * 8 + (j + 1))
                    out = cv[:, j % 2]
                    cols = k.cols[:, l, COLS["conv_w"][0]:COLS["conv_w"][0] + 80].rearrange("p (i c) -> p i c", i=5)
                    for i in range(5):
                        w = cols[:, i, bass.ds(it * 8 + j, 1)]
                        src = raw[:, j % 2, :, i:i + LC]
                        if i == 0:
                            b = k.cols[:, l, bass.ds(it * 8 + (COLS["conv_b"][0] + j), 1)]
                            do.do(nc.vector.tensor_scalar(out, src, w, b, ALU.mult, ALU.add))
                        else:
                            do.do(nc.vector.scalar_tensor_tensor(out, src, w, out, ALU.mult, ALU.add))
                    v.sem_inc(s.conv_done, 1)
                do.end()


def prepare_ssd(k, xbc, xtok):
    nc, l = k.nc, k.layer
    with ExitStack() as st:
        s = st.enter_context(phase(nc, "swapped moved turned copied vec"))
        t1 = st.enter_context(nc.sbuf_tensor(f"rot{l}", [P, 2, LC], F32))
        block = st.enter_context(nc.Block())

        @block.tensor
        def _(pe):
            for j in range(8):
                if j >= 2:
                    pe.wait_ge(s.moved, j - 1)
                nc.tensor.matmul(k.bank[j % 2][:, 0:LC], const(k, "rope_perm"), xbc[:, 8 + j, LC:], start=True, stop=True)\
                    .then_inc(s.swapped, 1)
            for j in range(16):
                tt, f = j // 4, (j % 4) * 2
                if j >= 4:
                    pe.wait_ge(s.copied, j - 3)
                for q in range(2):
                    mm = nc.tensor.transpose(k.bank[4 + j % 4][:, P * q:P * q + P], xbc[:, f + q, P * tt:P * tt + P], const(k, "ident"))
                mm.then_inc(s.turned, 1)

        @block.vector
        def _(v):
            do = Steps(v, s.vec)
            for j in range(8):
                v.wait_ge(s.swapped, j + 1)
                u = xbc[:, 8 + j, LC:]
                nc.vector.tensor_tensor(t1[:, j % 2], k.bank[j % 2][:, 0:LC], const(k, "sin"), ALU.mult).then_inc(s.moved, 1)
                do.do(nc.vector.tensor_tensor(u, u, const(k, "cos"), ALU.mult))
                do.do(nc.vector.tensor_tensor(u, u, t1[:, j % 2], ALU.add))

        @block.scalar
        def _(act):
            for j in range(16):
                tt, f = j // 4, (j % 4) * 2
                act.wait_ge(s.turned, j + 1)
                nc.scalar.activation(xtok[:, tt, P * f:P * f + 2 * P], k.bank[4 + j % 4][:, 0:2 * P], ACT.Copy).then_inc(s.copied, 1)


def ssd_segments(d, t0):
    out = []
    for a in range(3):
        seg = sorted((ORDER[d][b], ORDER[d][a + 1:b]) for b in range(a + 1, 4) if ORDER[d][b] * P >= t0)
        out += [(ORDER[d][a], t, mid) for t, mid in seg]
    return out


def decays(k, rows, bias):
    nc, l = k.nc, k.layer
    with ExitStack() as st:
        s = st.enter_context(phase(nc, "loaded dt_logit act vec turned stored"))
        wdt = st.enter_context(nc.sbuf_tensor(f"wdt{l}", [P, KT, 32], F32))
        par = st.enter_context(nc.sbuf_tensor(f"dtpar{l}", [16, 4], F32))
        arr = st.enter_context(nc.sbuf_tensor(f"dtarr{l}", [16, 8, 2, TT], F32))
        block = st.enter_context(nc.Block())
        VEC_COLUMNS = 39
        LOGIT, E, DT, PRE, CUM, NCUM, REST, DA = range(8)

        @block.sync
        def _(sp):
            sp.dma_start(wdt[:], k.d.w_in[l].rearrange("(kt p) c -> p kt c", p=P)[:, :, C_DT:C_DT + 32]).then_inc(s.loaded, 16)
            sp.dma_start(par[:], k.d.dt_par[l]).then_inc(s.loaded, 16)

        @block.tensor
        def _(pe):
            pe.wait_ge(s.loaded, 32)
            for d in range(2):
                for kt in range(KT):
                    mm = nc.tensor.matmul(k.bank[d][0:16, :], wdt[:, kt, 16 * d:16 * d + 16], k.h[:, kt],
                                          start=kt == 0, stop=kt == KT - 1)
            mm.then_inc(s.dt_logit, 1)
            pe.wait_ge(s.vec, VEC_COLUMNS)
            turned = k.bank[2][:, 0:384].rearrange("p (a c) -> p a c", c=16)
            for n, (which, d, t) in enumerate((w, d, t) for w in (NCUM, REST, DT) for d in range(2) for t in range(4)):
                mm = nc.tensor.matmul(turned[:, n], arr[:, which, d, P * t:P * t + P], const(k, "ident")[0:16, 0:16],
                                      start=True, stop=True)
            mm.then_inc(s.turned, 1)


        @block.scalar
        def _(act):
            do = Steps(act, s.act)
            act.wait_ge(s.vec, 2)
            do.do(nc.scalar.activation(arr[:, E], arr[:, LOGIT], ACT.Abs))
            do.do(nc.scalar.activation(arr[:, E], arr[:, E], ACT.Exp, scale=-1.0))
            do.do(nc.scalar.activation(arr[:, E], arr[:, E], ACT.Ln, bias=1.0))
            do.do(nc.scalar.activation(par[:, 2:4], par[:, 2:4], ACT.Exp))

        @block.vector
        def _(v):
            do = Steps(v, s.vec)
            v.wait_ge(s.dt_logit, 1)
            for d in range(2):
                do.do(nc.vector.tensor_scalar(arr[:, LOGIT, d], k.bank[d][0:16, :], par[:, d:d + 1], None, ALU.add))
            v.wait_ge(s.act, 4)
            for d in range(2):
                do.do(nc.vector.scalar_tensor_tensor(arr[:, DT, d], arr[:, LOGIT, d], 0.0, arr[:, E, d], ALU.max, ALU.add))
            do.do(nc.vector.tensor_scalar(par[:, 2:4], par[:, 2:4], -1.0, None, ALU.mult))
            for d in range(2):
                do.put(nc.vector.tensor_scalar(arr[:, DA, d], arr[:, DT, d], par[:, 2 + d:3 + d], None, ALU.mult))
            do.settle()
            for d in range(2):
                for t in range(4):
                    x = slice(P * t, P * t + P)
                    do.put(nc.vector.tensor_tensor_scan(arr[:, PRE, d, x], const(k, "ones")[0:16], arr[:, DA, d, x], 0.0, ALU.mult, ALU.add))
            do.settle()
            tot = [[arr[:, PRE, d, P * t + P - 1:P * t + P] for t in range(4)] for d in range(2)]
            for t in range(4):
                x = slice(P * t, P * t + P)
                do.put(nc.vector.scalar_tensor_tensor(arr[:, NCUM, 1, x], arr[:, PRE, 1, x], tot[1][t], arr[:, DA, 1, x], ALU.subtract, ALU.subtract))
            do.settle()
            for d in range(2):
                for t in range(4):
                    x = slice(P * t, P * t + P)
                    dst = rows[:, d, x]
                    if d == 0:
                        do.put(nc.vector.tensor_copy(dst, arr[:, PRE, 0, x]))
                        do.put(nc.vector.tensor_scalar(arr[:, NCUM, 0, x], arr[:, PRE, 0, x], -1.0, None, ALU.mult))
                    else:
                        do.put(nc.vector.tensor_scalar(dst, arr[:, NCUM, 1, x], -1.0, None, ALU.mult))
            do.settle()
            for d in range(2):
                for t in range(4):
                    x = slice(P * t, P * t + P)
                    do.put(nc.vector.tensor_scalar(arr[:, REST, d, x], arr[:, NCUM, d, x], tot[d][t], None, ALU.add))
            do.settle()
            assert do.n == VEC_COLUMNS, do.n
            for d in range(2):
                for n, (i, t, mid) in enumerate(ssd_segments(d, 0)):
                    dst = rows[:, d, TT + P * n:TT + P * n + P]
                    src = rows[:, d, P * t:P * t + P]
                    do.do(nc.vector.tensor_copy(dst, src) if not mid else
                          nc.vector.tensor_scalar(dst, src, tot[d][mid[0]], None, ALU.add))
                    for m in mid[1:]:
                        do.do(nc.vector.tensor_scalar(dst, dst, tot[d][m], None, ALU.add))
            v.wait_ge(s.turned, 1)
            nc.vector.tensor_copy(bias[:].rearrange("p w d t c -> p (w d t c)"), k.bank[2][:, 0:384]).then_inc(s.turned, 1)
            v.wait_ge(s.turned, 2)

    with ExitStack() as st:
        s = st.enter_context(phase(nc, "stored"))
        block = st.enter_context(nc.Block())

        @block.sync
        def _(sp):
            sp.dma_start(k.d.ssd_rows, rows[:]).then_inc(s.stored, 16)
            sp.wait_ge(s.stored, 16)


def ssd_mix(k, xbc, xtok, bias, y, t0):
    nc, l = k.nc, k.layer
    n = TT - t0
    tiles = [t for t in range(NT) if P * t >= t0]
    with ExitStack() as st:
        s = st.enter_context(phase(nc, "row0 row1 row_free c_ready c_done c_copied x_ready diag expd off weighed summed y_free vec vec2"))
        rowb = st.enter_context(nc.sbuf_tensor(f"rowb{l}", [P, 2, 2, 10 * P], F32))
        e = st.enter_context(nc.sbuf_tensor(f"e{l}", [P, 2, 10 * P], F32))
        cb = st.enter_context(nc.sbuf_tensor(f"cb{l}", [P, NT, TT], F32))
        bst = st.enter_context(nc.sbuf_tensor(f"bst{l}", [P, TT], F32))
        xst = st.enter_context(nc.sbuf_tensor(f"xst{l}", [P, 2, NT, P], F32))
        hb = st.enter_context(nc.sbuf_tensor(f"hbias{l}", [P, 2, 3, 2, NT], F32))
        block = st.enter_context(nc.Block())
        segs = [ssd_segments(d, 0) for d in range(2)]
        use = [[(q, g) for q, g in enumerate(segs[d]) if g[1] * P >= t0] for d in range(2)]

        def runs(d):
            out = []
            for q, (i, t, _) in use[d]:
                if out and out[-1][0] == i and out[-1][1] + out[-1][3] == t and out[-1][2] + out[-1][3] == q:
                    out[-1][3] += 1
                else:
                    out.append([i, t, q, 1])
            return out

        def sources(d):
            out = []
            for q, (i, t, _) in use[d]:
                if out and out[-1][0] == i and out[-1][1] + out[-1][2] == q:
                    out[-1][2] += 1
                else:
                    out.append([i, q, 1])
            return out

        @block.sync
        def _(sp):
            with sp.Fori(0, GROUPS) as g:
                for hh in range(4):
                    sp.wait_ge(s.row_free, g * 4 + (hh + 1))
                    src = k.d.ssd_rows[bass.ds(g * 4 + hh, 1)].rearrange("h d c -> h (d c)").to_broadcast([P, 20 * P])
                    sp.dma_start(rowb[:, hh % 2].rearrange("p d c -> p (d c)"), src).then_inc((s.row0, s.row1)[hh % 2], 16)

        @block.vector
        def _(v):
            v.sem_inc(s.row_free, 2)
            do = Steps(v, s.vec2)
            do.do(nc.vector.memset(xst[:], 0.0))
            with v.Fori(0, GROUPS) as g:
                nc.vector.tensor_copy(bst[:].rearrange("p (o c) -> p o c", o=1), xbc[:, bass.ds(g + 8, 1), :]).then_inc(s.c_ready, 1)
                for hh in range(4):
                    h4 = g * 4 + (hh + 1)
                    par, buf = hh % 2, hh % 2
                    v.wait_ge(s.summed, h4)
                    nc.vector.tensor_copy(xst[:, par, :, 64 * par:64 * par + 64], xtok[:, :, bass.ds(g * 256 + 64 * hh, 64)])
                    nc.vector.tensor_copy(hb[:, buf].rearrange("p w d (t o) -> p (w d t) o", o=1),
                                          bias[:].rearrange("p w d t c -> p (w d t) c")[:, :, bass.ds(g * 4 + hh, 1)]).then_inc(s.x_ready, 1)
                    v.wait_ge(s.x_ready, h4)
                    v.wait_ge((s.row0, s.row1)[buf], g * 32 + 16 * (hh // 2 + 1))
                    for d in range(2):
                        for i in tiles:
                            mask = const(k, "ssdmask")[:, P * d:P * d + P]
                            ins = nc.vector.scalar_tensor_tensor(e[:, d, P * i:P * i + P], rowb[:, buf, d, P * i:P * i + P],
                                                                 hb[:, buf, 0, d, i:i + 1], mask, ALU.add, ALU.add)
                    ins.then_inc(s.diag, 1)
                    v.wait_ge(s.expd, h4)
                    v.wait_ge(s.c_copied, g * 4 + 4)
                    for d in range(2):
                        for i in tiles:
                            x = slice(P * i, P * i + P)
                            ins = nc.vector.scalar_tensor_tensor(e[:, d, x], e[:, d, x], hb[:, buf, 2, d, i:i + 1], cb[:, i, x], ALU.mult, ALU.mult)
                        for i, t, q, w in runs(d):
                            x = slice(TT + P * q, TT + P * (q + w))
                            ins = nc.vector.scalar_tensor_tensor(e[:, d, x], e[:, d, x], hb[:, buf, 2, d, i:i + 1],
                                                                 cb[:, i, P * t:P * (t + w)], ALU.mult, ALU.mult)
                    ins.then_inc(s.weighed, 1)
                    v.wait_ge(s.weighed, h4)
                    v.sem_inc(s.row_free, 1)
                    if par == 1:
                        f = g * 2 + hh // 2
                        v.wait_ge(s.summed, g * 4 + (hh + 2))
                        nc.vector.scalar_tensor_tensor(y[:, bass.ds(f, 1), t0:], xbc[:, bass.ds(f, 1), t0:],
                                                       k.cols[:, l, bass.ds(f + COLS["ssd_d"][0], 1)], three(k.bank[4 + (hh // 2) % 2][:, 0:n], 1),
                                                       ALU.mult, ALU.add).then_inc(s.y_free, 1)

        @block.scalar
        def _(act):
            with act.Fori(0, GROUPS) as g:
                act.wait_ge(s.c_done, g + 1)
                for i in range(NT):
                    ins = nc.scalar.activation(cb[:, i, t0:], k.bank[i][:, 0:n], ACT.Copy).then_inc(s.c_copied, 1)
                for hh in range(4):
                    h4 = g * 4 + (hh + 1)
                    act.wait_ge(s.diag, h4)
                    lo = P * tiles[0]
                    nc.scalar.activation(e[:, :, lo:TT], e[:, :, lo:TT], ACT.Exp)
                    for d in range(2):
                        for i, q, w in sources(d):
                            x = slice(TT + P * q, TT + P * (q + w))
                            ins = nc.scalar.activation(e[:, d, x], rowb[:, hh % 2, d, x], ACT.Exp, bias=hb[:, hh % 2, 1, d, i:i + 1])
                    ins.then_inc(s.expd, 1)

        @block.tensor
        def _(pe):
            pe.sem_inc(s.summed, 1)
            pe.sem_inc(s.y_free, 2)
            with pe.Fori(0, GROUPS) as g:
                pe.wait_ge(s.c_ready, g + 1)
                pe.wait_ge(s.summed, g * 4 + 1)
                for i in range(NT):
                    mm = nc.tensor.matmul(k.bank[i][:, 0:n].rearrange("p (o c) -> p o c", o=1), bst[:, P * i:P * i + P], xbc[:, bass.ds(g + 12, 1), t0:], start=True, stop=True)
                mm.then_inc(s.c_done, 1)
                for hh in range(4):
                    ps = k.bank[4 + (hh // 2) % 2]
                    pe.wait_ge(s.weighed, g * 4 + (hh + 1))
                    if hh % 2 == 0:
                        pe.wait_ge(s.y_free, g * 2 + (hh // 2 + 1))
                    first = hh % 2 == 0
                    jobs = [(i, i, 1, P * i, d) for d in range(2) for i in tiles]
                    jobs += [(i, t, w, TT + P * q, d) for d in range(2) for i, t, q, w in runs(d)]
                    for i, t, w, c, d in jobs:
                        mm = nc.tensor.matmul(ps[:, P * t - t0:P * (t + w) - t0], xst[:, hh % 2, i], e[:, d, c:c + P * w],
                                              start=first, stop=True, skip_group_check=True)
                        first = False
                    mm.then_inc(s.summed, 1)


def gate_by_z(k, y, t0):
    nc, l = k.nc, k.layer
    with ExitStack() as st:
        s = st.enter_context(phase(nc, STREAM + " silu_done multiplied"))
        zs = st.enter_context(nc.sbuf_tensor(f"zs{l}", [P, 2, TT], F32))
        block = st.enter_context(nc.Block())
        banks = [b[:, t0:] for b in k.bank[0:4]]

        @block.sync
        def _(sp):
            load_slabs(sp, s, k.ring, k.d.w_in[l], C_Z, 1)

        @block.tensor
        def _(pe):
            multiply_slabs(pe, nc, s, k.ring, k.h[:, :, t0:], banks, 1)

        @block.scalar
        def _(act):
            act.sem_inc(s.bank_free, 4)
            for j in range(KT):
                act.wait_ge(s.tile_done, j + 1)
                if j >= 2:
                    act.wait_ge(s.multiplied, j - 1)
                nc.scalar.activation(zs[:, j % 2, t0:], banks[j % 4], ACT.Silu).then_inc(s.silu_done, 1)
                act.wait_ge(s.silu_done, j + 1)
                act.sem_inc(s.bank_free, 1)

        @block.vector
        def _(v):
            for j in range(KT):
                v.wait_ge(s.silu_done, j + 1)
                nc.vector.tensor_tensor(y[:, j, t0:], y[:, j, t0:], zs[:, j % 2, t0:], ALU.mult).then_inc(s.multiplied, 1)


def ssd_branch(k, t0):
    nc, l = k.nc, k.layer
    with ExitStack() as st:
        xbc = st.enter_context(nc.sbuf_tensor(f"xbc{l}", [P, 16, TT], F32))
        conv_project(k, xbc)
        xtok = k.acc[:].rearrange("p (t a) c -> p t (a c)", t=NT)
        prepare_ssd(k, xbc, xtok)
        bias = st.enter_context(nc.sbuf_tensor(f"dtcol{l}", [P, 3, 2, NT, 16], F32))
        with nc.sbuf_tensor(f"rows{l}", [16, 2, 10 * P], F32) as rows:
            decays(k, rows, bias)
        ssd_mix(k, xbc, xtok, bias, k.br, t0)
    gate_by_z(k, k.br, t0)
    k.normcol = lambda m: col(k, "ssd_norm", m)
    norm(k, k.br, k.br, t0, "cols")
    merge(k, 0, k.br, t0)



def project_tokens(k, w, col0, dst):
    nc = k.nc
    with ExitStack() as st:
        s = st.enter_context(phase(nc, "loaded0 loaded1 done copied"))
        block = st.enter_context(nc.Block())
        wv = w.rearrange("(kt p) c -> p kt c", p=P)

        @block.sync
        def _(sp):
            for h in range(2):
                sp.dma_start(k.ring[:, h], wv[:, :, col0 + 512 * h:col0 + 512 * h + 512]).then_inc((s.loaded0, s.loaded1)[h], 16)

        @block.tensor
        def _(pe):
            for h in range(2):
                pe.wait_ge((s.loaded0, s.loaded1)[h], 16)
                for t in range(NT):
                    j = 4 * h + t
                    for kt in range(KT):
                        mm = nc.tensor.matmul(k.bank[j][:], k.h[:, kt, P * t:P * t + P], k.ring[:, h, kt], start=kt == 0, stop=kt == KT - 1)
                    mm.then_inc(s.done, 1)

        @block.scalar
        def _(act):
            for j in range(8):
                act.wait_ge(s.done, j + 1)
                nc.scalar.activation(dst[:, j % 4, 512 * (j // 4):512 * (j // 4) + 512], k.bank[j][:], ACT.Copy).then_inc(s.copied, 1)


def attend(k, qk, vtok, y, t0):
    nc, l = k.nc, k.layer
    qt = list(range(t0 // P, NT))
    jobs = [(h, q) for h in range(2) for q in qt]
    NJ = len(jobs)
    NL = 4
    with ExitStack() as st:
        s = st.enter_context(phase(nc, "bias0 bias1 bias_free masked staged pair_free scores context_in latent_in maxed exped normed turned turned_out weighed out_done out_read vec"))
        bias = st.enter_context(nc.sbuf_tensor(f"nabias{l}", [P, 2, 4, 4, 64], F32))
        qst = st.enter_context(nc.sbuf_tensor(f"qst{l}", [P, TT], F32))
        kst = st.enter_context(nc.sbuf_tensor(f"kst{l}", [P, TT], F32))
        vst = st.enter_context(nc.sbuf_tensor(f"vst{l}", [P, 2, NT, P], F32))
        sc = st.enter_context(nc.sbuf_tensor(f"sc{l}", [P, 2, TT], F32))
        pt = st.enter_context(nc.sbuf_tensor(f"pt{l}", [P, 2, NT, P], F32))
        mx = st.enter_context(nc.sbuf_tensor(f"mx{l}", [P, 2, 4], F32))
        block = st.enter_context(nc.Block())

        def keys(q):
            return TT if q >= 2 else LC

        @block.sync
        def _(sp):
            def load(f, b, sem):
                for h in range(2):
                    for q in range(2):
                        for rr in range(2):
                            r = 2 * q + rr
                            src = k.d.na_bias[l, bass.ds(2 * f + h, 1), 3 - r:7 - r].rearrange("o i c k -> c (o i) k")
                            sp.dma_start(bias[64 * rr:64 * rr + 64, b, 2 * h + q], src).then_inc(sem, 16)

            with sp.Fori(0, KT // 2) as it:
                for b in range(2):
                    sp.wait_ge(s.bias_free, it * 2 + (b + 1))
                    load(it * 2 + b, b, (s.bias0, s.bias1)[b])

        @block.gpsimd
        def _(pool):
            pool.sem_inc(s.bias_free, 2)
            with pool.Fori(0, KT // 2) as it:
                for b in range(2):
                    pool.wait_ge((s.bias0, s.bias1)[b], it * 128 + 128)
                    mask = const(k, "namask").rearrange("p (o c) -> p o c", o=1).to_broadcast([P, 4, 256])
                    dst = bias[:, b].rearrange("p j r c -> p j (r c)")
                    nc.gpsimd.tensor_tensor(dst, dst, mask, ALU.add).then_inc(s.masked, 1)

        def pair_turns(eng):
            return eng.Fori(0, KT // 2)

        @block.vector
        def _(v):
            v.sem_inc(s.pair_free, 1)
            nc.vector.memset(vst[:], 0.0).then_inc(s.vec, 1)
            v.wait_ge(s.vec, 1)
            with pair_turns(v) as it:
                for b in range(2):
                    f = it * 2 + b
                    v.wait_ge(s.pair_free, f + 1)
                    one = lambda ap: ap.rearrange("p (o c) -> p o c", o=1)
                    nc.vector.tensor_scalar(one(qst[:]), qk[:, bass.ds(f, 1), :], 0.125, None, ALU.mult)
                    nc.vector.tensor_copy(one(kst[:]), qk[:, bass.ds(f + 8, 1), :])
                    for h in range(2):
                        ins = nc.vector.tensor_copy(vst[:, h, :, 64 * h:64 * h + 64], vtok[:, :, bass.ds(f * P + 64 * h, 64)])
                    ins.then_inc(s.staged, 1)
                    for n, (h, q) in enumerate(jobs):
                        j = f * NJ + n
                        v.wait_ge(s.context_in, j + 1)
                        if q >= 2:
                            v.wait_ge(s.masked, f + 1)
                            nc.vector.tensor_tensor(sc[:, n % 2, LC:], k.bank[n % 2][:, LC:], bias[:, b, 2 * h + q - 2].rearrange("p r c -> p (r c)"), ALU.add)\
                                .then_inc(s.latent_in, 1)
                            v.wait_ge(s.latent_in, f * NL + (2 * h + q - 1))
                        nc.vector.tensor_reduce(mx[:, n % 2, 0:1], sc[:, n % 2, 0:keys(q)], AX.X, ALU.max).then_inc(s.vec, 1)
                        v.wait_ge(s.vec, j * 3 + 2)
                        nc.vector.tensor_scalar(mx[:, n % 2, 1:2], mx[:, n % 2, 0:1], -1.0, None, ALU.mult).then_inc(s.maxed, 1)
                        v.wait_ge(s.exped, j + 1)
                        nc.vector.reciprocal(mx[:, n % 2, 3:4], mx[:, n % 2, 2:3]).then_inc(s.vec, 1)
                        v.wait_ge(s.vec, j * 3 + 3)
                        nc.vector.tensor_scalar(sc[:, n % 2, 0:keys(q)], sc[:, n % 2, 0:keys(q)], mx[:, n % 2, 3:4], None, ALU.mult).then_inc(s.normed, 1)
                        v.wait_ge(s.turned, j + 1)
                        nc.vector.tensor_copy(pt[:, n % 2].rearrange("p t c -> p (t c)")[:, 0:keys(q)], k.bank[2 + n % 2][:, 0:keys(q)]).then_inc(s.turned_out, 1)
                        v.wait_ge(s.turned_out, j + 1)
                        nc.vector.memset(mx[:, n % 2, 0:1], 0.0).then_inc(s.vec, 1)
                    v.sem_inc(s.bias_free, 1)
                    v.wait_ge(s.out_done, f + 1)
                    nc.vector.tensor_copy(y[:, bass.ds(f, 1), t0:], one(k.bank[4][:, t0:])).then_inc(s.out_read, 1)

        @block.scalar
        def _(act):
            with pair_turns(act) as it:
                for b in range(2):
                    f = it * 2 + b
                    for n, (h, q) in enumerate(jobs):
                        j = f * NJ + n
                        act.wait_ge(s.scores, j + 1)
                        nc.scalar.activation(sc[:, n % 2, 0:LC], k.bank[n % 2][:, 0:LC], ACT.Copy).then_inc(s.context_in, 1)
                        act.wait_ge(s.maxed, j + 1)
                        nc.scalar.activation(sc[:, n % 2, 0:keys(q)], sc[:, n % 2, 0:keys(q)], ACT.Exp, bias=mx[:, n % 2, 1:2],
                                             accum_out=mx[:, n % 2, 2:3]).then_inc(s.exped, 1)

        @block.tensor
        def _(pe):
            with pair_turns(pe) as it:
                for b in range(2):
                    f = it * 2 + b
                    pe.wait_ge(s.staged, f + 1)

                    def scores(n):
                        h, q = jobs[n]
                        hs = slice(64 * h, 64 * h + 64)
                        nc.tensor.matmul(k.bank[n % 2][:, 0:keys(q)], qst[hs, P * q:P * q + P], kst[hs, 0:keys(q)],
                                         start=True, stop=True).then_inc(s.scores, 1)

                    scores(0)
                    for n, (h, q) in enumerate(jobs):
                        j = f * NJ + n
                        pe.wait_ge(s.normed, j + 1)
                        if n + 1 < NJ:
                            scores(n + 1)
                        for t in range(keys(q) // P):
                            mm = nc.tensor.transpose(k.bank[2 + n % 2][:, P * t:P * t + P], sc[:, n % 2, P * t:P * t + P], const(k, "ident"))
                        mm.then_inc(s.turned, 1)
                        pe.wait_ge(s.turned_out, j + 1)
                        for t in range(keys(q) // P):
                            mm = nc.tensor.matmul(k.bank[4][:, P * q:P * q + P], vst[:, h, t], pt[:, n % 2, t],
                                                  start=(n == 0 and t == 0), stop=True, skip_group_check=True)
                        if n == NJ - 1:
                            mm.then_inc(s.out_done, 1)
                    pe.wait_ge(s.out_done, f + 1)
                    pe.wait_ge(s.out_read, f + 1)
                    pe.sem_inc(s.pair_free, 1)


def natten_branch(k, t0):
    nc, l = k.nc, k.layer
    with ExitStack() as st:
        qk = st.enter_context(nc.sbuf_tensor(f"qk{l}", [P, 16, TT], F32))
        vtok = st.enter_context(nc.sbuf_tensor(f"vtok{l}", [P, NT, D], F32))
        project(k, k.d.w_in[l], C_Q, 16, qk)
        project_tokens(k, k.d.w_in[l], C_V, vtok)
        attend(k, qk, vtok, k.br, t0)
    merge(k, 2, k.br, t0)



def rwkv_low(k, low):
    nc, l = k.nc, k.layer
    with ExitStack() as st:
        s = st.enter_context(phase(nc, "loaded proj rawin vec shifted"))
        w = st.enter_context(nc.sbuf_tensor(f"wlow{l}", [P, KT, 2 * P], F32))
        raw = st.enter_context(nc.sbuf_tensor(f"rawlow{l}", [P, 2, 2, LC + 2], F32))
        block = st.enter_context(nc.Block())

        @block.sync
        def _(sp):
            sp.dma_start(w[:], k.d.w_in[l].rearrange("(kt p) c -> p kt c", p=P)[:, :, C_WA:C_WA + 2 * P]).then_inc(s.loaded, 16)

        @block.tensor
        def _(pe):
            pe.wait_ge(s.loaded, 16)
            for j in range(2):
                for kt in range(KT):
                    mm = nc.tensor.matmul(k.bank[j], w[:, kt, P * j:P * j + P], k.h[:, kt], start=kt == 0, stop=kt == KT - 1)
                mm.then_inc(s.proj, 1)

        @block.scalar
        def _(act):
            act.wait_ge(s.vec, 1)
            for j in range(2):
                act.wait_ge(s.proj, j + 1)
                nc.scalar.activation(raw[:, j, :, 1:1 + LC], three(k.bank[j], 2), ACT.Copy).then_inc(s.rawin, 1)
            act.wait_ge(s.vec, 1 + 6)
            nc.scalar.activation(low[0:64, 0], low[0:64, 0], ACT.Tanh)
            nc.scalar.activation(low[:, 1], low[:, 1], ACT.Sigmoid).then_inc(s.shifted, 1)
            act.wait_ge(s.shifted, 1)

        @block.vector
        def _(v):
            do = Steps(v, s.vec)
            do.do(nc.vector.memset(raw[:], 0.0))
            for j in range(2):
                v.wait_ge(s.rawin, j + 1)
                token_shift(nc, do, raw[:, j], three(low[:, j], 2), col(k, ("mu_wa", "mu_g")[j]))


def token_shift(nc, do, raw, out, mu):
    mid = raw[:, :, 1:1 + LC]
    do.do(nc.vector.tensor_tensor(out, raw[:, :, 0:LC], raw[:, :, 2:2 + LC], ALU.add))
    do.do(nc.vector.scalar_tensor_tensor(out, out, 0.5, mid, ALU.mult, ALU.subtract))
    do.do(nc.vector.scalar_tensor_tensor(out, out, mu, mid, ALU.mult, ALU.add))


STAGES = [
    (("b1", "b0", "b2", "copy"), ("b0", "b1", "b3", "vcopy")),
    (("b3", "X", "X", "add"), ("b2", "XT", "XT", "add")),
    (("b3", "b2", "b0", "copy"), ("b2", "b3", "b1", "vcopy")),
    (("b1", "X", "X", "add"), ("b0", "XT", "XT", "add")),
    (("b1", "b0", "b2", "copy"), ("b0", "b1", "b3", "vcopy")),
    (("b3", "X", "X", "add"), ("b2", "XT", "XT", "off32")),
    (("b1", "XT", "b0", "copy"),),
    (("X", "b0", "XT", "off64"), ("b0", "X", "X", "add")),
    (("b1", "XT", "b0", "copy"),),
    (("X", "b0", "XT", "off128"), ("b0", "X", "X", "add")),
    (("b1", "XT", "b0", "copy"),),
    (("X", "b0", "XT", "add"),),
]


def stage_counts():
    prod, a, v, out = 0, 0, 0, {}
    for n, stage in enumerate(STAGES):
        for q in range(2):
            first = prod
            prod += len(stage)
            a += sum(how == "copy" for *_, how in stage)
            v += sum(how != "copy" for *_, how in stage)
            out[n, q] = (first, a, v)
    return out, prod, a, v


COUNTS, N_PROD, N_EV_A, N_EV_V = stage_counts()


def rwkv_heads(k, low, y, t0):
    nc, l = k.nc, k.layer
    n = TT - t0
    TURNS = KT
    with ExitStack() as st:
        s = st.enter_context(phase(nc, "w_in w_free turn_free proj rawin shifted lora lact kksq kkn kkroot cen exps feat turned tok "
                                       "gdone gevac prod ev_a ev_v r_done r_in u_done u_in y_done y_in s_done s_in ysum mean_d yc sq "
                                       "var_d var_in root yn lnd bonus_in bonus_d padded vec"))

        def sb(name, *shape):
            return st.enter_context(nc.sbuf_tensor(f"{name}{l}", [P, *shape], F32))

        w3, lora, g2 = sb("w3", 3, KT, P), sb("lora", 2, P), sb("g2_", P)
        raw, rkv = sb("raw3", 3, 2, LC + 2), sb("rkv", 3, TT)
        ld, aa, ci, ce = sb("ld", 2, TT), sb("aa", 2, TT), sb("ci", 2, TT), sb("ce", 2, TT)
        kk, ks, tmp = sb("kk", TT), sb("ks", TT), sb("tmp", TT)
        pc, half, em = sb("pc", N_RCOL), sb("half", 2, 4), sb("em", 2, 4)
        ar, bk = sb("ar", 2, 4, 2, P), sb("bk", 2, 2, TT)
        vpad, bkt = sb("vpad", 2, 4, P), sb("bkt", 2, 2, 4, P)
        s0, rs, up = sb("s0", 2, P), sb("rs_", 2, P), sb("up", 2, 2, P)
        t1 = rs
        buf = [{b: sb(f"{b}q{q}", 4, P) for b in ("b0", "b1", "b2", "b3", "X", "XT", "A")} for q in range(2)]
        gm = [sb(f"gm{q}", 4, 4, P) for q in range(2)]
        yy = aa
        r, kf, vv = (rkv[:, j] for j in range(3))
        block = st.enter_context(nc.Block())
        win = k.d.w_in[l].rearrange("(kt p) c -> p kt c", p=P)
        ident = const(k, "ident")
        flat = lambda b: b[:].rearrange("p a c -> p (a c)")
        one = lambda ap: ap.rearrange("p (o c) -> p o c", o=1)

        def chunk(z, pos):
            return slice(P * ORDER[z][pos], P * ORDER[z][pos] + P)

        def wanted(pos):
            return P * ORDER[0][pos] >= t0 or P * ORDER[1][pos] >= t0

        @block.sync
        def _(sp):
            with sp.Fori(0, TURNS) as it:
                sp.wait_ge(s.w_free, it + 1)
                for j in range(3):
                    sp.dma_start(w3[:, j], win[:, :, bass.ds(it * P + (C_R + D * j), P)]).then_inc(s.w_in, 16)
                sp.dma_start(lora[:], k.d.wa2[l, :, :, bass.ds(it * P, P)]).then_inc(s.w_in, 16)
                sp.dma_start(g2[:], k.d.g2[l, :, bass.ds(it * P, P)]).then_inc(s.w_in, 16)

        @block.tensor
        def _(pe):
            pe.sem_inc(s.w_free, 1)
            mm = nc.tensor.matmul
            with pe.Fori(0, TURNS) as it:
                pe.wait_ge(s.w_in, it * 80 + 80)
                pe.wait_ge(s.turn_free, it + 1)
                for j in range(3):
                    for kt in range(KT):
                        m = mm(k.bank[j], w3[:, j, kt], k.h[:, kt], start=kt == 0, stop=kt == KT - 1)
                    m.then_inc(s.proj, 1)
                for z in range(2):
                    mm(k.bank[3 + z], lora[0:64, z], low[0:64, 0], start=True, stop=True)
                for z in range(2):
                    mm(k.bank[5 + z], lora[64:128, z], low[64:128, 0], start=True, stop=True)
                mm(k.bank[7], g2[:], low[:, 1], start=True, stop=True).then_inc(s.lora, 1)
                pe.wait_ge(s.lora, it + 1)
                pe.sem_inc(s.w_free, 1)
                pe.wait_ge(s.kksq, it + 1)
                mm(k.bank[0], const(k, "headones"), tmp[:], start=True, stop=True).then_inc(s.kkn, 1)
                pe.wait_ge(s.feat, it + 1)
                for c in range(4):
                    m = nc.tensor.transpose(k.bank[1][:, P * c:P * c + P], vv[:, P * c:P * c + P], ident)
                m.then_inc(s.turned, 1)
                for j in range(4):
                    for c in range(4):
                        m = nc.tensor.transpose(k.bank[2 + j][:, P * c:P * c + P], bk[:, j // 2, j % 2, P * c:P * c + P], ident)
                    m.then_inc(s.turned, 1)
                pe.wait_ge(s.tok, it * 5 + 5)
                for pp in range(2):
                    for q in range(2):
                        pos = 2 * pp + q
                        pe.wait_ge(s.gevac, it * 4 + pos) if pos else None
                        for p in range(4):
                            h, z = p // 2, p % 2
                            hs, c = slice(64 * h, 64 * h + 64), ORDER[z][pos]
                            x = slice(P * c, P * c + P)
                            arc = ar[hs, z, c].rearrange("p a c -> p (a c)")
                            mm(k.bank[p][:, 0:256], bk[hs, z, 0, x], arc, start=True, stop=True, skip_group_check=True)
                            mm(k.bank[p][:, 256:512], bk[hs, z, 1, x], arc, start=False, stop=True, skip_group_check=True)
                            m = mm(k.bank[4 + h][:, P * z:P * z + P], ar[hs, z, c, 0], bk[hs, z, 0, x], start=z == 0, stop=True, skip_group_check=True)
                        m.then_inc(s.gdone, 1)
                    turn2 = it * 2 + pp
                    for q in range(2):
                        pe.wait_ge(s.gevac, it * 4 + (2 * pp + q + 1))
                    for g, stage in enumerate(STAGES):
                        for q in range(2):
                            if g:
                                _, a, v = COUNTS[g - 1, q]
                                pe.wait_ge(s.ev_a, turn2 * N_EV_A + a)
                                pe.wait_ge(s.ev_v, turn2 * N_EV_V + v)
                            for j, (left, right, _, _) in enumerate(stage):
                                for p in range(4):
                                    m = mm(k.bank[2 * q + j][:, P * p:P * p + P], buf[q][left][:, p], buf[q][right][:, p],
                                           start=p == 0, stop=True, skip_group_check=True)
                                m.then_inc(s.prod, 1)
                    for q in range(2):
                        pos = 2 * pp + q
                        P4 = it * 4 + (pos + 1)
                        pe.wait_ge(s.ev_v, turn2 * N_EV_V + N_EV_V)
                        if pos:
                            pe.wait_ge(s.s_in, it * 3 + pos)
                        else:
                            pe.wait_ge(s.padded, it + 1)
                        for z in range(2):
                            c = ORDER[z][pos]
                            mm(k.bank[4][:, P * z:P * z + P], ar[:, z, c, 0], s0[:, z], start=z == 0, stop=True, skip_group_check=True)
                            for h in range(2):
                                m = mm(k.bank[4][:, P * z + 64 * h:P * z + 64 * h + 64], gm[q][:, 2 * h + z, 2], vpad[:, h, c, 64 * h:64 * h + 64],
                                       start=False, stop=True, skip_group_check=True)
                        m.then_inc(s.r_done, 1)
                        pe.wait_ge(s.r_in, P4)
                        for z in range(2):
                            for h in range(2):
                                m = mm(k.bank[5][:, P * z + 64 * h:P * z + 64 * h + 64], buf[q]["XT"][:, 2 * h + z], rs[:, z, 64 * h:64 * h + 64],
                                       start=z + h == 0, stop=True, skip_group_check=True)
                        m.then_inc(s.u_done, 1)
                        pe.wait_ge(s.u_in, P4)
                        if pos < 3:
                            for z in range(2):
                                c = ORDER[z][pos]
                                for h in range(2):
                                    mm(k.bank[7][:, P * z:P * z + P], bkt[:, z, 0, c], up[:, z, h], start=z + h == 0, stop=True, skip_group_check=True)
                                    m = mm(k.bank[7][:, P * z:P * z + P], bkt[:, z, 1, c], vpad[:, h, c], start=False, stop=True, skip_group_check=True)
                        if pos:
                            pe.wait_ge(s.y_in, it * 4 + pos)
                        for z in range(2):
                            c = ORDER[z][pos]
                            my = mm(k.bank[6][:, P * z:P * z + P], s0[:, z], ar[:, z, c, 1], start=z == 0, stop=True, skip_group_check=True)
                            for h in range(2):
                                mm(k.bank[6][:, P * z:P * z + P], vpad[:, h, c], gm[q][:, 2 * h + z, 3], start=False, stop=True, skip_group_check=True)
                                my = mm(k.bank[6][:, P * z:P * z + P], up[:, z, h], gm[q][:, 2 * h + z, 1], start=False, stop=True, skip_group_check=True)
                        my.then_inc(s.y_done, 1)
                pe.wait_ge(s.ysum, it + 1)
                mm(k.bank[0][:, 0:n], const(k, "headones"), ks[:, t0:], start=True, stop=True).then_inc(s.mean_d, 1)
                pe.wait_ge(s.sq, it + 1)
                mm(k.bank[1][:, 0:n], const(k, "headones"), tmp[:, t0:], start=True, stop=True).then_inc(s.var_d, 1)
                pe.wait_ge(s.bonus_in, it + 1)
                mm(k.bank[2][:, 0:n], const(k, "headones"), kk[:, t0:], start=True, stop=True).then_inc(s.bonus_d, 1)

        @block.scalar
        def _(act):
            ac = nc.scalar.activation
            with act.Fori(0, TURNS) as it:
                act.wait_ge(s.padded, it + 1)
                for j in range(3):
                    act.wait_ge(s.proj, it * 3 + (j + 1))
                    ac(raw[:, j, :, 1:1 + LC], three(k.bank[j], 2), ACT.Copy).then_inc(s.rawin, 1)
                act.wait_ge(s.lora, it + 1)
                for z in range(2):
                    ac(ld[:, z], k.bank[3 + z], ACT.Sigmoid, bias=pc[:, W0 + z:W0 + z + 1])
                    ac(aa[:, z], k.bank[5 + z], ACT.Sigmoid, bias=pc[:, A0 + z:A0 + z + 1])
                ac(y[:, bass.ds(it, 1), t0:], one(k.bank[7][:, t0:]), ACT.Copy).then_inc(s.lact, 1)
                act.wait_ge(s.kkn, it + 1)
                ac(tmp[:], k.bank[0], ACT.Sqrt).then_inc(s.kkroot, 1)
                act.wait_ge(s.cen, it + 1)
                ac(ld[:], ci[:], ACT.Exp, scale=-1.0)
                ac(ci[:], ci[:], ACT.Exp)
                ac(em[:], half[:], ACT.Exp)
                ac(ce[:], ce[:], ACT.Exp).then_inc(s.exps, 1)
                act.wait_ge(s.turned, it * 5 + 1)
                for h in range(2):
                    m = ac(vpad[:, h, :, 64 * h:64 * h + 64], three(k.bank[1], 4)[:, :, 64 * h:64 * h + 64], ACT.Copy)
                m.then_inc(s.tok, 1)
                for j in range(4):
                    act.wait_ge(s.turned, it * 5 + (j + 2))
                    ac(bkt[:, j // 2, j % 2], three(k.bank[2 + j], 4), ACT.Copy).then_inc(s.tok, 1)
                for pp in range(2):
                    turn2 = it * 2 + pp
                    for g, stage in enumerate(STAGES):
                        for q in range(2):
                            first, _, _ = COUNTS[g, q]
                            for j, (_, _, into, how) in enumerate(stage):
                                if how == "copy":
                                    act.wait_ge(s.prod, turn2 * N_PROD + (first + j + 1))
                                    ac(flat(buf[q][into]), k.bank[2 * q + j], ACT.Copy).then_inc(s.ev_a, 1)
                    for q in range(2):
                        pos = 2 * pp + q
                        act.wait_ge(s.y_done, it * 4 + (pos + 1))
                        for z in range(2):
                            m = ac(yy[:, z, chunk(z, pos)], k.bank[6][:, P * z:P * z + P], ACT.Copy)
                        m.then_inc(s.y_in, 1)
                act.wait_ge(s.yc, it + 1)
                ac(tmp[:, t0:], ks[:, t0:], ACT.Square).then_inc(s.sq, 1)
                act.wait_ge(s.var_in, it + 1)
                ac(tmp[:, t0:], tmp[:, t0:], ACT.Sqrt).then_inc(s.root, 1)
                act.wait_ge(s.yn, it + 1)
                ac(ks[:, t0:], ks[:, t0:], ACT.Identity, bias=pc[:, LNB:LNB + 1], scale=pc[:, LNW:LNW + 1]).then_inc(s.lnd, 1)

        @block.vector
        def _(v):
            tt, stt, ts = nc.vector.tensor_tensor, nc.vector.scalar_tensor_tensor, nc.vector.tensor_scalar
            v.sem_inc(s.turn_free, 1)
            do = Steps(v, s.vec)
            for t in (raw, vpad, up):
                do.do(nc.vector.memset(t[:], 0.0))
            with v.Fori(0, TURNS) as it:
                do = Steps(v, s.vec, it, 91, 3)
                p1 = lambda j: pc[:, j:j + 1]
                do.do(nc.vector.tensor_copy(one(pc[:]), k.rcols[:, l, bass.ds(it, 1), :]))
                nc.vector.memset(s0[:], 0.0).then_inc(s.padded, 1)
                v.wait_ge(s.padded, it + 1)
                for j in range(3):
                    v.wait_ge(s.rawin, it * 3 + (j + 1))
                    token_shift(nc, do, raw[:, j], three(rkv[:, j], 2), p1(MU + j))
                do.do(ts(kk[:], kf, p1(KK), None, ALU.mult))
                tt(tmp[:], kk[:], kk[:], ALU.mult).then_inc(s.kksq, 1)
                v.wait_ge(s.lact, it + 1)
                do.do(ts(ld[:], ld[:], -DECAY_SCALE, None, ALU.mult))
                for z, pre in ((0, ce), (1, ci)):
                    for c in range(4):
                        x = slice(P * c, P * c + P)
                        do.put(nc.vector.tensor_tensor_scan(pre[:, z, x], const(k, "ones"), ld[:, z, x], 0.0, ALU.mult, ALU.add))
                do.settle()
                for z, pre in ((0, ce), (1, ci)):
                    do.put(ts(half[:, z], three(pre[:, z], 4)[:, :, P - 1], 0.5, None, ALU.mult))
                do.settle()
                hb = [half[:, z].unsqueeze(2).to_broadcast([P, 4, P]) for z in range(2)]
                do.do(tt(three(ci[:, 0], 4), three(ce[:, 0], 4), hb[0], ALU.subtract))
                do.do(tt(three(ce[:, 1], 4), hb[1], three(ci[:, 1], 4), ALU.subtract))
                do.do(tt(ce[:, 0], ci[:, 0], ld[:, 0], ALU.subtract))
                tt(ci[:, 1], ce[:, 1], ld[:, 1], ALU.add).then_inc(s.cen, 1)
                v.wait_ge(s.cen, it + 1)
                v.wait_ge(s.kkroot, it + 1)
                do.do(ts(tmp[:], tmp[:], 1e-12, None, ALU.max))
                do.do(nc.vector.reciprocal(tmp[:], tmp[:]))
                do.do(tt(kk[:], kk[:], tmp[:], ALU.mult))
                for z in range(2):
                    do.do(ts(bk[:, z, 1], aa[:, z], -1.0, p1(KA), ALU.add, ALU.mult))
                    do.do(stt(bk[:, z, 1], bk[:, z, 1], 1.0, kf, ALU.add, ALU.mult))
                    do.put(stt(bk[:, z, 0], kk[:], -1.0, aa[:, z], ALU.mult, ALU.mult))
                do.do(tt(ks[:], bk[:, 0, 1], bk[:, 1, 1], ALU.add))
                v.wait_ge(s.exps, it + 1)
                for z in range(2):
                    do.put(tt(ar[:, z, :, 0], three(ce[:, z], 4), three(kk[:], 4), ALU.mult))
                    do.put(tt(ar[:, z, :, 1], three(ci[:, z], 4), three(r, 4), ALU.mult))
                    for j in range(2):
                        do.put(tt(bk[:, z, j], bk[:, z, j], ld[:, z], ALU.mult))
                do.settle()
                stt(kk[:], ks[:], p1(RK), r, ALU.mult, ALU.mult).then_inc(s.feat, 1)
                for pp in range(2):
                    turn2 = it * 2 + pp
                    for q in range(2):
                        pos = 2 * pp + q
                        b = buf[q]
                        v.wait_ge(s.gdone, it * 4 + (pos + 1))
                        for p in range(4):
                            do.put(tt(gm[q][:, p].rearrange("p a c -> p (a c)"), k.bank[p], three(const(k, "gmask"), 2)[:, p % 2], ALU.mult))
                        for h in range(2):
                            do.put(tt(b["A"][:, 2 * h:2 * h + 2].rearrange("p a c -> p (a c)"), k.bank[4 + h][:, 0:256], const(k, "amask"), ALU.mult))
                        do.settle()
                        bd = one(const(k, "bd16")).to_broadcast([P, 4, P])
                        do.put(tt(b["b0"][:], b["A"][:], bd, ALU.mult))
                        do.put(tt(b["b1"][:], gm[q][:, :, 0], bd, ALU.mult))
                        do.settle()
                        eye = one(ident).to_broadcast([P, 4, P])
                        tt(b["X"][:], b["b0"][:], eye, ALU.add)
                        tt(b["XT"][:], b["b1"][:], eye, ALU.add).then_inc(s.gevac, 1)
                    for g, stage in enumerate(STAGES):
                        for q in range(2):
                            first, _, _ = COUNTS[g, q]
                            for j, (_, _, into, how) in enumerate(stage):
                                if how == "copy":
                                    continue
                                v.wait_ge(s.prod, turn2 * N_PROD + (first + j + 1))
                                dst, bank = flat(buf[q][into]), k.bank[2 * q + j]
                                if how == "vcopy":
                                    nc.vector.tensor_copy(dst, bank).then_inc(s.ev_v, 1)
                                elif how == "add":
                                    tt(dst, dst, bank, ALU.add).then_inc(s.ev_v, 1)
                                else:
                                    tt(dst, dst, bank, ALU.add)
                                    off = one(const(k, how)).to_broadcast([P, 4, P])
                                    tt(buf[q]["b1"][:], buf[q]["A"][:], off, ALU.mult).then_inc(s.ev_v, 1)
                    for q in range(2):
                        pos = 2 * pp + q
                        P4 = it * 4 + (pos + 1)
                        v.wait_ge(s.r_done, P4)
                        nc.vector.tensor_copy(flat(rs), k.bank[4][:, 0:256]).then_inc(s.r_in, 1)
                        v.wait_ge(s.u_done, P4)
                        if pos:
                            v.wait_ge(s.y_done, it * 4 + pos)
                        ub = k.bank[5][:, 0:256].rearrange("p (z h c) -> p z h c", z=2, h=2)
                        for h in range(2):
                            m = nc.vector.tensor_copy(up[:, :, h, 64 * h:64 * h + 64], ub[:, :, h])
                        m.then_inc(s.u_in, 1)
                        v.wait_ge(s.y_done, P4)
                        if pos < 3:
                            for z in range(2):
                                c, c2 = ORDER[z][pos], ORDER[z][pos + 1]
                                e1, e2 = em[:, z, c:c + 1], em[:, z, c2:c2 + 1]
                                do.do(stt(t1[:, z], k.bank[7][:, P * z:P * z + P], e1, const(k, "headones"), ALU.mult, ALU.mult))
                                do.do(stt(s0[:, z], s0[:, z], e1, t1[:, z], ALU.mult, ALU.add))
                                m = ts(s0[:, z], s0[:, z], e2, None, ALU.mult)
                            m.then_inc(s.s_in, 1)
                v.wait_ge(s.y_in, it * 4 + 4)
                tt(ks[:, t0:], yy[:, 0, t0:], yy[:, 1, t0:], ALU.add).then_inc(s.ysum, 1)
                v.wait_ge(s.mean_d, it + 1)
                stt(ks[:, t0:], k.bank[0][:, 0:n], -1.0 / 64, ks[:, t0:], ALU.mult, ALU.add).then_inc(s.yc, 1)
                v.sem_inc(s.bonus_in, 1)
                v.wait_ge(s.var_d, it + 1)
                ts(tmp[:, t0:], k.bank[1][:, 0:n], 1.0 / 64, GN_EPS, ALU.mult, ALU.add).then_inc(s.var_in, 1)
                v.wait_ge(s.root, it + 1)
                do.do(nc.vector.reciprocal(tmp[:, t0:], tmp[:, t0:]))
                tt(ks[:, t0:], ks[:, t0:], tmp[:, t0:], ALU.mult).then_inc(s.yn, 1)
                v.wait_ge(s.bonus_d, it + 1)
                v.wait_ge(s.yn, it + 1)
                do.do(stt(tmp[:, t0:], k.bank[2][:, 0:n], 0.5, vv[:, t0:], ALU.mult, ALU.mult))
                v.wait_ge(s.lnd, it + 1)
                do.do(tt(ks[:, t0:], ks[:, t0:], tmp[:, t0:], ALU.add))
                out = y[:, bass.ds(it, 1), t0:]
                do.do(tt(out, one(ks[:, t0:]), out, ALU.mult))
                v.sem_inc(s.turn_free, 1)
                do.end()


def rwkv_branch(k, t0):
    nc, l = k.nc, k.layer
    with nc.sbuf_tensor(f"low{l}", [P, 2, TT], F32) as low:
        rwkv_low(k, low)
        rwkv_heads(k, low, k.br, t0)



def route(k, comb, t0):
    nc, l = k.nc, k.layer
    tiles = list(range(t0 // P, NT))
    nt = len(tiles)
    with ExitStack() as st:
        s = st.enter_context(phase(nc, "loaded logits vec act turned stored"))
        wr = st.enter_context(nc.sbuf_tensor(f"wr{l}", [P, KT, 20], F32))
        br = st.enter_context(nc.sbuf_tensor(f"rb{l}", [P, 20], F32))
        lg = st.enter_context(nc.sbuf_tensor(f"lg{l}", [P, nt, 20], F32))
        a = st.enter_context(nc.sbuf_tensor(f"ra{l}", [P, 8, nt, 4], F32))
        one = st.enter_context(nc.sbuf_tensor(f"r1{l}", [P, 8, nt, 1], F32))
        sel = st.enter_context(nc.sbuf_tensor(f"rs{l}", [P, nt, 4, 4], F32))
        row = st.enter_context(nc.sbuf_tensor(f"rr{l}", [16, TT], F32))
        block = st.enter_context(nc.Block())
        OHG, TMP, LS, OH1, OH2, LS2 = range(6)
        MX, EX, SM, PT, MX2, W1, W2, PM = range(8)

        @block.sync
        def _(sp):
            sp.dma_start(wr[:], k.d.router_w[l].rearrange("(kt p) c -> p kt c", p=P)).then_inc(s.loaded, 16)
            sp.dma_start(br[:], k.d.router_b[l:l + 1].to_broadcast([P, 20])).then_inc(s.loaded, 16)
            sp.wait_ge(s.turned, 2)
            sp.dma_start(k.d.comb[:, t0:], row[:, t0:]).then_inc(s.stored, 16)
            sp.wait_ge(s.stored, 16)

        @block.tensor
        def _(pe):
            pe.wait_ge(s.loaded, 32)
            for n, t in enumerate(tiles):
                for kt in range(KT):
                    mm = nc.tensor.matmul(k.bank[0][:, 20 * n:20 * n + 20], k.h[:, kt, P * t:P * t + P], wr[:, kt],
                                          start=kt == 0, stop=kt == KT - 1)
            mm.then_inc(s.logits, 1)
            pe.wait_ge(s.turned, 1)
            for n, t in enumerate(tiles):
                mm = nc.tensor.transpose(k.bank[1][0:16, P * n:P * n + P], sel[:, n].rearrange("p g e -> p (g e)"), const(k, "ident"))
            mm.then_inc(s.logits, 1)

        @block.scalar
        def _(act):
            act.wait_ge(s.vec, 3)
            nc.scalar.activation(a[:, TMP], a[:, TMP], ACT.Exp).then_inc(s.act, 1)
            act.wait_ge(s.vec, 19)
            nc.scalar.activation(one[:, EX], one[:, EX], ACT.Exp).then_inc(s.act, 1)

        @block.vector
        def _(v):
            do = Steps(v, s.vec)
            tt, B4 = nc.vector.tensor_tensor, [P, nt, 4]
            v.wait_ge(s.logits, 1)
            v.wait_ge(s.loaded, 32)
            do.do(tt(lg[:], k.bank[0][:, 0:20 * nt].rearrange("p (t c) -> p t c", c=20),
                     br[:].rearrange("p (o c) -> p o c", o=1).to_broadcast([P, nt, 20]), ALU.add))
            grp = lg[:, :, 0:4]
            do.do(nc.vector.tensor_reduce(one[:, MX], grp, AX.X, ALU.max))
            do.do(tt(a[:, TMP], grp, one[:, MX].to_broadcast(B4), ALU.subtract))
            v.wait_ge(s.act, 1)
            do.do(nc.vector.tensor_reduce(one[:, SM], a[:, TMP], AX.X, ALU.add))
            do.do(nc.vector.reciprocal(one[:, PT], one[:, SM]))
            pref = const(k, "pref").rearrange("p (o c) -> p o c", o=1).to_broadcast(B4)

            def first_max(dst, src, mx):
                do.do(tt(dst, src, mx.to_broadcast(B4), ALU.is_equal))
                do.do(tt(dst, dst, pref, ALU.mult))
                do.do(nc.vector.tensor_reduce(one[:, PM], dst, AX.X, ALU.max))
                do.do(tt(dst, dst, one[:, PM].to_broadcast(B4), ALU.is_equal))

            first_max(a[:, OHG], grp, one[:, MX])
            ex = lg[:, :, 4:20].rearrange("p t (g e) -> p t g e", g=4)
            do.do(tt(sel[:], ex, a[:, OHG].unsqueeze(3).to_broadcast([P, nt, 4, 4]), ALU.mult))
            do.do(nc.vector.tensor_reduce(a[:, LS], sel[:].rearrange("p t g e -> p t e g"), AX.X, ALU.add))
            do.do(nc.vector.tensor_reduce(one[:, MX], a[:, LS], AX.X, ALU.max))
            first_max(a[:, OH1], a[:, LS], one[:, MX])
            do.do(nc.vector.scalar_tensor_tensor(a[:, LS2].rearrange("p t c -> p (t c)"), a[:, OH1].rearrange("p t c -> p (t c)"), NEG,
                                                 a[:, LS].rearrange("p t c -> p (t c)"), ALU.mult, ALU.add))
            do.do(nc.vector.tensor_reduce(one[:, MX2], a[:, LS2], AX.X, ALU.max))
            do.do(tt(one[:, EX], one[:, MX2], one[:, MX], ALU.subtract))
            first_max(a[:, OH2], a[:, LS2], one[:, MX2])
            v.wait_ge(s.act, 2)
            do.do(nc.vector.tensor_scalar(one[:, SM], one[:, EX], 1.0, None, ALU.add))
            do.do(nc.vector.reciprocal(one[:, SM], one[:, SM]))
            do.do(tt(one[:, W1], one[:, SM], one[:, PT], ALU.mult))
            do.do(tt(one[:, W2], one[:, W1], one[:, EX], ALU.mult))
            do.do(tt(a[:, OH1], a[:, OH1], one[:, W1].to_broadcast(B4), ALU.mult))
            do.do(tt(a[:, OH2], a[:, OH2], one[:, W2].to_broadcast(B4), ALU.mult))
            do.do(tt(a[:, OH1], a[:, OH1], a[:, OH2], ALU.add))
            w = a[:, OH1].unsqueeze(2).to_broadcast([P, nt, 4, 4])
            tt(sel[:], a[:, OHG].unsqueeze(3).to_broadcast([P, nt, 4, 4]), w, ALU.mult).then_inc(s.turned, 1)
            v.wait_ge(s.logits, 2)
            nc.vector.tensor_copy(row[:, t0:], k.bank[1][0:16, 0:P * nt]).then_inc(s.turned, 1)


def experts(k, t0):
    nc, l = k.nc, k.layer
    n = TT - t0
    R = 3
    with ExitStack() as st:
        s = st.enter_context(phase(nc, "gu0 gu1 gu2 down w0 gu_free down_free w_free gate_done up_done gu_bank_free silu_done hidden_done hidden_free hmul out_done out_bank_free"))
        gu = st.enter_context(nc.sbuf_tensor(f"gu{l}", [P, R, 2, KT, P], F32))
        down = st.enter_context(nc.sbuf_tensor(f"down{l}", [P, HT, D], F32))
        hid = st.enter_context(nc.sbuf_tensor(f"hid{l}", [P, HT, TT], F32))
        sg = st.enter_context(nc.sbuf_tensor(f"msg{l}", [P, 2, TT], F32))
        wb = st.enter_context(nc.sbuf_tensor(f"wb{l}", [P, TT], F32))
        block = st.enter_context(nc.Block())
        gus = (s.gu0, s.gu1, s.gu2)
        gate = k.d.moe_w_gate[l].rearrange("e (kt p) c -> p e kt c", p=P)
        up = k.d.moe_w_up[l].rearrange("e (kt p) c -> p e kt c", p=P)
        dn = k.d.moe_w_down[l].rearrange("e (f p) c -> p e f c", p=P)

        @block.sync
        def _(sp):
            with sp.Fori(0, EXPERTS) as e:
                for f in range(HT):
                    sp.wait_ge(s.gu_free, e * HT + (f + 1))
                    sp.dma_start(gu[:, f % R, 0], gate[:, bass.ds(e, 1), :, P * f:P * f + P].rearrange("p o kt c -> p (o kt) c")).then_inc(gus[f % R], 16)
                    sp.dma_start(gu[:, f % R, 1], up[:, bass.ds(e, 1), :, P * f:P * f + P].rearrange("p o kt c -> p (o kt) c")).then_inc(gus[f % R], 16)
                    if f == 0:
                        sp.wait_ge(s.w_free, e + 1)
                        sp.dma_start(wb[:, t0:], k.d.comb[bass.ds(e, 1), t0:].to_broadcast([P, n])).then_inc(s.w0, 16)
                    if f == 2:
                        sp.wait_ge(s.down_free, e + 1)
                        sp.dma_start(down[:], dn[:, bass.ds(e, 1)].rearrange("p o f c -> p (o f) c")).then_inc(s.down, 16)

        @block.tensor
        def _(pe):
            pe.sem_inc(s.gu_free, R)
            pe.sem_inc(s.down_free, 1)
            with pe.Fori(0, EXPERTS) as e:
                for f in range(HT):
                    pe.wait_ge(gus[f % R], e * 64 + 32 * (f // R + 1))
                    pe.wait_ge(s.gu_bank_free, e * HT + (f + 1))
                    for w, done in ((0, s.gate_done), (1, s.up_done)):
                        for kt in range(KT):
                            mm = nc.tensor.matmul(k.bank[2 * w + f % 2][:, 0:n], gu[:, f % R, w, kt], k.h[:, kt, t0:],
                                                  start=kt == 0, stop=kt == KT - 1)
                        mm.then_inc(done, 1)
                    pe.wait_ge(s.up_done, e * HT + (f + 1))
                    pe.sem_inc(s.gu_free, 1)
                pe.wait_ge(s.down, e * 16 + 16)
                pe.wait_ge(s.hidden_done, e * HT + HT)
                for m in range(KT):
                    pe.wait_ge(s.out_bank_free, e * KT + (m + 1))
                    for f in range(HT):
                        mm = nc.tensor.matmul(k.bank[4 + m % 4][:, 0:n], down[:, f, P * m:P * m + P], hid[:, f, t0:],
                                              start=f == 0, stop=f == HT - 1)
                    mm.then_inc(s.out_done, 1)
                pe.wait_ge(s.out_done, e * KT + KT)
                pe.sem_inc(s.down_free, 1)

        @block.scalar
        def _(act):
            with act.Fori(0, EXPERTS) as e:
                for f in range(HT):
                    act.wait_ge(s.gate_done, e * HT + (f + 1))
                    act.wait_ge(s.gu_bank_free, e * HT + (f + 1))
                    nc.scalar.activation(sg[:, f % 2, t0:], k.bank[f % 2][:, 0:n], ACT.Silu).then_inc(s.silu_done, 1)

        @block.vector
        def _(v):
            v.sem_inc(s.gu_bank_free, 2)
            v.sem_inc(s.out_bank_free, 4)
            v.sem_inc(s.w_free, 1)
            with v.Fori(0, EXPERTS) as e:
                v.wait_ge(s.w0, e * 16 + 16)
                for f in range(HT):
                    v.wait_ge(s.silu_done, e * HT + (f + 1))
                    v.wait_ge(s.up_done, e * HT + (f + 1))
                    nc.vector.tensor_tensor(sg[:, f % 2, t0:], sg[:, f % 2, t0:], k.bank[2 + f % 2][:, 0:n], ALU.mult).then_inc(s.hmul, 1)
                    v.wait_ge(s.hmul, e * HT + (f + 1))
                    nc.vector.tensor_tensor(hid[:, f, t0:], sg[:, f % 2, t0:], wb[:, t0:], ALU.mult).then_inc(s.hidden_done, 1)
                    v.wait_ge(s.hidden_done, e * HT + (f + 1))
                    v.sem_inc(s.gu_bank_free, 1)
                v.sem_inc(s.w_free, 1)
                for m in range(KT):
                    v.wait_ge(s.out_done, e * KT + (m + 1))
                    nc.vector.tensor_tensor(k.acc[:, m, t0:], k.acc[:, m, t0:], k.bank[4 + m % 4][:, 0:n], ALU.add).then_inc(s.out_bank_free, 1)


def residual_ffn(k, t0):
    nc, l = k.nc, k.layer
    with ExitStack() as st:
        s = st.enter_context(phase(nc, "added"))
        block = st.enter_context(nc.Block())

        @block.vector
        def _(v):
            for m in range(KT):
                for c in range(t0 // LC, 2):
                    x = k.x[:, m, LC * c:LC * c + LC]
                    nc.vector.scalar_tensor_tensor(x, k.acc[:, m, LC * c:LC * c + LC], k.mod[:, 40 + m, c:c + 1], x, ALU.mult, ALU.add).then_inc(s.added, 1)
            v.wait_ge(s.added, KT * (2 - t0 // LC))


def clear(k, buf):
    nc = k.nc
    with ExitStack() as st:
        s = st.enter_context(phase(nc, "cleared"))
        block = st.enter_context(nc.Block())

        @block.vector
        def _(v):
            nc.vector.memset(buf, 0.0).then_inc(s.cleared, 1)
            v.wait_ge(s.cleared, 1)



class State:
    pass


def program(nc, d):
    with ExitStack() as st:
        def sb(name, shape):
            return st.enter_context(nc.sbuf_tensor("sb_" + name, shape, F32))

        k = State()
        k.nc, k.d = nc, d
        k.bank = [st.enter_context(nc.psum_tensor(f"bank{i}", [P, 512], F32))[:] for i in range(8)]
        k.x, k.h, k.acc, k.br = (sb(n, [P, KT, TT]) for n in ("x", "h", "acc", "branch"))
        k.const, k.cols, k.rcols = sb("consts", [P, N_CONST]), sb("cols", [P, DEPTH, N_COL]), sb("rcols", [P, DEPTH, 8, N_RCOL])
        k.cvec, k.final = sb("cvec", [P, KT, 2]), sb("final", [P, KT])
        k.mod, k.nscale = sb("mod", [P, 48, 2]), sb("nscale", [P, 2, KT, 2])

        with phase(nc, "loaded") as s, nc.Block() as block:
            @block.sync
            def _(sp):
                for dst, src in ((k.x[:], d.xT.rearrange("(kt p) t -> p kt t", p=P)), (k.const[:], d.consts), (k.cols[:], d.cols),
                                 (k.rcols[:], d.rcols), (k.cvec[:], d.cvec), (k.final[:], d.final)):
                    sp.dma_start(dst, src).then_inc(s.loaded, 16)
                sp.wait_ge(s.loaded, 6 * 16)

        for l in range(DEPTH):
            k.layer = l
            t0 = LC if l == DEPTH - 1 else 0
            with nc.sbuf_tensor(f"ring{l}", [P, 2, KT, 512], F32) as ring:
                k.ring = ring
                modulation(k)
                norm(k, k.x, k.h, 0, 0)
                ssd_branch(k, t0)
                natten_branch(k, t0)
            rwkv_branch(k, t0)
            with nc.sbuf_tensor(f"ringb{l}", [P, 2, KT, 512], F32) as ring:
                k.ring = ring
                merge(k, 1, k.br, t0)
                residual_out(k, t0)
            norm(k, k.x, k.h, t0, 1)
            route(k, None, t0)
            clear(k, k.acc[:])
            experts(k, t0)
            residual_ffn(k, t0)
        k.normcol = lambda m: k.final[:, m:m + 1]
        norm(k, k.x, k.h, LC, "cols")
        with phase(nc, "stored") as s, nc.Block() as block:
            @block.sync
            def _(sp):
                sp.dma_start(d.out.rearrange("(kt p) t -> p kt t", p=P), k.h[:, :, LC:]).then_inc(s.stored, 16)
                sp.wait_ge(s.stored, 16)



def layout(i):
    L = DEPTH

    def tiles(a):
        a = np.asarray(a)
        a = a.reshape(a.shape[:-1] + (a.shape[-1] // P, P))
        return np.moveaxis(a, -1, 0)

    a = {n: np.asarray(i[n]) for n in ("w_mod", "w_in", "w_branch", "w_out", "moe_w_gate", "moe_w_up", "moe_w_down")}
    a["xT"] = np.concatenate([i["ctx"][0].T, i["x"][0].T], 1)
    a["cvec"] = np.stack([tiles(i["c_ctx"]), tiles(i["c"][0])], -1)
    a["final"] = tiles(i["final_norm_w"])
    mu = np.asarray(i["rwkv_mu"])
    parts = [tiles(i["norm1_w"]), tiles(i["norm2_w"]), tiles(i["b_mod"]), tiles(i["ssd_conv_b"]),
             tiles(i["ssd_conv_w"]).reshape(P, L, 80), tiles(np.repeat(np.asarray(i["ssd_d"]), 64, -1)),
             tiles(i["ssd_norm_w"]), tiles(mu[:, 3072:3200]), tiles(mu[:, 3200:3328])]
    a["cols"] = np.concatenate(parts, 2)
    r = [tiles(mu[:, 1024 * n:1024 * n + 1024]) for n in range(3)]
    r += [tiles(i["rwkv_w0"])[:, :, n] for n in range(2)] + [tiles(i["rwkv_a0"])[:, :, n] for n in range(2)]
    r += [tiles(i["rwkv_k_k"]), tiles(i["rwkv_k_a"]), tiles(np.asarray(i["rwkv_r_k"]).reshape(L, D)), tiles(i["rwkv_ln_w"]), tiles(i["rwkv_ln_b"])]
    a["rcols"] = np.stack(r, -1)
    a["wa2"] = np.concatenate([np.asarray(i["rwkv_w2"]), np.asarray(i["rwkv_a2"])], 2).transpose(0, 2, 1, 3)
    a["g2"] = np.asarray(i["rwkv_g2"])
    a["dt_par"] = np.concatenate([np.asarray(i["ssd_dt_bias"]), np.asarray(i["ssd_a_log"])], 1).transpose(0, 2, 1)
    a["router_w"] = np.concatenate([np.asarray(i["moe_w_group"]), np.asarray(i["moe_w_expert"])], 2)
    a["router_b"] = np.concatenate([np.asarray(i["moe_b_group"]), np.asarray(i["moe_b_expert"])], 1)
    col = np.arange(64)
    dc = np.clip(col[None] - col[:, None], -15, 15) + 15
    a["na_bias"] = np.asarray(i["na_rpb"])[:, :, 4:11][:, :, :, dc]
    a["consts"] = constants()
    return {n: np.ascontiguousarray(v) for n, v in a.items()}


def kernel(**inputs):
    import concourse.bacc as bacc
    from concourse.bass_utils import run_bass_kernel_spmd

    nc = bacc.Bacc("TRN2", target_bir_lowering=False, num_devices=1)
    arrays = layout(inputs)
    d = {n: nc.dram_tensor(n, a.shape, F32, kind="ExternalInput").ap() for n, a in arrays.items()}
    d["ssd_rows"] = nc.dram_tensor("ssd_rows", [16, 2, 10 * P], F32).ap()
    d["comb"] = nc.dram_tensor("comb", [16, TT], F32).ap()
    d["out"] = nc.dram_tensor("out", [D, LC], F32, kind="ExternalOutput").ap()
    program(nc, namedtuple("Arrays", " ".join(d))(**d))
    r = run_bass_kernel_spmd(nc, [arrays], core_ids=[0])
    return np.ascontiguousarray(r.results[0]["out"].T)[None]
```

```python
from collections import namedtuple
from contextlib import ExitStack, contextmanager

import numpy as np

import concourse.bass as bass
from concourse import mybir

F32 = mybir.dt.float32
ALU = mybir.AluOpType
ACT = mybir.ActivationFunctionType
AX = mybir.AxisListType

P = 128
D = 1024
KT = D // P
LC = 256
TT = 512
NT = TT // P
DEPTH = 2
EPS = 1e-6
GN_EPS = 64e-5
HEADS = 16
GROUPS = 4
EXPERTS = 16
HID = 768
HT = HID // P
C_Z, C_XBC, C_DT, C_R, C_WA, C_G, C_Q, C_V, C_GATE = 0, 1024, 3072, 3104, 6176, 6304, 6432, 8480, 9504
ORDER = ((0, 1, 2, 3), (1, 0, 3, 2))
DECAY_SCALE = float(np.exp(-0.5))
NEG = -1e30

CONSTS = {}


def _layout(parts):
    at = 0
    for name, n in parts:
        CONSTS[name] = (at, n)
        at += n
    return at


N_CONST = _layout([("ident", P), ("ones", P), ("headones", P), ("rope_perm", P), ("cos", 256),
                   ("sin", 256), ("gmask", 2 * 256), ("amask", 2 * P), ("bd16", P), ("off32", P),
                   ("off64", P), ("off128", P), ("ssdmask", 2 * P), ("namask", 256), ("pref", 4),
                   ("iota", P)])

COLS = {}


def _columns():
    at = 0
    for name, n in [("norm1", 8), ("norm2", 8), ("b_mod", 48), ("conv_b", 16), ("conv_w", 80),
                    ("ssd_d", 8), ("ssd_norm", 8), ("mu_wa", 1), ("mu_g", 1)]:
        COLS[name] = (at, n)
        at += n
    return at


N_COL = _columns()
N_RCOL = 12
MU, W0, A0, KK, KA, RK, LNW, LNB = 0, 3, 5, 7, 8, 9, 10, 11


def constants():
    c = np.zeros((P, N_CONST), np.float32)

    def put(name, a):
        at, n = CONSTS[name]
        c[:, at:at + n] = a.reshape(P, n)

    i = np.arange(P)
    put("ident", np.eye(P))
    put("ones", np.ones((P, P)))
    put("headones", (i[:, None] // 64 == i[None] // 64).astype(np.float32))
    perm = np.zeros((P, P))
    for m in range(P):
        if (m // 32) % 2 == 0:
            perm[m + 32, m] = -1.0
        else:
            perm[m - 32, m] = 1.0
    put("rope_perm", perm)
    inv = (10000.0 ** (-np.arange(32, dtype=np.float32) / np.float32(32))).astype(np.float32)
    tok = np.arange(256)
    pos = np.stack([tok // 64, tok % 64]).astype(np.float32)
    ang = (pos[(i // 64)] * inv[i % 32][:, None]).astype(np.float32)
    put("cos", np.cos(ang))
    put("sin", np.sin(ang))
    up = (i[:, None] < i[None]).astype(np.float32)
    eye = np.eye(P, dtype=np.float32)
    put("gmask", np.stack([np.concatenate([s, s + eye], 1) for s in (up, up.T)], 1))
    put("amask", np.stack([up.T, up], 1))
    bd = {n: (i[:, None] // n == i[None] // n).astype(np.float32) for n in (16, 32, 64, 128)}
    put("bd16", bd[16])
    put("off32", bd[32] - bd[16])
    put("off64", bd[64] - bd[32])
    put("off128", bd[128] - bd[64])
    put("ssdmask", np.stack([np.where(s + eye > 0, 0.0, NEG) for s in (up, up.T)], 1))
    col = np.arange(64)
    first = np.clip(col - 8, 0, 48)
    ok = (col[None] >= first[:, None]) & (col[None] < first[:, None] + 16)
    put("namask", np.tile(np.where(ok, 0.0, NEG), (2, 4)))
    put("pref", np.tile(np.arange(4, 0, -1, dtype=np.float32), (P, 1)))
    put("iota", np.tile(i.astype(np.float32), (P, 1)))
    return c


class Steps:

    def __init__(self, eng, sem, turn=0, per=0, before=0):
        self.eng, self.sem, self.base, self.per, self.n = eng, sem, turn * per if per else 0, per, before
        self.before = before

    def put(self, ins):
        ins.then_inc(self.sem, 1)
        self.n += 1

    def settle(self):
        self.eng.wait_ge(self.sem, self.base + self.n)

    def do(self, ins):
        self.put(ins)
        self.settle()

    def end(self):
        assert self.n - self.before == self.per, f"a turn takes {self.n - self.before} steps, not {self.per}"


_phase = [0]


@contextmanager
def phase(nc, names):
    _phase[0] += 1
    with ExitStack() as st:
        sems = namedtuple("Semaphores", names)(*(st.enter_context(nc.semaphore(f"{n}_{_phase[0]}")) for n in names.split()))
        yield sems
        for s in sems:
            nc.sync.sem_clear(s)
        nc.all_engine_barrier()


def const(k, name):
    at, n = CONSTS[name]
    return k.const[:, at:at + n]


def col(k, name, j=0, n=1):
    at, _ = COLS[name]
    return k.cols[:, k.layer, at + j:at + j + n]


def three(ap, a):
    return ap.rearrange("p (a b) -> p a b", a=a)



STREAM = "loaded0 loaded1 slab_free0 slab_free1 tile_done bank_free"


def slab_parts(k, plan, h):
    kind, w, arg = plan
    wv = w.rearrange("(kt p) c -> p kt c", p=P)
    if kind == "plain":
        return [(k.ring[:, h], wv[:, :, arg + 512 * h:arg + 512 * h + 512])]
    wb = k.d.w_branch[k.layer, arg].rearrange("(kt p) c -> p kt c", p=P)
    at = C_GATE + D * arg + 256 * h
    return [(merge_slab(k, h)[:, 0], wv[:, :, at:at + 256]), (merge_slab(k, h)[:, 1], wb[:, :, 256 * h:256 * h + 256])]


def merge_slab(k, h):
    return k.ring[:, h].rearrange("p kt c -> p (kt c)").rearrange("p (w kt c) -> p w kt c", w=2, kt=KT)


def take_first_slabs(k, sp, loaded, amount):
    plan = k.plans.pop(0)
    if not k.asked:
        for h in range(2):
            for dst, src in slab_parts(k, plan, h):
                sp.dma_start(dst, src).then_inc(k.first[h], 16)
    k.n_first += 16 * len(slab_parts(k, plan, 0))
    k.asked = False
    for h in range(2):
        sp.wait_ge(k.first[h], k.n_first)
        sp.sem_inc(loaded[h], amount)


def ask_next_slabs(k, sp, frees):
    if not k.plans:
        return
    for h in range(2):
        sp.wait_ge(*frees[h])
        for dst, src in slab_parts(k, k.plans[0], h):
            sp.dma_start(dst, src).then_inc(k.first[h], 16)
    k.asked = True


def load_slabs(k, sp, s, w, col0, turns):
    wv = w.rearrange("(kt p) c -> p kt c", p=P)
    loaded, free = (s.loaded0, s.loaded1), (s.slab_free0, s.slab_free1)
    take_first_slabs(k, sp, loaded, 16)
    if turns > 1:
        with sp.Fori(0, turns - 1) as it:
            for h in range(2):
                sp.wait_ge(free[h], it + 1)
                sp.dma_start(k.ring[:, h], wv[:, :, bass.ds(it * 1024 + (col0 + 1024 + 512 * h), 512)]).then_inc(loaded[h], 16)
    ask_next_slabs(k, sp, [(free[h], turns) for h in range(2)])


def multiply_slabs(pe, nc, s, ring, rhs, banks, turns):
    loaded, free = (s.loaded0, s.loaded1), (s.slab_free0, s.slab_free1)
    with pe.Fori(0, turns) as it:
        for h in range(2):
            pe.wait_ge(loaded[h], it * 16 + 16)
            for j in range(4):
                pe.wait_ge(s.bank_free, it * 8 + (4 * h + j + 1))
                for kt in range(KT):
                    mm = nc.tensor.matmul(banks[j % len(banks)], ring[:, h, kt, P * j:P * j + P], rhs[:, kt],
                                          start=kt == 0, stop=kt == KT - 1)
                mm.then_inc(s.tile_done, 1)
            pe.wait_ge(s.tile_done, it * 8 + (4 * h + 4))
            pe.sem_inc(free[h], 1)



def modulation(k):
    nc, l = k.nc, k.layer
    with ExitStack() as st:
        s = st.enter_context(phase(nc, "loaded0 loaded1 slab_free0 slab_free1 rows_done row_free turned silu_c vec"))
        sc = st.enter_context(nc.sbuf_tensor(f"silu_c{l}", [P, KT, 2], F32))
        rows = st.enter_context(nc.sbuf_tensor(f"mod_rows{l}", [2, 12, 512], F32))
        block = st.enter_context(nc.Block())
        pm = three(k.bank[0][:, 0:96], 48)
        TURNS = 6

        @block.sync
        def _(sp):
            load_slabs(k, sp, s, k.d.w_mod[l], 0, TURNS)

        @block.scalar
        def _(act):
            nc.scalar.activation(sc[:], k.cvec[:], ACT.Silu).then_inc(s.silu_c, 1)
            act.sem_inc(s.row_free, 2)
            with act.Fori(0, TURNS) as it:
                for h in range(2):
                    act.wait_ge(s.rows_done, it * 2 + (h + 1))
                    nc.scalar.activation(rows[:, bass.ds(it * 2 + h, 1)], k.bank[1 + h][0:2].rearrange("p (o c) -> p o c", o=1), ACT.Copy)\
                        .then_inc(s.row_free, 1)

        @block.tensor
        def _(pe):
            pe.wait_ge(s.silu_c, 1)
            with pe.Fori(0, TURNS) as it:
                for h in range(2):
                    pe.wait_ge((s.loaded0, s.loaded1)[h], it * 16 + 16)
                    pe.wait_ge(s.row_free, it * 2 + (h + 1))
                    for kt in range(KT):
                        mm = nc.tensor.matmul(k.bank[1 + h][0:2], sc[:, kt], k.ring[:, h, kt], start=kt == 0, stop=kt == KT - 1)
                    mm.then_inc(s.rows_done, 1)
                    pe.wait_ge(s.rows_done, it * 2 + (h + 1))
                    pe.sem_inc((s.slab_free0, s.slab_free1)[h], 1)
            pe.wait_ge(s.row_free, 2 + 2 * TURNS)
            for j in range(48):
                mm = nc.tensor.transpose(pm[:, j], rows[:, j // 4, P * (j % 4):P * (j % 4) + P], const(k, "ident")[0:2, 0:2])
            mm.then_inc(s.turned, 1)

        @block.vector
        def _(v):
            do = Steps(v, s.vec)
            v.wait_ge(s.turned, 1)
            b = col(k, "b_mod", 0, 48)
            for c in range(2):
                do.do(nc.vector.tensor_tensor(k.mod[:, :, c], pm[:, :, c], b, ALU.add))
            for n, (name, at) in enumerate((("norm1", 8), ("norm2", 32))):
                for c in range(2):
                    do.do(nc.vector.scalar_tensor_tensor(k.nscale[:, n, :, c], k.mod[:, at:at + 8, c], 1.0,
                                                         col(k, name, 0, 8), ALU.add, ALU.mult))



def norm(k, src, dst, t0, mode):
    nc, l = k.nc, k.layer
    n = TT - t0
    with ExitStack() as st:
        s = st.enter_context(phase(nc, "square square_used sum root inv scaled moved"))
        sq = st.enter_context(nc.sbuf_tensor(f"sq{_phase[0]}", [P, 2, TT], F32))
        ms = st.enter_context(nc.sbuf_tensor(f"ms{_phase[0]}", [P, TT], F32))
        rinv = st.enter_context(nc.sbuf_tensor(f"rinv{_phase[0]}", [P, TT], F32))
        xr = st.enter_context(nc.sbuf_tensor(f"xr{_phase[0]}", [P, 2, TT], F32))
        block = st.enter_context(nc.Block())

        @block.scalar
        def _(act):
            for m in range(KT):
                if m >= 2:
                    act.wait_ge(s.square_used, m - 1)
                nc.scalar.activation(sq[:, m % 2, t0:], src[:, m, t0:], ACT.Square).then_inc(s.square, 1)
            act.wait_ge(s.root, 1)
            nc.scalar.activation(ms[:, t0:], ms[:, t0:], ACT.Sqrt).then_inc(s.root, 1)
            if mode == "cols":
                return
            shift = 0 if mode == 0 else 24
            for m in range(KT):
                act.wait_ge(s.scaled, m + 1)
                for c in range(t0 // LC, 2):
                    nc.scalar.activation(dst[:, m, LC * c:LC * c + LC], xr[:, m % 2, LC * c:LC * c + LC], ACT.Identity,
                                         bias=k.mod[:, shift + m, c:c + 1],
                                         scale=k.nscale[:, mode, m, c:c + 1]).then_inc(s.moved, 1)

        @block.tensor
        def _(pe):
            for m in range(KT):
                pe.wait_ge(s.square, m + 1)
                nc.tensor.matmul(k.bank[0][:, 0:n], const(k, "ones"), sq[:, m % 2, t0:],
                                 start=m == 0, stop=m == KT - 1).then_inc(s.square_used, 1)

        @block.vector
        def _(v):
            v.wait_ge(s.square_used, KT)
            nc.vector.tensor_scalar(ms[:, t0:], k.bank[0][:, 0:n], 1.0 / D, EPS, ALU.mult, ALU.add).then_inc(s.root, 1)
            v.wait_ge(s.root, 2)
            nc.vector.reciprocal(rinv[:, t0:], ms[:, t0:]).then_inc(s.inv, 1)
            v.wait_ge(s.inv, 1)
            each = 2 - t0 // LC
            for m in range(KT):
                if mode == "cols":
                    nc.vector.scalar_tensor_tensor(dst[:, m, t0:], src[:, m, t0:], k.normcol(m), rinv[:, t0:],
                                                   ALU.mult, ALU.mult).then_inc(s.scaled, 1)
                    continue
                if m >= 2:
                    v.wait_ge(s.moved, each * (m - 1))
                nc.vector.tensor_tensor(xr[:, m % 2, t0:], src[:, m, t0:], rinv[:, t0:], ALU.mult).then_inc(s.scaled, 1)



def project(k, w, col0, tiles, dst, t0=0):
    nc = k.nc
    with ExitStack() as st:
        s = st.enter_context(phase(nc, STREAM))
        block = st.enter_context(nc.Block())
        banks = [b[:, t0:] for b in k.bank[0:4]]
        turns = tiles // 8

        @block.sync
        def _(sp):
            load_slabs(k, sp, s, w, col0, turns)

        @block.tensor
        def _(pe):
            multiply_slabs(pe, nc, s, k.ring, k.h[:, :, t0:], banks, turns)

        @block.scalar
        def _(act):
            act.sem_inc(s.bank_free, 4)
            with act.Fori(0, turns) as it:
                for j in range(8):
                    act.wait_ge(s.tile_done, it * 8 + (j + 1))
                    nc.scalar.activation(dst[:, bass.ds(it * 8 + j, 1), t0:], three(banks[j % 4], 1), ACT.Copy)\
                        .then_inc(s.bank_free, 1)


def merge(k, b, src, t0):
    nc, l = k.nc, k.layer
    wg = k.d.w_in[l].rearrange("(kt p) c -> p kt c", p=P)
    wb = k.d.w_branch[l, b].rearrange("(kt p) c -> p kt c", p=P)
    with ExitStack() as st:
        s = st.enter_context(phase(nc, "loaded0 loaded1 slab_free gate_done proj_done gate_free sig_done added"))
        sg = st.enter_context(nc.sbuf_tensor(f"sg{l}{b}", [P, 2, TT], F32))
        block = st.enter_context(nc.Block())
        n = TT - t0
        turns = KT // 4
        slab = lambda h: merge_slab(k, h)

        @block.sync
        def _(sp):
            take_first_slabs(k, sp, (s.loaded0, s.loaded1), 32)
            for it in range(1, turns):
                for h in range(2):
                    sp.wait_ge(s.slab_free, 2 * it + h - 1)
                    loaded, at = (s.loaded0, s.loaded1)[h], 512 * it + 256 * h
                    sp.dma_start(slab(h)[:, 0], wg[:, :, C_GATE + D * b + at:C_GATE + D * b + at + 256]).then_inc(loaded, 16)
                    sp.dma_start(slab(h)[:, 1], wb[:, :, at:at + 256]).then_inc(loaded, 16)
            ask_next_slabs(k, sp, [(s.slab_free, 2 * turns - 1), (s.slab_free, 2 * turns)])

        @block.tensor
        def _(pe):
            with pe.Fori(0, turns) as it:
                for h in range(2):
                    pe.wait_ge((s.loaded0, s.loaded1)[h], it * 32 + 32)
                    for j in range(2):
                        t = 2 * h + j
                        pe.wait_ge(s.gate_free, it * 4 + (t + 1))
                        for kt in range(KT):
                            mm = nc.tensor.matmul(k.bank[t % 2][:, 0:n], slab(h)[:, 0, kt, P * j:P * j + P], k.h[:, kt, t0:],
                                                  start=kt == 0, stop=kt == KT - 1)
                        mm.then_inc(s.gate_done, 1)
                        for kt in range(KT):
                            mm = nc.tensor.matmul(k.bank[2 + t % 2][:, 0:n], slab(h)[:, 1, kt, P * j:P * j + P], src[:, kt, t0:],
                                                  start=kt == 0, stop=kt == KT - 1)
                        mm.then_inc(s.proj_done, 1)
                    pe.wait_ge(s.proj_done, it * 4 + (2 * h + 2))
                    pe.sem_inc(s.slab_free, 1)

        @block.scalar
        def _(act):
            act.sem_inc(s.gate_free, 2)
            with act.Fori(0, turns) as it:
                for t in range(4):
                    act.wait_ge(s.gate_done, it * 4 + (t + 1))
                    act.wait_ge(s.gate_free, it * 4 + (t + 1))
                    nc.scalar.activation(sg[:, t % 2, t0:], k.bank[t % 2][:, 0:n], ACT.Sigmoid).then_inc(s.sig_done, 1)

        @block.vector
        def _(v):
            with v.Fori(0, turns) as it:
                for t in range(4):
                    v.wait_ge(s.sig_done, it * 4 + (t + 1))
                    v.wait_ge(s.proj_done, it * 4 + (t + 1))
                    dst = k.acc[:, bass.ds(it * 4 + t, 1), t0:]
                    a, pj = three(sg[:, t % 2, t0:], 1), three(k.bank[2 + t % 2][:, 0:n], 1)
                    if b == 0:
                        nc.vector.tensor_tensor(dst, a, pj, ALU.mult).then_inc(s.gate_free, 1)
                    else:
                        nc.vector.tensor_tensor(a, a, pj, ALU.mult).then_inc(s.added, 1)
                        v.wait_ge(s.added, it * 4 + (t + 1))
                        nc.vector.tensor_tensor(dst, dst, a, ALU.add).then_inc(s.gate_free, 1)


def residual_out(k, t0):
    nc, l = k.nc, k.layer
    with ExitStack() as st:
        s = st.enter_context(phase(nc, STREAM))
        block = st.enter_context(nc.Block())
        banks = [b[:, t0:] for b in k.bank[0:4]]

        @block.sync
        def _(sp):
            load_slabs(k, sp, s, k.d.w_out[l], 0, 1)

        @block.tensor
        def _(pe):
            multiply_slabs(pe, nc, s, k.ring, k.acc[:, :, t0:], banks, 1)

        @block.vector
        def _(v):
            add_gated(nc, v, s, k, banks, 16, t0)


def add_gated(nc, v, s, k, banks, at, t0):
    v.sem_inc(s.bank_free, 4)
    for m in range(KT):
        v.wait_ge(s.tile_done, m + 1)
        for c in range(t0 // LC, 2):
            ins = nc.vector.scalar_tensor_tensor(k.x[:, m, LC * c:LC * c + LC], banks[m % 4][:, LC * c - t0:LC * c - t0 + LC],
                                                 k.mod[:, at + m, c:c + 1], k.x[:, m, LC * c:LC * c + LC], ALU.mult, ALU.add)
        ins.then_inc(s.bank_free, 1)



def conv_project(k, xbc):
    nc, l = k.nc, k.layer
    with ExitStack() as st:
        s = st.enter_context(phase(nc, STREAM + " padded taps conv_done taps_free"))
        raw = st.enter_context(nc.sbuf_tensor(f"raw{l}", [P, 2, 2, LC + 4], F32))
        cv = st.enter_context(nc.sbuf_tensor(f"conv{l}", [P, 2, 2, LC], F32))
        block = st.enter_context(nc.Block())
        banks = k.bank[0:4]

        @block.sync
        def _(sp):
            load_slabs(k, sp, s, k.d.w_in[l], C_XBC, 2)

        @block.tensor
        def _(pe):
            multiply_slabs(pe, nc, s, k.ring, k.h, banks, 2)

        def finish(act, it, j):
            act.wait_ge(s.conv_done, it * 8 + (j + 1))
            nc.scalar.activation(xbc[:, bass.ds(it * 8 + j, 1), :], cv[:, j % 2].rearrange("p a b -> p (a b)").rearrange("p (o c) -> p o c", o=1),
                                 ACT.Silu).then_inc(s.taps_free, 1)

        @block.scalar
        def _(act):
            act.sem_inc(s.bank_free, 4)
            act.wait_ge(s.taps, 1)
            with act.Fori(0, 2) as it:
                for j in range(8):
                    act.wait_ge(s.tile_done, it * 8 + (j + 1))
                    act.wait_ge(s.taps_free, it * 8 + (j + 1))
                    nc.scalar.activation(raw[:, j % 2, :, 2:2 + LC], three(banks[j % 4][:], 2), ACT.Copy).then_inc(s.padded, 1)
                    act.wait_ge(s.padded, it * 8 + (j + 1))
                    act.sem_inc(s.bank_free, 1)
                    if j >= 1:
                        finish(act, it, j - 1)
                finish(act, it, 7)

        @block.vector
        def _(v):
            v.sem_inc(s.taps_free, 2)
            do = Steps(v, s.taps)
            do.do(nc.vector.memset(raw[:], 0.0))
            with v.Fori(0, 2) as it:
                do = Steps(v, s.taps, it, 40, 1)
                for j in range(8):
                    v.wait_ge(s.padded, it * 8 + (j + 1))
                    out = cv[:, j % 2]
                    cols = k.cols[:, l, COLS["conv_w"][0]:COLS["conv_w"][0] + 80].rearrange("p (i c) -> p i c", i=5)
                    for i in range(5):
                        w = cols[:, i, bass.ds(it * 8 + j, 1)]
                        src = raw[:, j % 2, :, i:i + LC]
                        if i == 0:
                            b = k.cols[:, l, bass.ds(it * 8 + (COLS["conv_b"][0] + j), 1)]
                            do.do(nc.vector.tensor_scalar(out, src, w, b, ALU.mult, ALU.add))
                        else:
                            do.do(nc.vector.scalar_tensor_tensor(out, src, w, out, ALU.mult, ALU.add))
                    v.sem_inc(s.conv_done, 1)
                do.end()


def prepare_ssd(k, xbc, xtok):
    nc, l = k.nc, k.layer
    with ExitStack() as st:
        s = st.enter_context(phase(nc, "swapped moved turned copied vec"))
        t1 = st.enter_context(nc.sbuf_tensor(f"rot{l}", [P, 2, LC], F32))
        block = st.enter_context(nc.Block())

        @block.tensor
        def _(pe):
            for j in range(8):
                if j >= 2:
                    pe.wait_ge(s.moved, j - 1)
                nc.tensor.matmul(k.bank[j % 2][:, 0:LC], const(k, "rope_perm"), xbc[:, 8 + j, LC:], start=True, stop=True)\
                    .then_inc(s.swapped, 1)
            for j in range(16):
                tt, f = j // 4, (j % 4) * 2
                if j >= 4:
                    pe.wait_ge(s.copied, j - 3)
                for q in range(2):
                    mm = nc.tensor.transpose(k.bank[4 + j % 4][:, P * q:P * q + P], xbc[:, f + q, P * tt:P * tt + P], const(k, "ident"))
                mm.then_inc(s.turned, 1)

        @block.vector
        def _(v):
            do = Steps(v, s.vec)
            for j in range(8):
                v.wait_ge(s.swapped, j + 1)
                u = xbc[:, 8 + j, LC:]
                nc.vector.tensor_tensor(t1[:, j % 2], k.bank[j % 2][:, 0:LC], const(k, "sin"), ALU.mult).then_inc(s.moved, 1)
                do.do(nc.vector.tensor_tensor(u, u, const(k, "cos"), ALU.mult))
                do.do(nc.vector.tensor_tensor(u, u, t1[:, j % 2], ALU.add))

        @block.scalar
        def _(act):
            for j in range(16):
                tt, f = j // 4, (j % 4) * 2
                act.wait_ge(s.turned, j + 1)
                nc.scalar.activation(xtok[:, tt, P * f:P * f + 2 * P], k.bank[4 + j % 4][:, 0:2 * P], ACT.Copy).then_inc(s.copied, 1)


def ssd_segments(d, t0):
    out = []
    for a in range(3):
        seg = sorted((ORDER[d][b], ORDER[d][a + 1:b]) for b in range(a + 1, 4) if ORDER[d][b] * P >= t0)
        out += [(ORDER[d][a], t, mid) for t, mid in seg]
    return out


def decays(k, rows, bias):
    nc, l = k.nc, k.layer
    with ExitStack() as st:
        s = st.enter_context(phase(nc, "loaded dt_logit act vec turned stored"))
        wdt = st.enter_context(nc.sbuf_tensor(f"wdt{l}", [P, KT, 32], F32))
        par = st.enter_context(nc.sbuf_tensor(f"dtpar{l}", [16, 4], F32))
        arr = st.enter_context(nc.sbuf_tensor(f"dtarr{l}", [16, 8, 2, TT], F32))
        block = st.enter_context(nc.Block())
        VEC_COLUMNS = 39
        LOGIT, E, DT, PRE, CUM, NCUM, REST, DA = range(8)

        @block.sync
        def _(sp):
            sp.dma_start(wdt[:], k.d.w_in[l].rearrange("(kt p) c -> p kt c", p=P)[:, :, C_DT:C_DT + 32]).then_inc(s.loaded, 16)
            sp.dma_start(par[:], k.d.dt_par[l]).then_inc(s.loaded, 16)

        @block.tensor
        def _(pe):
            pe.wait_ge(s.loaded, 32)
            for d in range(2):
                for kt in range(KT):
                    mm = nc.tensor.matmul(k.bank[d][0:16, :], wdt[:, kt, 16 * d:16 * d + 16], k.h[:, kt],
                                          start=kt == 0, stop=kt == KT - 1)
            mm.then_inc(s.dt_logit, 1)
            pe.wait_ge(s.vec, VEC_COLUMNS)
            turned = k.bank[2][:, 0:384].rearrange("p (a c) -> p a c", c=16)
            for n, (which, d, t) in enumerate((w, d, t) for w in (NCUM, REST, DT) for d in range(2) for t in range(4)):
                mm = nc.tensor.matmul(turned[:, n], arr[:, which, d, P * t:P * t + P], const(k, "ident")[0:16, 0:16],
                                      start=True, stop=True)
            mm.then_inc(s.turned, 1)


        @block.scalar
        def _(act):
            do = Steps(act, s.act)
            act.wait_ge(s.vec, 2)
            do.do(nc.scalar.activation(arr[:, E], arr[:, LOGIT], ACT.Abs))
            do.do(nc.scalar.activation(arr[:, E], arr[:, E], ACT.Exp, scale=-1.0))
            do.do(nc.scalar.activation(arr[:, E], arr[:, E], ACT.Ln, bias=1.0))
            do.do(nc.scalar.activation(par[:, 2:4], par[:, 2:4], ACT.Exp))

        @block.vector
        def _(v):
            do = Steps(v, s.vec)
            v.wait_ge(s.dt_logit, 1)
            for d in range(2):
                do.do(nc.vector.tensor_scalar(arr[:, LOGIT, d], k.bank[d][0:16, :], par[:, d:d + 1], None, ALU.add))
            v.wait_ge(s.act, 4)
            for d in range(2):
                do.do(nc.vector.scalar_tensor_tensor(arr[:, DT, d], arr[:, LOGIT, d], 0.0, arr[:, E, d], ALU.max, ALU.add))
            do.do(nc.vector.tensor_scalar(par[:, 2:4], par[:, 2:4], -1.0, None, ALU.mult))
            for d in range(2):
                do.put(nc.vector.tensor_scalar(arr[:, DA, d], arr[:, DT, d], par[:, 2 + d:3 + d], None, ALU.mult))
            do.settle()
            for d in range(2):
                for t in range(4):
                    x = slice(P * t, P * t + P)
                    do.put(nc.vector.tensor_tensor_scan(arr[:, PRE, d, x], const(k, "ones")[0:16], arr[:, DA, d, x], 0.0, ALU.mult, ALU.add))
            do.settle()
            tot = [[arr[:, PRE, d, P * t + P - 1:P * t + P] for t in range(4)] for d in range(2)]
            for t in range(4):
                x = slice(P * t, P * t + P)
                do.put(nc.vector.scalar_tensor_tensor(arr[:, NCUM, 1, x], arr[:, PRE, 1, x], tot[1][t], arr[:, DA, 1, x], ALU.subtract, ALU.subtract))
            do.settle()
            for d in range(2):
                for t in range(4):
                    x = slice(P * t, P * t + P)
                    dst = rows[:, d, x]
                    if d == 0:
                        do.put(nc.vector.tensor_copy(dst, arr[:, PRE, 0, x]))
                        do.put(nc.vector.tensor_scalar(arr[:, NCUM, 0, x], arr[:, PRE, 0, x], -1.0, None, ALU.mult))
                    else:
                        do.put(nc.vector.tensor_scalar(dst, arr[:, NCUM, 1, x], -1.0, None, ALU.mult))
            do.settle()
            for d in range(2):
                for t in range(4):
                    x = slice(P * t, P * t + P)
                    do.put(nc.vector.tensor_scalar(arr[:, REST, d, x], arr[:, NCUM, d, x], tot[d][t], None, ALU.add))
            do.settle()
            assert do.n == VEC_COLUMNS, do.n
            for d in range(2):
                for n, (i, t, mid) in enumerate(ssd_segments(d, 0)):
                    dst = rows[:, d, TT + P * n:TT + P * n + P]
                    src = rows[:, d, P * t:P * t + P]
                    do.do(nc.vector.tensor_copy(dst, src) if not mid else
                          nc.vector.tensor_scalar(dst, src, tot[d][mid[0]], None, ALU.add))
                    for m in mid[1:]:
                        do.do(nc.vector.tensor_scalar(dst, dst, tot[d][m], None, ALU.add))
            v.wait_ge(s.turned, 1)
            nc.vector.tensor_copy(bias[:].rearrange("p w d t c -> p (w d t c)"), k.bank[2][:, 0:384]).then_inc(s.turned, 1)
            v.wait_ge(s.turned, 2)

    with ExitStack() as st:
        s = st.enter_context(phase(nc, "stored"))
        block = st.enter_context(nc.Block())

        @block.sync
        def _(sp):
            sp.dma_start(k.d.ssd_rows, rows[:]).then_inc(s.stored, 16)
            sp.wait_ge(s.stored, 16)


def ssd_mix(k, xbc, xtok, bias, y, t0):
    nc, l = k.nc, k.layer
    n = TT - t0
    tiles = [t for t in range(NT) if P * t >= t0]
    with ExitStack() as st:
        s = st.enter_context(phase(nc, "row0 row1 row_free c_ready c_done c_copied x_ready diag expd off weighed summed y_free vec vec2"))
        rowb = st.enter_context(nc.sbuf_tensor(f"rowb{l}", [P, 2, 2, 10 * P], F32))
        ebuf = st.enter_context(nc.sbuf_tensor(f"e{l}", [P, 2, 2, 10 * P], F32))
        cb = st.enter_context(nc.sbuf_tensor(f"cb{l}", [P, NT, TT], F32))
        bst = st.enter_context(nc.sbuf_tensor(f"bst{l}", [P, TT], F32))
        xst = st.enter_context(nc.sbuf_tensor(f"xst{l}", [P, 2, NT, P], F32))
        hb = st.enter_context(nc.sbuf_tensor(f"hbias{l}", [P, 2, 3, 2, NT], F32))
        block = st.enter_context(nc.Block())
        segs = [ssd_segments(d, 0) for d in range(2)]
        use = [[(q, g) for q, g in enumerate(segs[d]) if g[1] * P >= t0] for d in range(2)]

        def runs(d):
            out = []
            for q, (i, t, _) in use[d]:
                if out and out[-1][0] == i and out[-1][1] + out[-1][3] == t and out[-1][2] + out[-1][3] == q:
                    out[-1][3] += 1
                else:
                    out.append([i, t, q, 1])
            return out

        def sources(d):
            out = []
            for q, (i, t, _) in use[d]:
                if out and out[-1][0] == i and out[-1][1] + out[-1][2] == q:
                    out[-1][2] += 1
                else:
                    out.append([i, q, 1])
            return out

        @block.sync
        def _(sp):
            with sp.Fori(0, GROUPS) as g:
                for hh in range(4):
                    sp.wait_ge(s.row_free, g * 4 + (hh + 1))
                    src = k.d.ssd_rows[bass.ds(g * 4 + hh, 1)].rearrange("h d c -> h (d c)").to_broadcast([P, 20 * P])
                    sp.dma_start(rowb[:, hh % 2].rearrange("p d c -> p (d c)"), src).then_inc((s.row0, s.row1)[hh % 2], 16)

        v = nc.vector

        def diagonal(g, hh):
            h4, buf, e = g * 4 + (hh + 1), hh % 2, ebuf[:, hh % 2]
            v.wait_ge(s.summed, h4)
            v.tensor_copy(xst[:, buf, :, 64 * buf:64 * buf + 64], xtok[:, :, bass.ds(g * 256 + 64 * hh, 64)])
            v.tensor_copy(hb[:, buf].rearrange("p w d (t o) -> p (w d t) o", o=1),
                          bias[:].rearrange("p w d t c -> p (w d t) c")[:, :, bass.ds(g * 4 + hh, 1)]).then_inc(s.x_ready, 1)
            v.wait_ge(s.x_ready, h4)
            v.wait_ge((s.row0, s.row1)[buf], g * 32 + 16 * (hh // 2 + 1))
            for d in range(2):
                for i in tiles:
                    mask = const(k, "ssdmask")[:, P * d:P * d + P]
                    ins = v.scalar_tensor_tensor(e[:, d, P * i:P * i + P], rowb[:, buf, d, P * i:P * i + P],
                                                 hb[:, buf, 0, d, i:i + 1], mask, ALU.add, ALU.add)
            ins.then_inc(s.diag, 1)

        def weigh(g, hh):
            h4, buf, e = g * 4 + (hh + 1), hh % 2, ebuf[:, hh % 2]
            v.wait_ge(s.expd, h4)
            v.wait_ge(s.c_copied, g * 4 + 4)
            for d in range(2):
                for i in tiles:
                    x = slice(P * i, P * i + P)
                    ins = v.scalar_tensor_tensor(e[:, d, x], e[:, d, x], hb[:, buf, 2, d, i:i + 1], cb[:, i, x], ALU.mult, ALU.mult)
                for i, t, q, w in runs(d):
                    x = slice(TT + P * q, TT + P * (q + w))
                    ins = v.scalar_tensor_tensor(e[:, d, x], e[:, d, x], hb[:, buf, 2, d, i:i + 1],
                                                 cb[:, i, P * t:P * (t + w)], ALU.mult, ALU.mult)
            ins.then_inc(s.weighed, 1)
            v.wait_ge(s.weighed, h4)
            v.sem_inc(s.row_free, 1)

        def skip(g, pair):
            f = g * 2 + pair
            v.wait_ge(s.summed, g * 4 + (2 * pair + 4))
            v.scalar_tensor_tensor(y[:, bass.ds(f, 1), t0:], xbc[:, bass.ds(f, 1), t0:], k.cols[:, l, bass.ds(f + COLS["ssd_d"][0], 1)],
                                   three(k.bank[4 + pair][:, 0:n], 1), ALU.mult, ALU.add).then_inc(s.y_free, 1)

        @block.vector
        def _(v):
            v.sem_inc(s.row_free, 2)
            do = Steps(v, s.vec2)
            do.do(nc.vector.memset(xst[:], 0.0))
            with v.Fori(0, GROUPS) as g:
                nc.vector.tensor_copy(bst[:].rearrange("p (o c) -> p o c", o=1), xbc[:, bass.ds(g + 8, 1), :]).then_inc(s.c_ready, 1)
                for hh in range(4):
                    if hh == 0:
                        diagonal(g, 0)
                    if hh < 3:
                        diagonal(g, hh + 1)
                    weigh(g, hh)
                    if hh % 2 == 0 and hh:
                        skip(g, 0)
                skip(g, 1)

        @block.scalar
        def _(act):
            with act.Fori(0, GROUPS) as g:
                act.wait_ge(s.c_done, g + 1)
                for i in range(NT):
                    ins = nc.scalar.activation(cb[:, i, t0:], k.bank[i][:, 0:n], ACT.Copy).then_inc(s.c_copied, 1)
                for hh in range(4):
                    h4 = g * 4 + (hh + 1)
                    act.wait_ge(s.diag, h4)
                    e = ebuf[:, hh % 2]
                    lo = P * tiles[0]
                    nc.scalar.activation(e[:, :, lo:TT], e[:, :, lo:TT], ACT.Exp)
                    for d in range(2):
                        for i, q, w in sources(d):
                            x = slice(TT + P * q, TT + P * (q + w))
                            ins = nc.scalar.activation(e[:, d, x], rowb[:, hh % 2, d, x], ACT.Exp, bias=hb[:, hh % 2, 1, d, i:i + 1])
                    ins.then_inc(s.expd, 1)

        @block.tensor
        def _(pe):
            pe.sem_inc(s.summed, 2)
            pe.sem_inc(s.y_free, 2)
            with pe.Fori(0, GROUPS) as g:
                pe.wait_ge(s.c_ready, g + 1)
                for i in range(NT):
                    mm = nc.tensor.matmul(k.bank[i][:, 0:n].rearrange("p (o c) -> p o c", o=1), bst[:, P * i:P * i + P], xbc[:, bass.ds(g + 12, 1), t0:], start=True, stop=True)
                mm.then_inc(s.c_done, 1)
                for hh in range(4):
                    ps, e = k.bank[4 + hh // 2], ebuf[:, hh % 2]
                    pe.wait_ge(s.weighed, g * 4 + (hh + 1))
                    if hh % 2 == 0:
                        pe.wait_ge(s.y_free, g * 2 + (hh // 2 + 1))
                    first = hh % 2 == 0
                    jobs = [(i, i, 1, P * i, d) for d in range(2) for i in tiles]
                    jobs += [(i, t, w, TT + P * q, d) for d in range(2) for i, t, q, w in runs(d)]
                    for i, t, w, c, d in jobs:
                        mm = nc.tensor.matmul(ps[:, P * t - t0:P * (t + w) - t0], xst[:, hh % 2, i], e[:, d, c:c + P * w],
                                              start=first, stop=True, skip_group_check=True)
                        first = False
                    mm.then_inc(s.summed, 1)


def gate_by_z(k, y, t0):
    nc, l = k.nc, k.layer
    with ExitStack() as st:
        s = st.enter_context(phase(nc, STREAM + " silu_done multiplied"))
        zs = st.enter_context(nc.sbuf_tensor(f"zs{l}", [P, 2, TT], F32))
        block = st.enter_context(nc.Block())
        banks = [b[:, t0:] for b in k.bank[0:4]]

        @block.sync
        def _(sp):
            load_slabs(k, sp, s, k.d.w_in[l], C_Z, 1)

        @block.tensor
        def _(pe):
            multiply_slabs(pe, nc, s, k.ring, k.h[:, :, t0:], banks, 1)

        @block.scalar
        def _(act):
            act.sem_inc(s.bank_free, 4)
            for j in range(KT):
                act.wait_ge(s.tile_done, j + 1)
                if j >= 2:
                    act.wait_ge(s.multiplied, j - 1)
                nc.scalar.activation(zs[:, j % 2, t0:], banks[j % 4], ACT.Silu).then_inc(s.silu_done, 1)
                act.wait_ge(s.silu_done, j + 1)
                act.sem_inc(s.bank_free, 1)

        @block.vector
        def _(v):
            for j in range(KT):
                v.wait_ge(s.silu_done, j + 1)
                nc.vector.tensor_tensor(y[:, j, t0:], y[:, j, t0:], zs[:, j % 2, t0:], ALU.mult).then_inc(s.multiplied, 1)


def ssd_branch(k, t0):
    nc, l = k.nc, k.layer
    with ExitStack() as st:
        xbc = st.enter_context(nc.sbuf_tensor(f"xbc{l}", [P, 16, TT], F32))
        conv_project(k, xbc)
        xtok = k.acc[:].rearrange("p (t a) c -> p t (a c)", t=NT)
        prepare_ssd(k, xbc, xtok)
        bias = st.enter_context(nc.sbuf_tensor(f"dtcol{l}", [P, 3, 2, NT, 16], F32))
        with nc.sbuf_tensor(f"rows{l}", [16, 2, 10 * P], F32) as rows:
            decays(k, rows, bias)
        ssd_mix(k, xbc, xtok, bias, k.br, t0)
    gate_by_z(k, k.br, t0)
    k.normcol = lambda m: col(k, "ssd_norm", m)
    norm(k, k.br, k.br, t0, "cols")
    merge(k, 0, k.br, t0)



def project_tokens(k, dst):
    nc = k.nc
    with ExitStack() as st:
        s = st.enter_context(phase(nc, "loaded0 loaded1 done copied"))
        block = st.enter_context(nc.Block())

        @block.sync
        def _(sp):
            take_first_slabs(k, sp, (s.loaded0, s.loaded1), 16)
            ask_next_slabs(k, sp, [(s.done, 4), (s.done, 8)])

        @block.tensor
        def _(pe):
            for h in range(2):
                pe.wait_ge((s.loaded0, s.loaded1)[h], 16)
                for t in range(NT):
                    j = 4 * h + t
                    for kt in range(KT):
                        mm = nc.tensor.matmul(k.bank[j][:], k.h[:, kt, P * t:P * t + P], k.ring[:, h, kt], start=kt == 0, stop=kt == KT - 1)
                    mm.then_inc(s.done, 1)

        @block.scalar
        def _(act):
            for j in range(8):
                act.wait_ge(s.done, j + 1)
                nc.scalar.activation(dst[:, j % 4, 512 * (j // 4):512 * (j // 4) + 512], k.bank[j][:], ACT.Copy).then_inc(s.copied, 1)


def attend(k, qk, vtok, y, t0):
    nc, l = k.nc, k.layer
    qt = list(range(t0 // P, NT))
    jobs = [(h, q) for h in range(2) for q in qt]
    NJ = len(jobs)
    NL = 4
    with ExitStack() as st:
        s = st.enter_context(phase(nc, "bias0 bias1 bias_free masked staged pair_free scores context_in latent_in maxed exped normed turned turned_out weighed out_done out_read vec"))
        bias = st.enter_context(nc.sbuf_tensor(f"nabias{l}", [P, 2, 4, 4, 64], F32))
        qst = st.enter_context(nc.sbuf_tensor(f"qst{l}", [P, TT], F32))
        kst = st.enter_context(nc.sbuf_tensor(f"kst{l}", [P, TT], F32))
        vst = st.enter_context(nc.sbuf_tensor(f"vst{l}", [P, 2, NT, P], F32))
        sc = st.enter_context(nc.sbuf_tensor(f"sc{l}", [P, 2, TT], F32))
        pt = st.enter_context(nc.sbuf_tensor(f"pt{l}", [P, 2, NT, P], F32))
        mx = st.enter_context(nc.sbuf_tensor(f"mx{l}", [P, 2, 4], F32))
        block = st.enter_context(nc.Block())

        def keys(q):
            return TT if q >= 2 else LC

        @block.sync
        def _(sp):
            def load(f, b, sem):
                for h in range(2):
                    for q in range(2):
                        for rr in range(2):
                            r = 2 * q + rr
                            src = k.d.na_bias[l, bass.ds(2 * f + h, 1), 3 - r:7 - r].rearrange("o i c k -> c (o i) k")
                            sp.dma_start(bias[64 * rr:64 * rr + 64, b, 2 * h + q], src).then_inc(sem, 16)

            with sp.Fori(0, KT // 2) as it:
                for b in range(2):
                    sp.wait_ge(s.bias_free, it * 2 + (b + 1))
                    load(it * 2 + b, b, (s.bias0, s.bias1)[b])

        @block.gpsimd
        def _(pool):
            pool.sem_inc(s.bias_free, 2)
            with pool.Fori(0, KT // 2) as it:
                for b in range(2):
                    pool.wait_ge((s.bias0, s.bias1)[b], it * 128 + 128)
                    mask = const(k, "namask").rearrange("p (o c) -> p o c", o=1).to_broadcast([P, 4, 256])
                    dst = bias[:, b].rearrange("p j r c -> p j (r c)")
                    nc.gpsimd.tensor_tensor(dst, dst, mask, ALU.add).then_inc(s.masked, 1)

        def pair_turns(eng):
            return eng.Fori(0, KT // 2)

        v = nc.vector

        def finish_scores(f, b, n):
            h, q = jobs[n]
            j = f * NJ + n
            v.wait_ge(s.context_in, j + 1)
            if q >= 2:
                v.wait_ge(s.masked, f + 1)
                v.tensor_tensor(sc[:, n % 2, LC:], k.bank[n % 2][:, LC:], bias[:, b, 2 * h + q - 2].rearrange("p r c -> p (r c)"), ALU.add)\
                    .then_inc(s.latent_in, 1)
                v.wait_ge(s.latent_in, f * NL + (2 * h + q - 1))
            v.tensor_reduce(mx[:, n % 2, 0:1], sc[:, n % 2, 0:keys(q)], AX.X, ALU.max).then_inc(s.vec, 1)
            v.wait_ge(s.vec, f * (2 * NJ) + (2 * n + 2 - (n > 0)))
            v.tensor_scalar(mx[:, n % 2, 1:2], mx[:, n % 2, 0:1], -1.0, None, ALU.mult).then_inc(s.maxed, 1)

        def normalise(f, n):
            h, q = jobs[n]
            j = f * NJ + n
            v.wait_ge(s.exped, j + 1)
            v.reciprocal(mx[:, n % 2, 3:4], mx[:, n % 2, 2:3]).then_inc(s.vec, 1)
            v.wait_ge(s.vec, f * (2 * NJ) + (2 * n + 4 - (n == NJ - 1)))
            v.tensor_scalar(sc[:, n % 2, 0:keys(q)], sc[:, n % 2, 0:keys(q)], mx[:, n % 2, 3:4], None, ALU.mult).then_inc(s.normed, 1)
            v.wait_ge(s.turned, j + 1)
            v.tensor_copy(pt[:, n % 2].rearrange("p t c -> p (t c)")[:, 0:keys(q)], k.bank[2 + n % 2][:, 0:keys(q)]).then_inc(s.turned_out, 1)

        @block.vector
        def _(v):
            v.sem_inc(s.pair_free, 1)
            nc.vector.memset(vst[:], 0.0).then_inc(s.vec, 1)
            v.wait_ge(s.vec, 1)
            with pair_turns(v) as it:
                for b in range(2):
                    f = it * 2 + b
                    v.wait_ge(s.pair_free, f + 1)
                    one = lambda ap: ap.rearrange("p (o c) -> p o c", o=1)
                    nc.vector.tensor_scalar(one(qst[:]), qk[:, bass.ds(f, 1), :], 0.125, None, ALU.mult)
                    nc.vector.tensor_copy(one(kst[:]), qk[:, bass.ds(f + 8, 1), :])
                    for h in range(2):
                        ins = nc.vector.tensor_copy(vst[:, h, :, 64 * h:64 * h + 64], vtok[:, :, bass.ds(f * P + 64 * h, 64)])
                    ins.then_inc(s.staged, 1)
                    for n in range(NJ + 1):
                        if n < NJ:
                            finish_scores(f, b, n)
                        if n:
                            normalise(f, n - 1)
                    v.sem_inc(s.bias_free, 1)
                    v.wait_ge(s.out_done, f + 1)
                    nc.vector.tensor_copy(y[:, bass.ds(f, 1), t0:], one(k.bank[4][:, t0:])).then_inc(s.out_read, 1)

        @block.scalar
        def _(act):
            with pair_turns(act) as it:
                for b in range(2):
                    f = it * 2 + b
                    for n in range(NJ + 1):
                        if n < NJ:
                            act.wait_ge(s.scores, f * NJ + (n + 1))
                            nc.scalar.activation(sc[:, n % 2, 0:LC], k.bank[n % 2][:, 0:LC], ACT.Copy).then_inc(s.context_in, 1)
                        if n:
                            m, used = n - 1, keys(jobs[n - 1][1])
                            act.wait_ge(s.maxed, f * NJ + n)
                            nc.scalar.activation(sc[:, m % 2, 0:used], sc[:, m % 2, 0:used], ACT.Exp, bias=mx[:, m % 2, 1:2],
                                                 accum_out=mx[:, m % 2, 2:3]).then_inc(s.exped, 1)

        @block.tensor
        def _(pe):
            with pair_turns(pe) as it:
                for b in range(2):
                    f = it * 2 + b
                    pe.wait_ge(s.staged, f + 1)

                    def scores(n):
                        h, q = jobs[n]
                        hs = slice(64 * h, 64 * h + 64)
                        nc.tensor.matmul(k.bank[n % 2][:, 0:keys(q)], qst[hs, P * q:P * q + P], kst[hs, 0:keys(q)],
                                         start=True, stop=True).then_inc(s.scores, 1)

                    scores(0)
                    scores(1)
                    for n, (h, q) in enumerate(jobs):
                        j = f * NJ + n
                        pe.wait_ge(s.normed, j + 1)
                        for t in range(keys(q) // P):
                            mm = nc.tensor.transpose(k.bank[2 + n % 2][:, P * t:P * t + P], sc[:, n % 2, P * t:P * t + P], const(k, "ident"))
                        mm.then_inc(s.turned, 1)
                        if n + 2 < NJ:
                            scores(n + 2)
                        pe.wait_ge(s.turned_out, j + 1)
                        for t in range(keys(q) // P):
                            mm = nc.tensor.matmul(k.bank[4][:, P * q:P * q + P], vst[:, h, t], pt[:, n % 2, t],
                                                  start=(n == 0 and t == 0), stop=True, skip_group_check=True)
                        if n == NJ - 1:
                            mm.then_inc(s.out_done, 1)
                    pe.wait_ge(s.out_done, f + 1)
                    pe.wait_ge(s.out_read, f + 1)
                    pe.sem_inc(s.pair_free, 1)


def natten_branch(k, t0):
    nc, l = k.nc, k.layer
    with ExitStack() as st:
        qk = st.enter_context(nc.sbuf_tensor(f"qk{l}", [P, 16, TT], F32))
        vtok = st.enter_context(nc.sbuf_tensor(f"vtok{l}", [P, NT, D], F32))
        project(k, k.d.w_in[l], C_Q, 16, qk)
        project_tokens(k, vtok)
        attend(k, qk, vtok, k.br, t0)
    merge(k, 2, k.br, t0)



def rwkv_low(k, low):
    nc, l = k.nc, k.layer
    with ExitStack() as st:
        s = st.enter_context(phase(nc, "loaded proj rawin vec shifted"))
        w = st.enter_context(nc.sbuf_tensor(f"wlow{l}", [P, KT, 2 * P], F32))
        raw = st.enter_context(nc.sbuf_tensor(f"rawlow{l}", [P, 2, 2, LC + 2], F32))
        block = st.enter_context(nc.Block())

        @block.sync
        def _(sp):
            sp.dma_start(w[:], k.d.w_in[l].rearrange("(kt p) c -> p kt c", p=P)[:, :, C_WA:C_WA + 2 * P]).then_inc(s.loaded, 16)

        @block.tensor
        def _(pe):
            pe.wait_ge(s.loaded, 16)
            for j in range(2):
                for kt in range(KT):
                    mm = nc.tensor.matmul(k.bank[j], w[:, kt, P * j:P * j + P], k.h[:, kt], start=kt == 0, stop=kt == KT - 1)
                mm.then_inc(s.proj, 1)

        @block.scalar
        def _(act):
            act.wait_ge(s.vec, 1)
            for j in range(2):
                act.wait_ge(s.proj, j + 1)
                nc.scalar.activation(raw[:, j, :, 1:1 + LC], three(k.bank[j], 2), ACT.Copy).then_inc(s.rawin, 1)
            act.wait_ge(s.vec, 1 + 6)
            nc.scalar.activation(low[0:64, 0], low[0:64, 0], ACT.Tanh)
            nc.scalar.activation(low[:, 1], low[:, 1], ACT.Sigmoid).then_inc(s.shifted, 1)
            act.wait_ge(s.shifted, 1)

        @block.vector
        def _(v):
            do = Steps(v, s.vec)
            do.do(nc.vector.memset(raw[:], 0.0))
            for j in range(2):
                v.wait_ge(s.rawin, j + 1)
                token_shift(nc, do, raw[:, j], three(low[:, j], 2), col(k, ("mu_wa", "mu_g")[j]))


def token_shift(nc, do, raw, out, mu):
    mid = raw[:, :, 1:1 + LC]
    do.do(nc.vector.tensor_tensor(out, raw[:, :, 0:LC], raw[:, :, 2:2 + LC], ALU.add))
    do.do(nc.vector.scalar_tensor_tensor(out, out, 0.5, mid, ALU.mult, ALU.subtract))
    do.do(nc.vector.scalar_tensor_tensor(out, out, mu, mid, ALU.mult, ALU.add))


STAGES = [
    (("b1", "b0", "b2", "copy"), ("b0", "b1", "b3", "vcopy")),
    (("b2", "XT", "XT", "add"), ("b3", "b2", "b0", "copy"), ("b2", "b3", "b1", "vcopy")),
    (("b0", "XT", "XT", "add"), ("b1", "b0", "b2", "copy")),
    (("b2", "XT", "XT", "off32"),),
    (("XT", None, "X", "copy"), ("b1", "XT", "b0", "vcopy")),
    (("X", "b0", "XT", "off64"),),
    (("XT", None, "X", "copy"), ("b1", "XT", "b0", "vcopy")),
    (("X", "b0", "XT", "off128"),),
    (("XT", None, "X", "copy"), ("b1", "XT", "b0", "vcopy")),
    (("X", "b0", "XT", "add"),),
]


def stage_bank(k, q, j):
    return k.bank[2 * q + j] if j < 2 else k.bank[4 + q]


def stage_counts():
    prod, a, v, out = 0, 0, 0, {}
    for n, stage in enumerate(STAGES):
        for q in range(2):
            first = prod
            prod += len(stage)
            a += sum(how == "copy" for *_, how in stage)
            v += sum(how != "copy" for *_, how in stage)
            out[n, q] = (first, a, v)
    return out, prod, a, v


COUNTS, N_PROD, N_EV_A, N_EV_V = stage_counts()


def rwkv_heads(k, low, y, t0):
    nc, l = k.nc, k.layer
    n = TT - t0
    TURNS = KT
    with ExitStack() as st:
        s = st.enter_context(phase(nc, "w_in w_free low_in low_free turn_free proj rawin shifted lora lact kksq kkn kkroot cen exps feat turned tok "
                                       "gdone gevac prod ev_a ev_v r_done r_in u_done u_in y_done y_in s_done s_in ysum mean_d yc sq "
                                       "var_d var_in root yn lnd bonus_in bonus_d padded vec"))

        def sb(name, *shape):
            return st.enter_context(nc.sbuf_tensor(f"{name}{l}", [P, *shape], F32))

        w3, lora, g2 = sb("w3", 3, KT, P), sb("lora", 2, P), sb("g2_", P)
        raw, rkv = sb("raw3", 3, 2, LC + 2), sb("rkv", 3, TT)
        ld, aa, ci, ce = sb("ld", 2, TT), sb("aa", 2, TT), sb("ci", 2, TT), sb("ce", 2, TT)
        kk, ks, tmp = sb("kk", TT), sb("ks", TT), sb("tmp", TT)
        pc, half, em = sb("pc", N_RCOL), sb("half", 2, 4), sb("em", 2, 4)
        ar, bk = sb("ar", 2, 4, 2, P), sb("bk", 2, 2, TT)
        vpad, bkt = sb("vpad", 2, 4, P), sb("bkt", 2, 2, 4, P)
        s0, rs, up = sb("s0", 2, P), sb("rs_", 2, P), sb("up", 2, 2, P)
        t1 = rs
        buf = [{b: sb(f"{b}q{q}", 4, P) for b in ("b0", "b1", "b2", "b3", "X", "XT", "A")} for q in range(2)]
        gm = [sb(f"gm{q}", 4, 4, P) for q in range(2)]
        yy = aa
        r, kf, vv = (rkv[:, j] for j in range(3))
        block = st.enter_context(nc.Block())
        win = k.d.w_in[l].rearrange("(kt p) c -> p kt c", p=P)
        ident = const(k, "ident")
        flat = lambda b: b[:].rearrange("p a c -> p (a c)")
        one = lambda ap: ap.rearrange("p (o c) -> p o c", o=1)

        def chunk(z, pos):
            return slice(P * ORDER[z][pos], P * ORDER[z][pos] + P)

        def wanted(pos):
            return P * ORDER[0][pos] >= t0 or P * ORDER[1][pos] >= t0

        @block.sync
        def _(sp):
            for j in range(3):
                sp.dma_start(w3[:, j], win[:, :, C_R + D * j:C_R + D * j + P]).then_inc(s.w_in, 16)
            with sp.Fori(0, TURNS) as it:
                sp.wait_ge(s.low_free, it + 1)
                sp.dma_start(lora[:], k.d.wa2[l, :, :, bass.ds(it * P, P)]).then_inc(s.low_in, 16)
                sp.dma_start(g2[:], k.d.g2[l, :, bass.ds(it * P, P)]).then_inc(s.low_in, 16)
                sp.wait_ge(s.w_free, it + 1)
                for j in range(3):
                    sp.dma_start(w3[:, j], win[:, :, bass.ds(it * P + (C_R + D * j + P), P)]).then_inc(s.w_in, 16)

        @block.tensor
        def _(pe):
            pe.sem_inc(s.low_free, 1)
            mm = nc.tensor.matmul

            def projection(j, bank):
                for kt in range(KT):
                    m = mm(bank, w3[:, j, kt], k.h[:, kt], start=kt == 0, stop=kt == KT - 1)
                m.then_inc(s.proj, 1)

            pe.wait_ge(s.w_in, 48)
            for j in range(3):
                projection(j, k.bank[j])
            pe.wait_ge(s.proj, 3)
            pe.sem_inc(s.w_free, 1)
            with pe.Fori(0, TURNS) as it:
                pe.wait_ge(s.low_in, it * 32 + 32)
                pe.wait_ge(s.turn_free, it + 1)
                for z in range(2):
                    mm(k.bank[3 + z], lora[0:64, z], low[0:64, 0], start=True, stop=True)
                for z in range(2):
                    mm(k.bank[5 + z], lora[64:128, z], low[64:128, 0], start=True, stop=True)
                mm(k.bank[7], g2[:], low[:, 1], start=True, stop=True).then_inc(s.lora, 1)
                pe.wait_ge(s.lora, it + 1)
                pe.sem_inc(s.low_free, 1)
                pe.wait_ge(s.kksq, it + 1)
                mm(k.bank[0], const(k, "headones"), tmp[:], start=True, stop=True).then_inc(s.kkn, 1)
                for c in range(4):
                    m = nc.tensor.transpose(k.bank[1][:, P * c:P * c + P], vv[:, P * c:P * c + P], ident)
                m.then_inc(s.turned, 1)
                pe.wait_ge(s.feat, it * 2 + 1)
                for j in range(4):
                    for c in range(4):
                        m = nc.tensor.transpose(k.bank[2 + j][:, P * c:P * c + P], bk[:, j // 2, j % 2, P * c:P * c + P], ident)
                    m.then_inc(s.turned, 1)
                pe.wait_ge(s.tok, it * 5 + 5)
                pe.wait_ge(s.feat, it * 2 + 2)
                for pp in range(2):
                    for q in range(2):
                        pos = 2 * pp + q
                        pe.wait_ge(s.gevac, it * 4 + pos) if pos else None
                        for p in range(4):
                            h, z = p // 2, p % 2
                            hs, c = slice(64 * h, 64 * h + 64), ORDER[z][pos]
                            x = slice(P * c, P * c + P)
                            arc = ar[hs, z, c].rearrange("p a c -> p (a c)")
                            mm(k.bank[p][:, 0:256], bk[hs, z, 0, x], arc, start=True, stop=True, skip_group_check=True)
                            mm(k.bank[p][:, 256:512], bk[hs, z, 1, x], arc, start=False, stop=True, skip_group_check=True)
                            m = mm(k.bank[4 + h][:, P * z:P * z + P], ar[hs, z, c, 0], bk[hs, z, 0, x], start=z == 0, stop=True, skip_group_check=True)
                        m.then_inc(s.gdone, 1)
                        if pos == 0:
                            pe.wait_ge(s.w_in, it * 48 + 96)
                            projection(0, k.bank[6])
                        elif pos == 1:
                            projection(1, k.bank[7])
                        elif pos == 2:
                            pe.wait_ge(s.y_in, it * 4 + 2)
                            projection(2, k.bank[6])
                            pe.wait_ge(s.proj, it * 3 + 6)
                            pe.sem_inc(s.w_free, 1)
                    turn2 = it * 2 + pp
                    for q in range(2):
                        pe.wait_ge(s.gevac, it * 4 + (2 * pp + q + 1))
                    for g, stage in enumerate(STAGES):
                        for q in range(2):
                            if g:
                                _, a, v = COUNTS[g - 1, q]
                                pe.wait_ge(s.ev_a, turn2 * N_EV_A + a)
                                pe.wait_ge(s.ev_v, turn2 * N_EV_V + v)
                            for j, (left, right, _, _) in enumerate(stage):
                                bank = stage_bank(k, q, j)
                                for p in range(4):
                                    if right is None:
                                        m = nc.tensor.transpose(bank[:, P * p:P * p + P], buf[q][left][:, p], ident)
                                    else:
                                        m = mm(bank[:, P * p:P * p + P], buf[q][left][:, p], buf[q][right][:, p],
                                               start=p == 0, stop=True, skip_group_check=True)
                                m.then_inc(s.prod, 1)
                    pe.wait_ge(s.rawin, it * 3 + (5 + pp))
                    for q in range(2):
                        pos = 2 * pp + q
                        P4 = it * 4 + (pos + 1)
                        pe.wait_ge(s.ev_v, turn2 * N_EV_V + N_EV_V)
                        if pos:
                            pe.wait_ge(s.s_in, it * 3 + pos)
                        else:
                            pe.wait_ge(s.padded, it + 1)
                        for z in range(2):
                            c = ORDER[z][pos]
                            mm(k.bank[4][:, P * z:P * z + P], ar[:, z, c, 0], s0[:, z], start=z == 0, stop=True, skip_group_check=True)
                            for h in range(2):
                                m = mm(k.bank[4][:, P * z + 64 * h:P * z + 64 * h + 64], gm[q][:, 2 * h + z, 2], vpad[:, h, c, 64 * h:64 * h + 64],
                                       start=False, stop=True, skip_group_check=True)
                        m.then_inc(s.r_done, 1)
                        pe.wait_ge(s.r_in, P4)
                        for z in range(2):
                            for h in range(2):
                                m = mm(k.bank[5][:, P * z + 64 * h:P * z + 64 * h + 64], buf[q]["XT"][:, 2 * h + z], rs[:, z, 64 * h:64 * h + 64],
                                       start=z + h == 0, stop=True, skip_group_check=True)
                        m.then_inc(s.u_done, 1)
                        pe.wait_ge(s.u_in, P4)
                        if pos < 3:
                            for z in range(2):
                                c = ORDER[z][pos]
                                for h in range(2):
                                    mm(k.bank[7][:, P * z:P * z + P], bkt[:, z, 0, c], up[:, z, h], start=z + h == 0, stop=True, skip_group_check=True)
                                    m = mm(k.bank[7][:, P * z:P * z + P], bkt[:, z, 1, c], vpad[:, h, c], start=False, stop=True, skip_group_check=True)
                        if pos:
                            pe.wait_ge(s.y_in, it * 4 + pos)
                        for z in range(2):
                            c = ORDER[z][pos]
                            my = mm(k.bank[6][:, P * z:P * z + P], s0[:, z], ar[:, z, c, 1], start=z == 0, stop=True, skip_group_check=True)
                            for h in range(2):
                                mm(k.bank[6][:, P * z:P * z + P], vpad[:, h, c], gm[q][:, 2 * h + z, 3], start=False, stop=True, skip_group_check=True)
                                my = mm(k.bank[6][:, P * z:P * z + P], up[:, z, h], gm[q][:, 2 * h + z, 1], start=False, stop=True, skip_group_check=True)
                        my.then_inc(s.y_done, 1)
                pe.wait_ge(s.ysum, it + 1)
                mm(k.bank[0][:, 0:n], const(k, "headones"), ks[:, t0:], start=True, stop=True).then_inc(s.mean_d, 1)
                pe.wait_ge(s.sq, it + 1)
                mm(k.bank[1][:, 0:n], const(k, "headones"), tmp[:, t0:], start=True, stop=True).then_inc(s.var_d, 1)
                pe.wait_ge(s.bonus_in, it + 1)
                mm(k.bank[2][:, 0:n], const(k, "headones"), kk[:, t0:], start=True, stop=True).then_inc(s.bonus_d, 1)

        @block.scalar
        def _(act):
            ac = nc.scalar.activation

            def keep(j, bank, number):
                act.wait_ge(s.proj, number)
                ac(raw[:, j, :, 1:1 + LC], three(bank, 2), ACT.Copy).then_inc(s.rawin, 1)

            act.wait_ge(s.vec, 1)
            for j in range(3):
                keep(j, k.bank[j], j + 1)
            with act.Fori(0, TURNS) as it:
                act.wait_ge(s.padded, it + 1)
                act.wait_ge(s.lora, it + 1)
                for z in range(2):
                    ac(ld[:, z], k.bank[3 + z], ACT.Sigmoid, bias=pc[:, W0 + z:W0 + z + 1])
                    ac(aa[:, z], k.bank[5 + z], ACT.Sigmoid, bias=pc[:, A0 + z:A0 + z + 1])
                ac(y[:, bass.ds(it, 1), t0:], one(k.bank[7][:, t0:]), ACT.Copy).then_inc(s.lact, 1)
                act.wait_ge(s.kkn, it + 1)
                ac(tmp[:], k.bank[0], ACT.Sqrt).then_inc(s.kkroot, 1)
                act.wait_ge(s.turned, it * 5 + 1)
                for h in range(2):
                    m = ac(vpad[:, h, :, 64 * h:64 * h + 64], three(k.bank[1], 4)[:, :, 64 * h:64 * h + 64], ACT.Copy)
                m.then_inc(s.tok, 1)
                act.wait_ge(s.cen, it + 1)
                ac(ld[:], ci[:], ACT.Exp, scale=-1.0)
                ac(ci[:], ci[:], ACT.Exp)
                ac(em[:], half[:], ACT.Exp)
                ac(ce[:], ce[:], ACT.Exp).then_inc(s.exps, 1)
                for j in range(4):
                    act.wait_ge(s.turned, it * 5 + (j + 2))
                    ac(bkt[:, j // 2, j % 2], three(k.bank[2 + j], 4), ACT.Copy).then_inc(s.tok, 1)
                for pp in range(2):
                    turn2 = it * 2 + pp
                    if pp == 0:
                        keep(0, k.bank[6], it * 3 + 4)
                        keep(1, k.bank[7], it * 3 + 5)
                    else:
                        keep(2, k.bank[6], it * 3 + 6)
                    for g, stage in enumerate(STAGES):
                        for q in range(2):
                            first, _, _ = COUNTS[g, q]
                            for j, (_, _, into, how) in enumerate(stage):
                                if how == "copy":
                                    act.wait_ge(s.prod, turn2 * N_PROD + (first + j + 1))
                                    ac(flat(buf[q][into]), stage_bank(k, q, j), ACT.Copy).then_inc(s.ev_a, 1)
                    for q in range(2):
                        pos = 2 * pp + q
                        act.wait_ge(s.y_done, it * 4 + (pos + 1))
                        for z in range(2):
                            m = ac(yy[:, z, chunk(z, pos)], k.bank[6][:, P * z:P * z + P], ACT.Copy)
                        m.then_inc(s.y_in, 1)
                act.wait_ge(s.yc, it + 1)
                ac(tmp[:, t0:], ks[:, t0:], ACT.Square).then_inc(s.sq, 1)
                act.wait_ge(s.var_in, it + 1)
                ac(tmp[:, t0:], tmp[:, t0:], ACT.Sqrt).then_inc(s.root, 1)
                act.wait_ge(s.yn, it + 1)
                ac(ks[:, t0:], ks[:, t0:], ACT.Identity, bias=pc[:, LNB:LNB + 1], scale=pc[:, LNW:LNW + 1]).then_inc(s.lnd, 1)

        @block.vector
        def _(v):
            tt, stt, ts = nc.vector.tensor_tensor, nc.vector.scalar_tensor_tensor, nc.vector.tensor_scalar
            v.sem_inc(s.turn_free, 1)
            do = Steps(v, s.vec)
            for t in (raw, vpad, up):
                do.do(nc.vector.memset(t[:], 0.0))
            with v.Fori(0, TURNS) as it:
                do = Steps(v, s.vec, it, 92, 3)
                p1 = lambda j: pc[:, j:j + 1]
                do.do(nc.vector.tensor_copy(one(pc[:]), k.rcols[:, l, bass.ds(it, 1), :]))
                nc.vector.memset(s0[:], 0.0).then_inc(s.padded, 1)
                v.wait_ge(s.padded, it + 1)
                for j in range(3):
                    v.wait_ge(s.rawin, it * 3 + (j + 1))
                    token_shift(nc, do, raw[:, j], three(rkv[:, j], 2), p1(MU + j))
                do.do(ts(kk[:], kf, p1(KK), None, ALU.mult))
                tt(tmp[:], kk[:], kk[:], ALU.mult).then_inc(s.kksq, 1)
                v.wait_ge(s.lact, it + 1)
                do.do(ts(ld[:], ld[:], -DECAY_SCALE, None, ALU.mult))
                for z, pre in ((0, ce), (1, ci)):
                    for c in range(4):
                        x = slice(P * c, P * c + P)
                        do.put(nc.vector.tensor_tensor_scan(pre[:, z, x], const(k, "ones"), ld[:, z, x], 0.0, ALU.mult, ALU.add))
                do.settle()
                for z, pre in ((0, ce), (1, ci)):
                    do.put(ts(half[:, z], three(pre[:, z], 4)[:, :, P - 1], 0.5, None, ALU.mult))
                do.settle()
                hb = [half[:, z].unsqueeze(2).to_broadcast([P, 4, P]) for z in range(2)]
                do.do(tt(three(ci[:, 0], 4), three(ce[:, 0], 4), hb[0], ALU.subtract))
                do.do(tt(three(ce[:, 1], 4), hb[1], three(ci[:, 1], 4), ALU.subtract))
                do.do(tt(ce[:, 0], ci[:, 0], ld[:, 0], ALU.subtract))
                tt(ci[:, 1], ce[:, 1], ld[:, 1], ALU.add).then_inc(s.cen, 1)
                v.wait_ge(s.cen, it + 1)
                v.wait_ge(s.kkroot, it + 1)
                do.do(ts(tmp[:], tmp[:], 1e-12, None, ALU.max))
                do.do(nc.vector.reciprocal(tmp[:], tmp[:]))
                do.do(tt(kk[:], kk[:], tmp[:], ALU.mult))
                for z in range(2):
                    do.do(ts(bk[:, z, 1], aa[:, z], -1.0, p1(KA), ALU.add, ALU.mult))
                    do.do(stt(bk[:, z, 1], bk[:, z, 1], 1.0, kf, ALU.add, ALU.mult))
                    do.put(stt(bk[:, z, 0], kk[:], -1.0, aa[:, z], ALU.mult, ALU.mult))
                do.do(tt(ks[:], bk[:, 0, 1], bk[:, 1, 1], ALU.add))
                v.wait_ge(s.exps, it + 1)
                for z in range(2):
                    for j in range(2):
                        do.put(tt(bk[:, z, j], bk[:, z, j], ld[:, z], ALU.mult))
                do.settle()
                v.sem_inc(s.feat, 1)
                for z in range(2):
                    do.put(tt(ar[:, z, :, 0], three(ce[:, z], 4), three(kk[:], 4), ALU.mult))
                    do.put(tt(ar[:, z, :, 1], three(ci[:, z], 4), three(r, 4), ALU.mult))
                do.settle()
                v.sem_inc(s.feat, 1)
                do.do(stt(kk[:], ks[:], p1(RK), r, ALU.mult, ALU.mult))
                for pp in range(2):
                    turn2 = it * 2 + pp
                    for q in range(2):
                        pos = 2 * pp + q
                        b = buf[q]
                        v.wait_ge(s.gdone, it * 4 + (pos + 1))
                        for p in range(4):
                            do.put(tt(gm[q][:, p].rearrange("p (a b) c -> p a (b c)", a=2), three(k.bank[p], 2),
                                      one(three(const(k, "gmask"), 2)[:, p % 2]).to_broadcast([P, 2, 256]), ALU.mult))
                        for h in range(2):
                            do.put(tt(b["A"][:, 2 * h:2 * h + 2].rearrange("p a c -> p (a c)"), k.bank[4 + h][:, 0:256], const(k, "amask"), ALU.mult))
                        do.settle()
                        bd = one(const(k, "bd16")).to_broadcast([P, 4, P])
                        do.put(tt(b["b0"][:], b["A"][:], bd, ALU.mult))
                        do.put(tt(b["b1"][:], gm[q][:, :, 0], bd, ALU.mult))
                        do.settle()
                        eye = one(ident).to_broadcast([P, 4, P])
                        tt(b["XT"][:], b["b1"][:], eye, ALU.add).then_inc(s.gevac, 1)
                    for g, stage in enumerate(STAGES):
                        for q in range(2):
                            first, _, _ = COUNTS[g, q]
                            for j, (_, _, into, how) in enumerate(stage):
                                if how == "copy":
                                    continue
                                v.wait_ge(s.prod, turn2 * N_PROD + (first + j + 1))
                                dst, bank = flat(buf[q][into]), stage_bank(k, q, j)
                                if how == "vcopy":
                                    nc.vector.tensor_copy(dst, bank).then_inc(s.ev_v, 1)
                                elif how == "add":
                                    tt(dst, dst, bank, ALU.add).then_inc(s.ev_v, 1)
                                else:
                                    tt(dst, dst, bank, ALU.add)
                                    off = one(const(k, how)).to_broadcast([P, 4, P])
                                    tt(buf[q]["b1"][:], buf[q]["A"][:], off, ALU.mult).then_inc(s.ev_v, 1)
                    for q in range(2):
                        pos = 2 * pp + q
                        P4 = it * 4 + (pos + 1)
                        v.wait_ge(s.r_done, P4)
                        nc.vector.tensor_copy(flat(rs), k.bank[4][:, 0:256]).then_inc(s.r_in, 1)
                        v.wait_ge(s.u_done, P4)
                        if pos:
                            v.wait_ge(s.y_done, it * 4 + pos)
                        ub = k.bank[5][:, 0:256].rearrange("p (z h c) -> p z h c", z=2, h=2)
                        for h in range(2):
                            m = nc.vector.tensor_copy(up[:, :, h, 64 * h:64 * h + 64], ub[:, :, h])
                        m.then_inc(s.u_in, 1)
                        v.wait_ge(s.y_done, P4)
                        if pos < 3:
                            for z in range(2):
                                c, c2 = ORDER[z][pos], ORDER[z][pos + 1]
                                e1, e2 = em[:, z, c:c + 1], em[:, z, c2:c2 + 1]
                                do.do(stt(t1[:, z], k.bank[7][:, P * z:P * z + P], e1, const(k, "headones"), ALU.mult, ALU.mult))
                                do.do(stt(s0[:, z], s0[:, z], e1, t1[:, z], ALU.mult, ALU.add))
                                m = ts(s0[:, z], s0[:, z], e2, None, ALU.mult)
                            m.then_inc(s.s_in, 1)
                v.wait_ge(s.y_in, it * 4 + 4)
                tt(ks[:, t0:], yy[:, 0, t0:], yy[:, 1, t0:], ALU.add).then_inc(s.ysum, 1)
                v.wait_ge(s.mean_d, it + 1)
                stt(ks[:, t0:], k.bank[0][:, 0:n], -1.0 / 64, ks[:, t0:], ALU.mult, ALU.add).then_inc(s.yc, 1)
                v.sem_inc(s.bonus_in, 1)
                v.wait_ge(s.var_d, it + 1)
                ts(tmp[:, t0:], k.bank[1][:, 0:n], 1.0 / 64, GN_EPS, ALU.mult, ALU.add).then_inc(s.var_in, 1)
                v.wait_ge(s.root, it + 1)
                do.do(nc.vector.reciprocal(tmp[:, t0:], tmp[:, t0:]))
                tt(ks[:, t0:], ks[:, t0:], tmp[:, t0:], ALU.mult).then_inc(s.yn, 1)
                v.wait_ge(s.bonus_d, it + 1)
                v.wait_ge(s.yn, it + 1)
                do.do(stt(tmp[:, t0:], k.bank[2][:, 0:n], 0.5, vv[:, t0:], ALU.mult, ALU.mult))
                v.wait_ge(s.lnd, it + 1)
                do.do(tt(ks[:, t0:], ks[:, t0:], tmp[:, t0:], ALU.add))
                out = y[:, bass.ds(it, 1), t0:]
                do.do(tt(out, one(ks[:, t0:]), out, ALU.mult))
                v.sem_inc(s.turn_free, 1)
                do.end()


def rwkv_branch(k, t0):
    nc, l = k.nc, k.layer
    with nc.sbuf_tensor(f"low{l}", [P, 2, TT], F32) as low:
        rwkv_low(k, low)
        rwkv_heads(k, low, k.br, t0)



def route(k, rt, slots, t0):
    nc, l = k.nc, k.layer
    tiles = list(range(t0 // P, NT))
    nt = len(tiles)
    with ExitStack() as st:
        s = st.enter_context(phase(nc, "loaded logits vec act turned ranked last stored"))
        wr = st.enter_context(nc.sbuf_tensor(f"wr{l}", [P, KT, 20], F32))
        br = st.enter_context(nc.sbuf_tensor(f"rb{l}", [P, 20], F32))
        lg = st.enter_context(nc.sbuf_tensor(f"lg{l}", [P, nt, 20], F32))
        a = st.enter_context(nc.sbuf_tensor(f"ra{l}", [P, 8, nt, 4], F32))
        one = st.enter_context(nc.sbuf_tensor(f"r1{l}", [P, 8, nt, 1], F32))
        sel = st.enter_context(nc.sbuf_tensor(f"rs{l}", [P, nt, 4, 4], F32))
        over = st.enter_context(nc.sbuf_tensor(f"ro{l}", [P, nt, 16], F32))
        last = st.enter_context(nc.sbuf_tensor(f"rl{l}", [P, 4], F32))
        row = st.enter_context(nc.sbuf_tensor(f"rr{l}", [16, TT], F32))
        block = st.enter_context(nc.Block())
        OHG, TMP, LS, OH1, OH2, LS2 = range(6)
        MX, EX, SM, PT, MX2, W1, W2, PM = range(8)

        @block.sync
        def _(sp):
            sp.dma_start(wr[:], k.d.router_w[l].rearrange("(kt p) c -> p kt c", p=P)).then_inc(s.loaded, 16)
            sp.dma_start(br[:], k.d.router_b[l:l + 1].to_broadcast([P, 20])).then_inc(s.loaded, 16)
            sp.wait_ge(s.turned, 2)
            sp.dma_start(k.d.comb[:, t0:], row[:, t0:]).then_inc(s.stored, 16)
            sp.wait_ge(s.stored, 16)

        @block.tensor
        def _(pe):
            pe.wait_ge(s.loaded, 32)
            for n, t in enumerate(tiles):
                for kt in range(KT):
                    mm = nc.tensor.matmul(k.bank[0][:, 20 * n:20 * n + 20], k.h[:, kt, P * t:P * t + P], wr[:, kt],
                                          start=kt == 0, stop=kt == KT - 1)
            mm.then_inc(s.logits, 1)
            pe.wait_ge(s.turned, 1)
            for n in range(nt):
                for m in range(n + 1):
                    before = const(k, "gmask")[:, 0:P] if m == n else const(k, "ones")
                    mm = nc.tensor.matmul(k.bank[2][:, 16 * n:16 * n + 16], before, over[:, m], start=m == 0, stop=m == n)
            mm.then_inc(s.ranked, 1)
            pe.wait_ge(s.last, 1)
            for n, t in enumerate(tiles):
                mm = nc.tensor.transpose(k.bank[1][0:16, P * n:P * n + P], over[:, n], const(k, "ident"))
            mm = nc.tensor.transpose(k.bank[3][0:1, 0:P], last[:, 0:1], const(k, "ident"))
            mm.then_inc(s.logits, 1)

        @block.scalar
        def _(act):
            act.wait_ge(s.vec, 3)
            nc.scalar.activation(a[:, TMP], a[:, TMP], ACT.Exp).then_inc(s.act, 1)
            act.wait_ge(s.vec, 19)
            nc.scalar.activation(one[:, EX], one[:, EX], ACT.Exp).then_inc(s.act, 1)

        @block.vector
        def _(v):
            do = Steps(v, s.vec)
            tt, B4 = nc.vector.tensor_tensor, [P, nt, 4]
            v.wait_ge(s.logits, 1)
            v.wait_ge(s.loaded, 32)
            do.do(tt(lg[:], k.bank[0][:, 0:20 * nt].rearrange("p (t c) -> p t c", c=20),
                     br[:].rearrange("p (o c) -> p o c", o=1).to_broadcast([P, nt, 20]), ALU.add))
            grp = lg[:, :, 0:4]
            do.do(nc.vector.tensor_reduce(one[:, MX], grp, AX.X, ALU.max))
            do.do(tt(a[:, TMP], grp, one[:, MX].to_broadcast(B4), ALU.subtract))
            v.wait_ge(s.act, 1)
            do.do(nc.vector.tensor_reduce(one[:, SM], a[:, TMP], AX.X, ALU.add))
            do.do(nc.vector.reciprocal(one[:, PT], one[:, SM]))
            pref = const(k, "pref").rearrange("p (o c) -> p o c", o=1).to_broadcast(B4)

            def first_max(dst, src, mx):
                do.do(tt(dst, src, mx.to_broadcast(B4), ALU.is_equal))
                do.do(tt(dst, dst, pref, ALU.mult))
                do.do(nc.vector.tensor_reduce(one[:, PM], dst, AX.X, ALU.max))
                do.do(tt(dst, dst, one[:, PM].to_broadcast(B4), ALU.is_equal))

            first_max(a[:, OHG], grp, one[:, MX])
            ex = lg[:, :, 4:20].rearrange("p t (g e) -> p t g e", g=4)
            do.do(tt(sel[:], ex, a[:, OHG].unsqueeze(3).to_broadcast([P, nt, 4, 4]), ALU.mult))
            do.do(nc.vector.tensor_reduce(a[:, LS], sel[:].rearrange("p t g e -> p t e g"), AX.X, ALU.add))
            do.do(nc.vector.tensor_reduce(one[:, MX], a[:, LS], AX.X, ALU.max))
            first_max(a[:, OH1], a[:, LS], one[:, MX])
            do.do(nc.vector.scalar_tensor_tensor(a[:, LS2].rearrange("p t c -> p (t c)"), a[:, OH1].rearrange("p t c -> p (t c)"), NEG,
                                                 a[:, LS].rearrange("p t c -> p (t c)"), ALU.mult, ALU.add))
            do.do(nc.vector.tensor_reduce(one[:, MX2], a[:, LS2], AX.X, ALU.max))
            do.do(tt(one[:, EX], one[:, MX2], one[:, MX], ALU.subtract))
            first_max(a[:, OH2], a[:, LS2], one[:, MX2])
            v.wait_ge(s.act, 2)
            do.do(nc.vector.tensor_scalar(one[:, SM], one[:, EX], 1.0, None, ALU.add))
            do.do(nc.vector.reciprocal(one[:, SM], one[:, SM]))
            do.do(tt(one[:, W1], one[:, SM], one[:, PT], ALU.mult))
            do.do(tt(one[:, W2], one[:, W1], one[:, EX], ALU.mult))
            do.do(tt(a[:, OH1], a[:, OH1], one[:, W1].to_broadcast(B4), ALU.mult))
            do.do(tt(a[:, OH2], a[:, OH2], one[:, W2].to_broadcast(B4), ALU.mult))
            do.do(tt(a[:, OH1], a[:, OH1], a[:, OH2], ALU.add))
            w = a[:, OH1].unsqueeze(2).to_broadcast([P, nt, 4, 4])
            do.do(tt(sel[:], a[:, OHG].unsqueeze(3).to_broadcast([P, nt, 4, 4]), w, ALU.mult))
            comb = sel[:].rearrange("p t g e -> p t (g e)")
            do.do(nc.vector.tensor_copy(rt.w[:, 0:nt, 0:16], comb))
            ts = nc.vector.tensor_scalar
            ts(over[:], comb, 0.0, None, ALU.is_gt).then_inc(s.turned, 1)
            v.wait_ge(s.ranked, 1)
            pos = rt.pos[:, 0:nt, 0:16]
            do.do(ts(pos, k.bank[2][:, 0:16 * nt].rearrange("p (t c) -> p t c", c=16), 1.0, None, ALU.add))
            do.do(tt(pos, pos, over[:], ALU.mult))
            do.do(ts(pos, pos, -1.0, None, ALU.add))
            do.do(nc.vector.tensor_reduce(last[:, 0:1], pos, AX.XY, ALU.max))
            do.do(ts(over[:], pos, float(slots), None, ALU.is_ge))
            tt(over[:], over[:], comb, ALU.mult).then_inc(s.last, 1)
            v.wait_ge(s.logits, 2)
            do.do(nc.vector.tensor_reduce(last[0:1, 1:2], k.bank[3][0:1, 0:P], AX.X, ALU.max))
            do.do(ts(last[0:1, 2:3], last[0:1, 1:2], float(slots), None, ALU.is_ge))
            do.do(nc.vector.tensor_copy(rt.flag[0:1, 0:1], last[0:1, 2:3]))
            nc.vector.tensor_copy(row[:, t0:], k.bank[1][0:16, 0:P * nt]).then_inc(s.turned, 1)


def turn_tokens(k, dst, t0):
    nc = k.nc
    with ExitStack() as st:
        s = st.enter_context(phase(nc, "turned copied"))
        block = st.enter_context(nc.Block())
        jobs = [(n, half) for n in range((TT - t0) // P) for half in range(2)]

        @block.tensor
        def _(pe):
            for j, (n, half) in enumerate(jobs):
                if j >= 4:
                    pe.wait_ge(s.copied, j - 3)
                for f in range(4):
                    mm = nc.tensor.transpose(k.bank[j % 4][:, P * f:P * f + P], k.h[:, 4 * half + f, t0 + P * n:t0 + P * n + P], const(k, "ident"))
                mm.then_inc(s.turned, 1)

        @block.scalar
        def _(act):
            for j, (n, half) in enumerate(jobs):
                act.wait_ge(s.turned, j + 1)
                nc.scalar.activation(dst[:, n, 512 * half:512 * half + 512], k.bank[j % 4], ACT.Copy).then_inc(s.copied, 1)


def experts(k, rt, tok, slots, t0):
    nc, l = k.nc, k.layer
    n, nt, C = TT - t0, (TT - t0) // P, slots
    with ExitStack() as st:
        s = st.enter_context(phase(nc, "gu0 gu1 gu2 gu3 gu_free down0 down1 down_free onehot gathered gath_in gu_done silu hid "
                                       "hid_turned hid_in out_done ys_in sc_done acc_in"))

        def sb(name, *shape):
            return st.enter_context(nc.sbuf_tensor(f"{name}{l}", [P, *shape], F32))

        gu, down = sb("gu", 4, 2, 2, HID), sb("down", 2, HT, D)
        oh, ohw, oht = sb("oh", nt, C), sb("ohw", nt, C), sb("oht", 2, n)
        xs, hid, hrow, ys = sb("xs", KT, C), sb("hid", HT, C), sb("hrow", HID), sb("ys", D)
        block = st.enter_context(nc.Block())
        gus, downs = (s.gu0, s.gu1, s.gu2, s.gu3), (s.down0, s.down1)
        gate = k.d.moe_w_gate[l].rearrange("e (kt p) c -> p e kt c", p=P)
        up = k.d.moe_w_up[l].rearrange("e (kt p) c -> p e kt c", p=P)
        dn = k.d.moe_w_down[l].rearrange("e (f p) c -> p e f c", p=P)
        TURNS = EXPERTS // 2
        wide = [k.bank[3 + i][0:C, :] for i in range(3)]

        @block.sync
        def _(sp):
            with sp.Fori(0, TURNS) as it:
                for b in range(2):
                    e = it * 2 + b
                    for j in range(4):
                        if j < 3:
                            sp.wait_ge(s.gu_free, e * 3 + (j + 1))
                        else:
                            sp.wait_ge(s.gu_done, e + 1)
                        for w, src in enumerate((gate, up)):
                            sp.dma_start(gu[:, j, :, w], src[:, bass.ds(e, 1), 2 * j:2 * j + 2].rearrange("p o kt c -> p (o kt) c")).then_inc(gus[j], 16)
                    sp.wait_ge(s.down_free, e + 1)
                    sp.dma_start(down[:, b], dn[:, bass.ds(e, 1)].rearrange("p o f c -> p (o f) c")).then_inc(downs[b], 16)

        @block.vector
        def _(v):
            def onehots(e):
                for t in range(nt):
                    iota, pos = const(k, "iota")[:, 0:C], rt.pos[:, t, e]
                    nc.vector.tensor_scalar(oh[:, t], iota, pos, None, ALU.is_equal)
                    ins = nc.vector.tensor_scalar(ohw[:, t], iota, pos, rt.w[:, t, e], ALU.is_equal, ALU.mult)
                ins.then_inc(s.onehot, 1)

            v.sem_inc(s.acc_in, 2)
            onehots(slice(0, 1))
            with v.Fori(0, TURNS) as it:
                for b in range(2):
                    e = it * 2 + b
                    v.wait_ge(s.gathered, e * 3 + 3)
                    onehots(bass.ds(e + 1, 1))
                    v.wait_ge(s.silu, e + 1)
                    nc.vector.tensor_tensor(hrow[0:C, 0:256], hrow[0:C, 0:256], wide[1][:, 256:512], ALU.mult)
                    nc.vector.tensor_tensor(hrow[0:C, 256:768], hrow[0:C, 256:768], wide[2], ALU.mult).then_inc(s.hid, 1)
                    for m in range(KT):
                        v.wait_ge(s.sc_done, e * KT + (m + 1))
                        nc.vector.tensor_tensor(k.acc[:, m, t0:], k.acc[:, m, t0:], k.bank[6 + m % 2][:, 0:n], ALU.add).then_inc(s.acc_in, 1)

        @block.scalar
        def _(act):
            ac = nc.scalar.activation

            def take_tokens(e):
                for half in range(2):
                    act.wait_ge(s.gathered, e * 3 + (half + 1))
                    ac(xs[:, 4 * half:4 * half + 4].rearrange("p a c -> p (a c)"), k.bank[half][:, 0:4 * C], ACT.Copy).then_inc(s.gath_in, 1)

            def take_scatter(e, par):
                act.wait_ge(s.gathered, e * 3 + 3)
                ac(oht[0:C, par], k.bank[2][0:C, 0:n], ACT.Copy).then_inc(s.gath_in, 1)

            take_tokens(0)
            take_scatter(0, 0)
            with act.Fori(0, TURNS) as it:
                for b in range(2):
                    e = it * 2 + b
                    act.wait_ge(s.gu_done, e + 2)
                    ac(hrow[0:C, 0:512], wide[0], ACT.Silu)
                    ac(hrow[0:C, 512:768], wide[1][:, 0:256], ACT.Silu).then_inc(s.silu, 1)
                    take_tokens(e + 1)
                    act.wait_ge(s.hid_turned, e + 1)
                    ac(hid[:, 0:4].rearrange("p a c -> p (a c)"), k.bank[3][:, 0:4 * C], ACT.Copy)
                    ac(hid[:, 4:6].rearrange("p a c -> p (a c)"), k.bank[4][:, 0:2 * C], ACT.Copy).then_inc(s.hid_in, 1)
                    take_scatter(e + 1, 1 - b)
                    for half in range(2):
                        act.wait_ge(s.out_done, e * 2 + (half + 1))
                        ac(ys[0:C, 512 * half:512 * half + 512], k.bank[half][0:C, :], ACT.Copy).then_inc(s.ys_in, 1)

        @block.tensor
        def _(pe):
            mm, turn, ident = nc.tensor.matmul, nc.tensor.transpose, const(k, "ident")

            def gather_tokens():
                for half in range(2):
                    for f in range(4):
                        for t in range(nt):
                            m = mm(k.bank[half][:, C * f:C * f + C], tok[:, t, 512 * half + P * f:512 * half + P * f + P], oh[:, t],
                                   start=t == 0, stop=t == nt - 1)
                    m.then_inc(s.gathered, 1)

            def turn_scatter():
                for t in range(nt):
                    m = turn(k.bank[2][0:C, P * t:P * t + P], ohw[:, t], ident)
                m.then_inc(s.gathered, 1)

            pe.sem_inc(s.gu_free, 3)
            pe.sem_inc(s.gu_done, 1)
            pe.sem_inc(s.down_free, 2)
            pe.wait_ge(s.onehot, 1)
            gather_tokens()
            turn_scatter()
            with pe.Fori(0, TURNS) as it:
                for b in range(2):
                    e = it * 2 + b
                    pe.wait_ge(s.gath_in, e * 3 + 3)
                    for j in range(4):
                        pe.wait_ge(gus[j], e * 32 + 32)
                        cols = gu[:, j].rearrange("p a w c -> p a (w c)")
                        for a in range(2):
                            for i in range(3):
                                m = mm(wide[i], xs[:, 2 * j + a], cols[:, a, 512 * i:512 * i + 512], start=j + a == 0, stop=j + a == 4)
                        m.then_inc(s.gu_done if j == 3 else s.gu_free, 1)
                    pe.wait_ge(s.onehot, e + 2)
                    gather_tokens()
                    pe.wait_ge(s.hid, e + 1)
                    for f in range(HT):
                        m = turn(k.bank[3 + f // 4][:, C * (f % 4):C * (f % 4) + C], hrow[0:C, P * f:P * f + P], ident[0:C, 0:C])
                    m.then_inc(s.hid_turned, 1)
                    turn_scatter()
                    pe.wait_ge(downs[b], it * 16 + 16)
                    pe.wait_ge(s.hid_in, e + 1)
                    pe.wait_ge(s.gath_in, e * 3 + 5)
                    for half in range(2):
                        for f in range(HT):
                            m = mm(k.bank[half][0:C, :], hid[:, f], down[:, b, f, 512 * half:512 * half + 512], start=f == 0, stop=f == HT - 1)
                        m.then_inc(s.out_done, 1)
                    pe.wait_ge(s.out_done, e * 2 + 2)
                    pe.sem_inc(s.down_free, 1)
                    pe.wait_ge(s.ys_in, e * 2 + 2)
                    for m8 in range(KT):
                        pe.wait_ge(s.acc_in, e * KT + (m8 + 1))
                        mm(k.bank[6 + m8 % 2][:, 0:n], ys[0:C, P * m8:P * m8 + P], oht[0:C, b, 0:n], start=True, stop=True).then_inc(s.sc_done, 1)


def experts_dense(k, flag, t0):
    nc, l = k.nc, k.layer
    n = TT - t0
    R = 3
    with ExitStack() as st:
        s = st.enter_context(phase(nc, "gu0 gu1 gu2 down w0 gu_free down_free w_free gate_done up_done gu_bank_free silu_done hidden_done hidden_free hmul out_done out_bank_free"))
        gu = st.enter_context(nc.sbuf_tensor(f"dense_gu{l}", [P, R, 2, KT, P], F32))
        down = st.enter_context(nc.sbuf_tensor(f"dense_down{l}", [P, HT, D], F32))
        hid = st.enter_context(nc.sbuf_tensor(f"dense_hid{l}", [P, HT, TT], F32))
        sg = st.enter_context(nc.sbuf_tensor(f"msg{l}", [P, 2, TT], F32))
        wb = st.enter_context(nc.sbuf_tensor(f"wb{l}", [P, TT], F32))
        block = st.enter_context(nc.Block())
        gus = (s.gu0, s.gu1, s.gu2)
        gate = k.d.moe_w_gate[l].rearrange("e (kt p) c -> p e kt c", p=P)
        up = k.d.moe_w_up[l].rearrange("e (kt p) c -> p e kt c", p=P)
        dn = k.d.moe_w_down[l].rearrange("e (f p) c -> p e f c", p=P)

        @block.sync
        def _(sp):
            left_over = sp.value_load(flag[0:1, 0:1], min_val=0, max_val=1)
            with sp.If(left_over > 0):
                with sp.Fori(0, EXPERTS) as e:
                    for f in range(HT):
                        sp.wait_ge(s.gu_free, e * HT + (f + 1))
                        sp.dma_start(gu[:, f % R, 0], gate[:, bass.ds(e, 1), :, P * f:P * f + P].rearrange("p o kt c -> p (o kt) c")).then_inc(gus[f % R], 16)
                        sp.dma_start(gu[:, f % R, 1], up[:, bass.ds(e, 1), :, P * f:P * f + P].rearrange("p o kt c -> p (o kt) c")).then_inc(gus[f % R], 16)
                        if f == 0:
                            sp.wait_ge(s.w_free, e + 1)
                            sp.dma_start(wb[:, t0:], k.d.comb[bass.ds(e, 1), t0:].to_broadcast([P, n])).then_inc(s.w0, 16)
                        if f == 2:
                            sp.wait_ge(s.down_free, e + 1)
                            sp.dma_start(down[:], dn[:, bass.ds(e, 1)].rearrange("p o f c -> p (o f) c")).then_inc(s.down, 16)

        @block.tensor
        def _(pe):
            left_over = pe.value_load(flag[0:1, 0:1], min_val=0, max_val=1)
            with pe.If(left_over > 0):
                pe.sem_inc(s.gu_free, R)
                pe.sem_inc(s.down_free, 1)
                with pe.Fori(0, EXPERTS) as e:
                    for f in range(HT):
                        pe.wait_ge(gus[f % R], e * 64 + 32 * (f // R + 1))
                        pe.wait_ge(s.gu_bank_free, e * HT + (f + 1))
                        for w, done in ((0, s.gate_done), (1, s.up_done)):
                            for kt in range(KT):
                                mm = nc.tensor.matmul(k.bank[2 * w + f % 2][:, 0:n], gu[:, f % R, w, kt], k.h[:, kt, t0:],
                                                      start=kt == 0, stop=kt == KT - 1)
                            mm.then_inc(done, 1)
                        pe.wait_ge(s.up_done, e * HT + (f + 1))
                        pe.sem_inc(s.gu_free, 1)
                    pe.wait_ge(s.down, e * 16 + 16)
                    pe.wait_ge(s.hidden_done, e * HT + HT)
                    for m in range(KT):
                        pe.wait_ge(s.out_bank_free, e * KT + (m + 1))
                        for f in range(HT):
                            mm = nc.tensor.matmul(k.bank[4 + m % 4][:, 0:n], down[:, f, P * m:P * m + P], hid[:, f, t0:],
                                                  start=f == 0, stop=f == HT - 1)
                        mm.then_inc(s.out_done, 1)
                    pe.wait_ge(s.out_done, e * KT + KT)
                    pe.sem_inc(s.down_free, 1)

        @block.scalar
        def _(act):
            left_over = act.value_load(flag[0:1, 0:1], min_val=0, max_val=1)
            with act.If(left_over > 0):
                with act.Fori(0, EXPERTS) as e:
                    for f in range(HT):
                        act.wait_ge(s.gate_done, e * HT + (f + 1))
                        act.wait_ge(s.gu_bank_free, e * HT + (f + 1))
                        nc.scalar.activation(sg[:, f % 2, t0:], k.bank[f % 2][:, 0:n], ACT.Silu).then_inc(s.silu_done, 1)

        @block.vector
        def _(v):
            left_over = v.value_load(flag[0:1, 0:1], min_val=0, max_val=1)
            with v.If(left_over > 0):
                v.sem_inc(s.gu_bank_free, 2)
                v.sem_inc(s.out_bank_free, 4)
                v.sem_inc(s.w_free, 1)
                with v.Fori(0, EXPERTS) as e:
                    v.wait_ge(s.w0, e * 16 + 16)
                    for f in range(HT):
                        v.wait_ge(s.silu_done, e * HT + (f + 1))
                        v.wait_ge(s.up_done, e * HT + (f + 1))
                        nc.vector.tensor_tensor(sg[:, f % 2, t0:], sg[:, f % 2, t0:], k.bank[2 + f % 2][:, 0:n], ALU.mult).then_inc(s.hmul, 1)
                        v.wait_ge(s.hmul, e * HT + (f + 1))
                        nc.vector.tensor_tensor(hid[:, f, t0:], sg[:, f % 2, t0:], wb[:, t0:], ALU.mult).then_inc(s.hidden_done, 1)
                        v.wait_ge(s.hidden_done, e * HT + (f + 1))
                        v.sem_inc(s.gu_bank_free, 1)
                    v.sem_inc(s.w_free, 1)
                    for m in range(KT):
                        v.wait_ge(s.out_done, e * KT + (m + 1))
                        nc.vector.tensor_tensor(k.acc[:, m, t0:], k.acc[:, m, t0:], k.bank[4 + m % 4][:, 0:n], ALU.add).then_inc(s.out_bank_free, 1)


def residual_ffn(k, t0):
    nc, l = k.nc, k.layer
    with ExitStack() as st:
        s = st.enter_context(phase(nc, "added"))
        block = st.enter_context(nc.Block())

        @block.vector
        def _(v):
            for m in range(KT):
                for c in range(t0 // LC, 2):
                    x = k.x[:, m, LC * c:LC * c + LC]
                    nc.vector.scalar_tensor_tensor(x, k.acc[:, m, LC * c:LC * c + LC], k.mod[:, 40 + m, c:c + 1], x, ALU.mult, ALU.add).then_inc(s.added, 1)
            v.wait_ge(s.added, KT * (2 - t0 // LC))


def clear(k, *bufs):
    nc = k.nc
    with ExitStack() as st:
        s = st.enter_context(phase(nc, "cleared"))
        block = st.enter_context(nc.Block())

        @block.vector
        def _(v):
            for buf, value in bufs:
                nc.vector.memset(buf, value).then_inc(s.cleared, 1)
            v.wait_ge(s.cleared, len(bufs))



SLOTS = P


class State:
    pass


def program(nc, d):
    with ExitStack() as st:
        def sb(name, shape):
            return st.enter_context(nc.sbuf_tensor("sb_" + name, shape, F32))

        k = State()
        k.nc, k.d = nc, d
        k.first = [st.enter_context(nc.semaphore(f"first_slab{h}")) for h in range(2)]
        k.n_first, k.asked = 0, False
        k.bank = [st.enter_context(nc.psum_tensor(f"bank{i}", [P, 512], F32))[:] for i in range(8)]
        k.x, k.h, k.acc, k.br = (sb(n, [P, KT, TT]) for n in ("x", "h", "acc", "branch"))
        k.const, k.cols, k.rcols = sb("consts", [P, N_CONST]), sb("cols", [P, DEPTH, N_COL]), sb("rcols", [P, DEPTH, 8, N_RCOL])
        k.cvec, k.final = sb("cvec", [P, KT, 2]), sb("final", [P, KT])
        flag = st.enter_context(nc.sbuf_tensor("left_over", [1, 1], mybir.dt.int32))
        k.mod, k.nscale = sb("mod", [P, 48, 2]), sb("nscale", [P, 2, KT, 2])

        with phase(nc, "loaded") as s, nc.Block() as block:
            @block.sync
            def _(sp):
                for dst, src in ((k.x[:], d.xT.rearrange("(kt p) t -> p kt t", p=P)), (k.const[:], d.consts), (k.cols[:], d.cols),
                                 (k.rcols[:], d.rcols), (k.cvec[:], d.cvec), (k.final[:], d.final)):
                    sp.dma_start(dst, src).then_inc(s.loaded, 16)
                sp.wait_ge(s.loaded, 6 * 16)

        for l in range(DEPTH):
            k.layer = l
            t0 = LC if l == DEPTH - 1 else 0
            with nc.sbuf_tensor(f"ring{l}", [P, 2, KT, 512], F32) as ring:
                k.ring = ring
                w = d.w_in[l]
                k.plans = [("plain", d.w_mod[l], 0), ("plain", w, C_XBC), ("plain", w, C_Z), ("merge", w, 0), ("plain", w, C_Q),
                           ("plain", w, C_V), ("merge", w, 2)]
                modulation(k)
                norm(k, k.x, k.h, 0, 0)
                ssd_branch(k, t0)
                natten_branch(k, t0)
            rwkv_branch(k, t0)
            with nc.sbuf_tensor(f"ringb{l}", [P, 2, KT, 512], F32) as ring:
                k.ring = ring
                k.plans = [("merge", d.w_in[l], 1), ("plain", d.w_out[l], 0)]
                merge(k, 1, k.br, t0)
                residual_out(k, t0)
            norm(k, k.x, k.h, t0, 1)
            slots = SLOTS
            rt = State()
            with nc.sbuf_tensor(f"pos{l}", [P, NT, 18], F32) as pos, nc.sbuf_tensor(f"rw{l}", [P, NT, 18], F32) as rw:
                rt.pos, rt.w, rt.flag = pos, rw, flag
                clear(k, (k.acc[:], 0.0), (pos[:], -1.0), (rw[:], 0.0))
                route(k, rt, slots, t0)
                tok = k.br[:].rearrange("p (t a) c -> p t (a c)", t=NT)
                turn_tokens(k, tok, t0)
                experts(k, rt, tok, slots, t0)
            experts_dense(k, flag, t0)
            residual_ffn(k, t0)
        k.normcol = lambda m: k.final[:, m:m + 1]
        norm(k, k.x, k.h, LC, "cols")
        with phase(nc, "stored") as s, nc.Block() as block:
            @block.sync
            def _(sp):
                sp.dma_start(d.out.rearrange("(kt p) t -> p kt t", p=P), k.h[:, :, LC:]).then_inc(s.stored, 16)
                sp.wait_ge(s.stored, 16)



def layout(i):
    L = DEPTH

    def tiles(a):
        a = np.asarray(a)
        a = a.reshape(a.shape[:-1] + (a.shape[-1] // P, P))
        return np.moveaxis(a, -1, 0)

    a = {n: np.asarray(i[n]) for n in ("w_mod", "w_in", "w_branch", "w_out", "moe_w_gate", "moe_w_up", "moe_w_down")}
    a["xT"] = np.concatenate([i["ctx"][0].T, i["x"][0].T], 1)
    a["cvec"] = np.stack([tiles(i["c_ctx"]), tiles(i["c"][0])], -1)
    a["final"] = tiles(i["final_norm_w"])
    mu = np.asarray(i["rwkv_mu"])
    parts = [tiles(i["norm1_w"]), tiles(i["norm2_w"]), tiles(i["b_mod"]), tiles(i["ssd_conv_b"]),
             tiles(i["ssd_conv_w"]).reshape(P, L, 80), tiles(np.repeat(np.asarray(i["ssd_d"]), 64, -1)),
             tiles(i["ssd_norm_w"]), tiles(mu[:, 3072:3200]), tiles(mu[:, 3200:3328])]
    a["cols"] = np.concatenate(parts, 2)
    r = [tiles(mu[:, 1024 * n:1024 * n + 1024]) for n in range(3)]
    r += [tiles(i["rwkv_w0"])[:, :, n] for n in range(2)] + [tiles(i["rwkv_a0"])[:, :, n] for n in range(2)]
    r += [tiles(i["rwkv_k_k"]), tiles(i["rwkv_k_a"]), tiles(np.asarray(i["rwkv_r_k"]).reshape(L, D)), tiles(i["rwkv_ln_w"]), tiles(i["rwkv_ln_b"])]
    a["rcols"] = np.stack(r, -1)
    a["wa2"] = np.concatenate([np.asarray(i["rwkv_w2"]), np.asarray(i["rwkv_a2"])], 2).transpose(0, 2, 1, 3)
    a["g2"] = np.asarray(i["rwkv_g2"])
    a["dt_par"] = np.concatenate([np.asarray(i["ssd_dt_bias"]), np.asarray(i["ssd_a_log"])], 1).transpose(0, 2, 1)
    a["router_w"] = np.concatenate([np.asarray(i["moe_w_group"]), np.asarray(i["moe_w_expert"])], 2)
    a["router_b"] = np.concatenate([np.asarray(i["moe_b_group"]), np.asarray(i["moe_b_expert"])], 1)
    col = np.arange(64)
    dc = np.clip(col[None] - col[:, None], -15, 15) + 15
    a["na_bias"] = np.asarray(i["na_rpb"])[:, :, 4:11][:, :, :, dc]
    a["consts"] = constants()
    return {n: np.ascontiguousarray(v) for n, v in a.items()}


def kernel(**inputs):
    import concourse.bacc as bacc
    from concourse.bass_utils import run_bass_kernel_spmd

    nc = bacc.Bacc("TRN2", target_bir_lowering=False, num_devices=1)
    arrays = layout(inputs)
    d = {n: nc.dram_tensor(n, a.shape, F32, kind="ExternalInput").ap() for n, a in arrays.items()}
    d["ssd_rows"] = nc.dram_tensor("ssd_rows", [16, 2, 10 * P], F32).ap()
    d["comb"] = nc.dram_tensor("comb", [16, TT], F32).ap()
    d["out"] = nc.dram_tensor("out", [D, LC], F32, kind="ExternalOutput").ap()
    program(nc, namedtuple("Arrays", " ".join(d))(**d))
    r = run_bass_kernel_spmd(nc, [arrays], core_ids=[0])
    return np.ascontiguousarray(r.results[0]["out"].T)[None]
```
